# Optimizing a Trainium2 kernel written in Bass

```python
import math
import jax, jax.numpy as jnp
from jax import lax
import numpy as np

D_MODEL = 1024
BATCH = 1
SEQ = 1024
DEPTH = 1

MLA_HEADS = 8
MLA_Q_LORA = 256
MLA_KV_LORA = 128
MLA_NOPE_DIM = 64
MLA_ROPE_DIM = 32
MLA_V_DIM = 64
ROPE_THETA = 10000.0
Q_BLOCK = 128
SC_DIM = 256
SC_WIDTH = 3
SSD_HEADS = 4
SSD_HEAD_DIM = 64
SSD_GROUPS = 2
SSD_STATE = 128
SSD_CONV_WIDTH = 4
SSD_CHUNK = 128
FFN_DIM = 2816
FFN_CONV_WIDTH = 3
NORM_EPS = 1e-6

MLA_QK_DIM = MLA_NOPE_DIM + MLA_ROPE_DIM
MLA_OUT = MLA_HEADS * MLA_V_DIM
SSD_DIM = SSD_HEADS * SSD_HEAD_DIM
SSD_CONV_DIM = SSD_DIM + 2 * SSD_GROUPS * SSD_STATE
SSD_IN = SSD_DIM + SSD_CONV_DIM + SSD_HEADS
IN_WIDTHS = (MLA_Q_LORA, MLA_KV_LORA, MLA_ROPE_DIM, SC_DIM, SC_DIM, SC_DIM, SSD_IN)
IN_SPLITS = tuple(int(v) for v in np.cumsum(IN_WIDTHS)[:-1])
D_IN = sum(IN_WIDTHS)
D_MIX = MLA_OUT + SC_DIM + SSD_DIM


def rms_norm(x, w):
    xf = x.astype(jnp.float32)
    y = xf * lax.rsqrt(jnp.mean(xf * xf, axis=-1, keepdims=True) + NORM_EPS)
    return (y * w.astype(jnp.float32)).astype(x.dtype)

def causal_dwconv(u, w):
    width = w.shape[0]
    s = u.shape[1]
    up = jnp.pad(u, ((0, 0), (width - 1, 0), (0, 0)))
    out = up[:, 0:s] * w[0]
    for i in range(1, width):
        out = out + up[:, i:i + s] * w[i]
    return out

def rope(x, cos, sin):
    x1, x2 = jnp.split(x, 2, axis=-1)
    return jnp.concatenate([x1 * cos - x2 * sin, x2 * cos + x1 * sin], axis=-1).astype(x.dtype)

def mla_mixer(c_q, c_kv, k_rope, cos, sin, q_norm, w_q_up, kv_norm, w_kv_up):
    b, s, _ = c_q.shape
    q = (rms_norm(c_q, q_norm) @ w_q_up).reshape(b, s, MLA_HEADS, MLA_QK_DIM)
    q_nope = q[..., :MLA_NOPE_DIM]
    q_rope = rope(q[..., MLA_NOPE_DIM:], cos[:, :, None, :], sin[:, :, None, :])
    kv = (rms_norm(c_kv, kv_norm) @ w_kv_up).reshape(b, s, MLA_HEADS, MLA_NOPE_DIM + MLA_V_DIM)
    k_nope = kv[..., :MLA_NOPE_DIM]
    v = kv[..., MLA_NOPE_DIM:]
    k_rope = rope(k_rope, cos, sin)
    scale = MLA_QK_DIM ** -0.5
    key_idx = jnp.arange(s)

    def block(i):
        start = i * Q_BLOCK
        qn = lax.dynamic_slice_in_dim(q_nope, start, Q_BLOCK, axis=1)
        qr = lax.dynamic_slice_in_dim(q_rope, start, Q_BLOCK, axis=1)
        sc = jnp.einsum("bqhd,bkhd->bhqk", qn, k_nope) + jnp.einsum("bqhd,bkd->bhqk", qr, k_rope)
        sc = sc.astype(jnp.float32) * scale
        causal = (start + jnp.arange(Q_BLOCK))[:, None] >= key_idx[None, :]
        p = jax.nn.softmax(jnp.where(causal, sc, -jnp.inf), axis=-1)
        return jnp.einsum("bhqk,bkhd->bqhd", p.astype(v.dtype), v)

    out = lax.map(block, jnp.arange(s // Q_BLOCK))
    return out.transpose(1, 0, 2, 3, 4).reshape(b, s, MLA_OUT)

def short_conv_mixer(gate_b, gate_c, h, conv_w):
    return gate_b * causal_dwconv(gate_c * h, conv_w)

def ssd_scan(xdt, a_dt, bh, ch):
    b, s, h, p = xdt.shape
    n = bh.shape[-1]
    L = SSD_CHUNK
    c = s // L
    xdt = xdt.reshape(b, c, L, h, p)
    bh = bh.reshape(b, c, L, h, n)
    ch = ch.reshape(b, c, L, h, n)
    a_cs = jnp.cumsum(a_dt.reshape(b, c, L, h).transpose(0, 3, 1, 2), axis=-1)
    diff = a_cs[..., :, None] - a_cs[..., None, :]
    tri = jnp.tril(jnp.ones((L, L), dtype=bool))
    decay_in = jnp.exp(jnp.where(tri, diff, -jnp.inf))
    scores = jnp.einsum("bclhn,bcshn->bhcls", ch, bh) * decay_in
    y_diag = jnp.einsum("bhcls,bcshp->bclhp", scores, xdt)
    decay_to_end = jnp.exp(a_cs[..., -1:] - a_cs).transpose(0, 2, 3, 1)
    chunk_states = jnp.einsum("bclhn,bclhp->bchpn", bh * decay_to_end[..., None], xdt)
    chunk_decay = jnp.exp(a_cs[..., -1]).transpose(2, 0, 1)

    def step(state, inp):
        st, dec = inp
        return state * dec[..., None, None] + st, state

    init = jnp.zeros((b, h, p, n), chunk_states.dtype)
    _, prev = lax.scan(step, init, (chunk_states.transpose(1, 0, 2, 3, 4), chunk_decay))
    prev = prev.transpose(1, 0, 2, 3, 4)
    decay_from_start = jnp.exp(a_cs).transpose(0, 2, 3, 1)
    y_off = jnp.einsum("bclhn,bchpn->bclhp", ch, prev) * decay_from_start[..., None]
    return (y_diag + y_off).reshape(b, s, h, p)

def ssd_mixer(zxbcdt, conv_w, conv_b, dt_bias, a_log, d_skip, norm_w):
    b, s, _ = zxbcdt.shape
    z = zxbcdt[..., :SSD_DIM]
    xbc = zxbcdt[..., SSD_DIM:SSD_DIM + SSD_CONV_DIM]
    dt = zxbcdt[..., SSD_DIM + SSD_CONV_DIM:]
    xbc = jax.nn.silu(causal_dwconv(xbc, conv_w) + conv_b)
    xs = xbc[..., :SSD_DIM].reshape(b, s, SSD_HEADS, SSD_HEAD_DIM)
    heads_per_group = SSD_HEADS // SSD_GROUPS
    gn = SSD_GROUPS * SSD_STATE
    bm = jnp.repeat(xbc[..., SSD_DIM:SSD_DIM + gn].reshape(b, s, SSD_GROUPS, SSD_STATE), heads_per_group, axis=2)
    cm = jnp.repeat(xbc[..., SSD_DIM + gn:].reshape(b, s, SSD_GROUPS, SSD_STATE), heads_per_group, axis=2)
    dt = jax.nn.softplus(dt.astype(jnp.float32) + dt_bias.astype(jnp.float32))
    a = -jnp.exp(a_log.astype(jnp.float32))
    y = ssd_scan(xs * dt[..., None], dt * a, bm, cm)
    y = y + xs * d_skip[:, None]
    y = y.reshape(b, s, SSD_DIM).astype(zxbcdt.dtype)
    return rms_norm(y * jax.nn.silu(z), norm_w)

def first_inputs(seed: int = 0) -> dict:
    key = jax.random.key(seed)
    ks = jax.random.split(key, 24)
    L = DEPTH

    def normal(k, shape, scale):
        return scale * jax.random.normal(k, shape, jnp.float32)

    def gain(k, n):
        return 1.0 + normal(k, (L, n), 0.02)

    dt0 = jnp.exp(jax.random.uniform(ks[15], (L, SSD_HEADS), jnp.float32, math.log(1e-3), math.log(1e-1)))
    return {
        "x": normal(ks[0], (BATCH, SEQ, D_MODEL), 1.0),
        "positions": jnp.broadcast_to(jnp.arange(SEQ, dtype=jnp.int32), (BATCH, SEQ)),
        "norm_mix_pre": gain(ks[1], D_MODEL),
        "norm_mix_post": gain(ks[2], D_MODEL),
        "norm_ffn_pre": gain(ks[3], D_MODEL),
        "norm_ffn_post": gain(ks[4], D_MODEL),
        "w_in": normal(ks[5], (L, D_MODEL, D_IN), D_MODEL ** -0.5),
        "mla_q_norm": gain(ks[6], MLA_Q_LORA),
        "mla_w_q_up": normal(ks[7], (L, MLA_Q_LORA, MLA_HEADS * MLA_QK_DIM), MLA_Q_LORA ** -0.5),
        "mla_kv_norm": gain(ks[8], MLA_KV_LORA),
        "mla_w_kv_up": normal(ks[9], (L, MLA_KV_LORA, MLA_HEADS * (MLA_NOPE_DIM + MLA_V_DIM)), MLA_KV_LORA ** -0.5),
        "sc_conv_w": normal(ks[10], (L, SC_WIDTH, SC_DIM), SC_WIDTH ** -0.5),
        "ssd_conv_w": normal(ks[11], (L, SSD_CONV_WIDTH, SSD_CONV_DIM), SSD_CONV_WIDTH ** -0.5),
        "ssd_conv_b": normal(ks[12], (L, SSD_CONV_DIM), 0.02),
        "ssd_dt_bias": dt0 + jnp.log(-jnp.expm1(-dt0)),
        "ssd_a_log": jnp.log(jax.random.uniform(ks[13], (L, SSD_HEADS), jnp.float32, 1.0, 16.0)),
        "ssd_d": 1.0 + normal(ks[14], (L, SSD_HEADS), 0.1),
        "ssd_norm": gain(ks[16], SSD_DIM),
        "w_out": normal(ks[17], (L, D_MIX, D_MODEL), D_MIX ** -0.5),
        "ffn_w_up": normal(ks[18], (L, D_MODEL, 2 * FFN_DIM), D_MODEL ** -0.5),
        "ffn_conv_w": normal(ks[19], (L, FFN_CONV_WIDTH, 2 * FFN_DIM), FFN_CONV_WIDTH ** -0.5),
        "ffn_conv_b": normal(ks[20], (L, 2 * FFN_DIM), 0.02),
        "ffn_w_down": normal(ks[21], (L, FFN_DIM, D_MODEL), FFN_DIM ** -0.5),
    }

def first_block(x, positions, norm_mix_pre, norm_mix_post, norm_ffn_pre, norm_ffn_post, w_in,
              mla_q_norm, mla_w_q_up, mla_kv_norm, mla_w_kv_up, sc_conv_w, ssd_conv_w, ssd_conv_b,
              ssd_dt_bias, ssd_a_log, ssd_d, ssd_norm, w_out, ffn_w_up, ffn_conv_w, ffn_conv_b,
              ffn_w_down):
    inv_freq = 1.0 / (ROPE_THETA ** (jnp.arange(0, MLA_ROPE_DIM, 2, dtype=jnp.float32) / MLA_ROPE_DIM))
    ang = positions.astype(jnp.float32)[..., None] * inv_freq
    cos = jnp.cos(ang).astype(x.dtype)
    sin = jnp.sin(ang).astype(x.dtype)
    for l in range(DEPTH):
        h = rms_norm(x, norm_mix_pre[l])
        c_q, c_kv, k_rope, sc_b, sc_c, sc_h, ssd_in = jnp.split(h @ w_in[l], IN_SPLITS, axis=-1)
        y_att = mla_mixer(c_q, c_kv, k_rope, cos, sin, mla_q_norm[l], mla_w_q_up[l], mla_kv_norm[l], mla_w_kv_up[l])
        y_conv = short_conv_mixer(sc_b, sc_c, sc_h, sc_conv_w[l])
        y_ssd = ssd_mixer(ssd_in, ssd_conv_w[l], ssd_conv_b[l], ssd_dt_bias[l], ssd_a_log[l], ssd_d[l], ssd_norm[l])
        mixed = jnp.concatenate([y_att, y_conv, y_ssd], axis=-1) @ w_out[l]
        x = x + rms_norm(mixed, norm_mix_post[l])
        h = rms_norm(x, norm_ffn_pre[l])
        u = causal_dwconv(h @ ffn_w_up[l], ffn_conv_w[l]) + ffn_conv_b[l]
        gate, up = jnp.split(u, 2, axis=-1)
        x = x + rms_norm((jax.nn.silu(gate) * up) @ ffn_w_down[l], norm_ffn_post[l])
    return x


N_HEADS_A = 4
HEAD_DIM_A = 64
W_A = N_HEADS_A * 2 * HEAD_DIM_A
N_HEADS_B = 4
HEAD_DIM_B = D_MODEL // 8
W_B = N_HEADS_B * HEAD_DIM_B
CONV_W = 4
MLSTM_CHUNK = 64
EPS = 1e-6
N_IN = 4 * W_A + 5 * W_B + 2 * N_HEADS_B + 2 * D_MODEL


def _rmsnorm(x, g):
    xf = x.astype(jnp.float32)
    y = xf * lax.rsqrt(jnp.mean(xf * xf, axis=-1, keepdims=True) + EPS)
    return (y * g.astype(jnp.float32)).astype(x.dtype)

def _split(t, sizes):
    idx = np.cumsum(sizes)[:-1].tolist()
    return jnp.split(t, idx, axis=-1)

def _causal_conv(x, w):
    S = x.shape[1]
    xp = jnp.pad(x, ((0, 0), (CONV_W - 1, 0), (0, 0)))
    y = xp[:, 0:S] * w[0]
    for k in range(1, CONV_W):
        y = y + xp[:, k:k + S] * w[k]
    return y

def _alibi_slopes(n_heads):
    return 2.0 ** (-8.0 * jnp.arange(1, n_heads + 1, dtype=jnp.float32) / n_heads)

def _diff_attention(q, k, v, lam):
    B, S, _ = q.shape
    H, d = N_HEADS_A, HEAD_DIM_A
    qh = q.reshape(B, S, H, 2, d).transpose(0, 2, 3, 1, 4)
    kh = k.reshape(B, S, H, 2, d).transpose(0, 2, 3, 1, 4)
    vh = v.reshape(B, S, H, 2 * d).transpose(0, 2, 1, 3)
    nb = S // Q_BLOCK
    q_blocks = qh.reshape(B, H, 2, nb, Q_BLOCK, d).transpose(3, 0, 1, 2, 4, 5)
    slopes = _alibi_slopes(H)
    s_pos = jnp.arange(S)
    scale = d ** -0.5

    def block(args):
        q_blk, i = args
        t_pos = i * Q_BLOCK + jnp.arange(Q_BLOCK)
        dist = (t_pos[:, None] - s_pos[None, :]).astype(jnp.float32)
        bias = jnp.where(dist >= 0, -slopes[:, None, None] * dist, -jnp.inf)
        scores = jnp.einsum('bhcqd,bhcsd->bhcqs', q_blk, kh,
                            preferred_element_type=jnp.float32) * scale + bias[None, :, None]
        p = jax.nn.softmax(scores, axis=-1)
        p = p[:, :, 0] - lam * p[:, :, 1]
        return jnp.einsum('bhqs,bhse->bhqe', p.astype(vh.dtype), vh)

    out = lax.map(block, (q_blocks, jnp.arange(nb)))
    return out.transpose(1, 0, 3, 2, 4).reshape(B, S, H, 2 * d)

def _mlstm(q, k, v, ig, fg):
    B, S, _ = q.shape
    H, d, L = N_HEADS_B, HEAD_DIM_B, MLSTM_CHUNK
    nc = S // L

    def heads(t):
        return t.astype(jnp.float32).reshape(B, nc, L, H, d).transpose(1, 0, 3, 2, 4)

    def gates(t):
        return t.astype(jnp.float32).reshape(B, nc, L, H).transpose(1, 0, 3, 2)

    qc, kc, vc = heads(q), heads(k) * (d ** -0.5), heads(v)
    igc = gates(ig)
    lfc = jax.nn.log_sigmoid(gates(fg))
    causal = jnp.tril(jnp.ones((L, L), dtype=bool))

    def body(carry, xs):
        C, n, m = carry
        qj, kj, vj, ij, lj = xs
        b = jnp.cumsum(lj, axis=-1)
        logD = b[..., :, None] - b[..., None, :] + ij[..., None, :]
        logD = jnp.where(causal, logD, -jnp.inf)
        inter = b + m[..., None]
        m_row = jnp.maximum(inter, jnp.max(logD, axis=-1))
        Dm = jnp.exp(logD - m_row[..., None])
        w_inter = jnp.exp(inter - m_row)
        Sm = jnp.einsum('bhjd,bhsd->bhjs', qj, kj) * Dm
        num = jnp.einsum('bhjs,bhse->bhje', Sm, vj) + w_inter[..., None] * jnp.einsum('bhjd,bhde->bhje', qj, C)
        den = jnp.sum(Sm, axis=-1) + w_inter * jnp.einsum('bhjd,bhd->bhj', qj, n)
        h = num / jnp.maximum(jnp.abs(den), jnp.exp(-m_row))[..., None]
        bL = b[..., -1]
        a = bL[..., None] - b + ij
        m_new = jnp.maximum(bL + m, jnp.max(a, axis=-1))
        decay = jnp.exp(bL + m - m_new)
        wk = jnp.exp(a - m_new[..., None])
        C_new = decay[..., None, None] * C + jnp.einsum('bhs,bhsd,bhse->bhde', wk, kj, vj)
        n_new = decay[..., None] * n + jnp.einsum('bhs,bhsd->bhd', wk, kj)
        return (C_new, n_new, m_new), h

    init = (jnp.zeros((B, H, d, d), jnp.float32), jnp.zeros((B, H, d), jnp.float32),
            jnp.zeros((B, H), jnp.float32))
    _, hs = lax.scan(body, init, (qc, kc, vc, igc, lfc))
    return hs.transpose(1, 0, 3, 2, 4).reshape(B, S, H, d)

def second_inputs(seed: int = 0) -> dict:
    key = jax.random.key(seed)
    ks = jax.random.split(key, 14)
    nrm = jax.random.normal
    x = nrm(ks[0], (BATCH, SEQ, D_MODEL), jnp.float32)
    norm_pre = 1.0 + 0.05 * nrm(ks[1], (DEPTH, D_MODEL), jnp.float32)
    norm_post = 1.0 + 0.05 * nrm(ks[2], (DEPTH, D_MODEL), jnp.float32)
    w_in = nrm(ks[3], (DEPTH, D_MODEL, N_IN), jnp.float32) * D_MODEL ** -0.5
    b_i = 0.1 * nrm(ks[4], (DEPTH, N_HEADS_B), jnp.float32)
    b_f = jnp.linspace(3.0, 6.0, N_HEADS_B, dtype=jnp.float32)[None, :] + 0.01 * nrm(ks[5], (DEPTH, N_HEADS_B), jnp.float32)
    b_if = jnp.concatenate([b_i, b_f], axis=-1)
    conv_qk = nrm(ks[6], (DEPTH, CONV_W, 2 * W_B), jnp.float32) * CONV_W ** -0.5
    lambda_qk = 0.1 * nrm(ks[7], (DEPTH, 4, HEAD_DIM_A), jnp.float32)
    norm_a = 1.0 + 0.05 * nrm(ks[8], (DEPTH, W_A), jnp.float32)
    norm_b = 1.0 + 0.05 * nrm(ks[9], (DEPTH, W_B), jnp.float32)
    w_a = nrm(ks[10], (DEPTH, W_A, D_MODEL), jnp.float32) * W_A ** -0.5
    w_b = nrm(ks[11], (DEPTH, W_B, D_MODEL), jnp.float32) * W_B ** -0.5
    w_out = nrm(ks[12], (DEPTH, D_MODEL, D_MODEL), jnp.float32) * D_MODEL ** -0.5
    return {"x": x, "norm_pre": norm_pre, "norm_post": norm_post, "w_in": w_in,
            "b_if": b_if, "conv_qk": conv_qk, "lambda_qk": lambda_qk,
            "norm_a": norm_a, "norm_b": norm_b, "w_a": w_a, "w_b": w_b, "w_out": w_out}

def second_block(x, norm_pre, norm_post, w_in, b_if, conv_qk, lambda_qk, norm_a, norm_b, w_a, w_b, w_out):
    B, S, _ = x.shape
    H_A, H_B = N_HEADS_A, N_HEADS_B
    sizes = [W_A, W_A, W_A, W_A, W_B, W_B, W_B, W_B, W_B, H_B, H_B, D_MODEL, D_MODEL]
    for l in range(DEPTH):
        h = _rmsnorm(x, norm_pre[l])
        proj = jnp.einsum('bsd,dn->bsn', h, w_in[l])
        qa, ka, va, za, qb, kb, vb, ob, zb, igb, fgb, ga, gb = _split(proj, sizes)

        lam_init = 0.8 - 0.6 * math.exp(-0.3 * l)
        lq = lambda_qk[l].astype(jnp.float32)
        lam = jnp.exp(jnp.sum(lq[0] * lq[1])) - jnp.exp(jnp.sum(lq[2] * lq[3])) + lam_init
        oa = _diff_attention(qa, ka, va, lam)
        oa = _rmsnorm(oa, norm_a[l].reshape(H_A, 2 * HEAD_DIM_A)) * (1.0 - lam_init)
        ya = oa.reshape(B, S, W_A) * jax.nn.silu(za)

        qk = jax.nn.silu(_causal_conv(jnp.concatenate([qb, kb], axis=-1), conv_qk[l]))
        qb_c, kb_c = qk[..., :W_B], qk[..., W_B:]
        ig = igb + b_if[l, :H_B]
        fg = fgb + b_if[l, H_B:]
        hb = _mlstm(qb_c, kb_c, vb, ig, fg)
        hb = jax.nn.sigmoid(ob.astype(jnp.float32)).reshape(B, S, H_B, HEAD_DIM_B) * hb
        hb = _rmsnorm(hb, norm_b[l].reshape(H_B, HEAD_DIM_B)).astype(x.dtype)
        yb = hb.reshape(B, S, W_B) * jax.nn.silu(zb)

        merged = (jax.nn.sigmoid(ga) * jnp.einsum('bsw,wd->bsd', ya, w_a[l])
                  + jax.nn.sigmoid(gb) * jnp.einsum('bsw,wd->bsd', yb, w_b[l]))
        out = jnp.einsum('bsd,de->bse', merged, w_out[l])
        x = x + _rmsnorm(out, norm_post[l])
    return x


def setup_inputs(seed=0):
    out = dict(first_inputs(seed))
    for name, value in second_inputs(seed + 1).items():
        if name != "x":
            out[name + "_2"] = value
    return out


def reference(
    x, positions, norm_mix_pre, norm_mix_post, norm_ffn_pre, norm_ffn_post, w_in, mla_q_norm,
    mla_w_q_up, mla_kv_norm, mla_w_kv_up, sc_conv_w, ssd_conv_w, ssd_conv_b, ssd_dt_bias,
    ssd_a_log, ssd_d, ssd_norm, w_out, ffn_w_up, ffn_conv_w, ffn_conv_b, ffn_w_down, norm_pre_2,
    norm_post_2, w_in_2, b_if_2, conv_qk_2, lambda_qk_2, norm_a_2, norm_b_2, w_a_2, w_b_2,
    w_out_2,
):
    x = first_block(
        x, positions, norm_mix_pre, norm_mix_post, norm_ffn_pre, norm_ffn_post, w_in,
        mla_q_norm, mla_w_q_up, mla_kv_norm, mla_w_kv_up, sc_conv_w, ssd_conv_w, ssd_conv_b,
        ssd_dt_bias, ssd_a_log, ssd_d, ssd_norm, w_out, ffn_w_up, ffn_conv_w, ffn_conv_b,
        ffn_w_down,
    )
    return second_block(
        x, norm_pre_2, norm_post_2, w_in_2, b_if_2, conv_qk_2, lambda_qk_2, norm_a_2, norm_b_2,
        w_a_2, w_b_2, w_out_2,
    )


_drawn_inputs = setup_inputs


def setup_inputs(seed=0):
    import zlib

    import numpy as np

    out = dict(_drawn_inputs(seed))
    spreads = {}
    factors = {'norm_ffn_pre': 2.82,
     'norm_ffn_post': 11.037,
     'mla_q_norm': 8.0,
     'mla_kv_norm': 8.0,
     'ssd_conv_b': 7.781,
     'ssd_dt_bias': 22.368,
     'ssd_norm': 30.112,
     'norm_a_2': 111.666,
     'norm_b_2': 96.828,
     'ssd_a_log': 8.0,
     'ffn_conv_b': 4.972,
     'norm_post_2': 13.955}
    for name, (base, spread) in spreads.items():
        noise = np.random.default_rng([zlib.crc32(name.encode()), seed]).standard_normal(out[name].shape)
        drawn = base * np.exp(spread * noise) if base else spread * noise
        out[name] = __import__('jax').numpy.asarray(drawn.astype(out[name].dtype))
    for name, factor in factors.items():
        out[name] = (out[name] * factor).astype(out[name].dtype)
    return out
```

```python
from contextlib import ExitStack, contextmanager

import numpy as np

import concourse.bass as bass
from concourse import mybir

ALU = mybir.AluOpType
ACT = mybir.ActivationFunctionType
AX = mybir.AxisListType
F32 = mybir.dt.float32
F32R = mybir.dt.float32r
BF16 = mybir.dt.bfloat16
I32 = mybir.dt.int32

P = 128
S = 1024
D = 1024
KT = D // P
TT = S // P
HALF = 512
MLA_HEADS, QK_DIM, NOPE, ROPE = 8, 96, 64, 32
FFN = 2816
FT = FFN // P
SSD_HEADS = 4
DIFF_HEADS = 4
ML_HEADS = 4
EPS = 1e-6
LAM_INIT = 0.8 - 0.6 * float(np.exp(-0.3 * 0))

STAGE_UNITS = [("in", 18), ("mla", MLA_HEADS), ("out", KT), ("ffn", 3 * FT),
               ("diff", 4 * DIFF_HEADS), ("gates", 1), ("mlstm", 5 * ML_HEADS),
               ("merge", 3 * KT), ("out2", KT)]
FFN_PAIRS = FT // 2
STAGE_GROUPS = [("x", TT), ("in", 18), ("krot", 1), ("cols", 1), ("ssd", 2 * 11), ("mla", 11 * MLA_HEADS),
                ("out", KT), ("ffn_first", 4), ("ffn", 12 * (FFN_PAIRS - 1)), ("ffn_last", 8),
                ("diff", 22 * DIFF_HEADS), ("gates", 2), ("mlstm", 17 * ML_HEADS),
                ("merge", 4 * KT), ("out2", KT), ("y", TT)]


def starts(stages):
    at, out = 0, {}
    for name, n in stages:
        out[name] = at
        at += n
    return out, at


UNIT0, UNITS = starts(STAGE_UNITS)
GROUP0, GROUPS = starts(STAGE_GROUPS)

NORMS = [("mix_pre", 8), ("ssd", 2), ("q", 2), ("kv", 1), ("mix_post", 8), ("ffn_pre", 8),
         ("ffn_post", 8), ("pre2", 8), ("post2", 8)]
NORM_TILES0, _ = starts(NORMS)
NORM_INDEX = {name: i for i, (name, _) in enumerate(NORMS)}
SPLITS = [("mix_pre", 8), ("q", 2), ("kv", 1), ("mix", 8), ("ffn_pre", 8), ("pre2", 8), ("y", 8),
          ("merged", 8)]
SPLIT0, _ = starts(SPLITS)

VECTORS = [("norm_mix_pre", 8), ("norm_mix_post", 8), ("norm_ffn_pre", 8), ("norm_ffn_post", 8),
           ("norm_pre_2", 8), ("norm_post_2", 8), ("mla_q_norm", 2), ("mla_kv_norm", 1),
           ("ssd_norm", 2), ("sc_conv", 2 * 3), ("ssd_conv", 6 * 5), ("dt_bias", 1), ("a_log", 1),
           ("ssd_d", 2), ("ffn_conv", FT * 2 * 4), ("gate_bias", 1), ("ml_conv", ML_HEADS * 2 * 4),
           ("norm_a", 4), ("norm_b", 4), ("inv_freq", 1), ("phase", 1), ("turn", 1), ("sign", 1),
           ("eps", 1)]
VEC0, NVEC = starts(VECTORS)
SQUARES = ["ident", "ones", "upto", "rope_sum", "ahead"]


def program(nc, wts, x_in, pos, vec_in, sq_in, aug_in, lam_in, y_out):
    spill = nc.dram_tensor("x_spill", (P, KT * S), F32).ap()
    with ExitStack() as ctx:
        KB = 1024
        base = nc.sbuf_base
        base += (-base) % 64

        def at(name, kb, shape, dt=F32):
            return nc.alloc_sbuf_tensor_at(name, shape, dt, offset=base + int(kb * KB))

        def sem(name):
            return ctx.enter_context(nc.semaphore(name))

        X = at("X", 0, [P, KT, S])
        RAW = at("RAW", 32, [P, KT, S])
        HH = at("HH", 64, [P, KT, S], F32R)
        HL = at("HL", 96, [P, KT, S], F32R)
        WR = at("WR", 128, [P, 2, KT * P])
        WH = at("WH", 136, [P, 2, KT * P], F32R)
        WL = at("WL", 144, [P, 2, KT * P], F32R)
        SQ = at("SQ", 152, [P, 2, S])
        RS = at("RS", 160, [P, S])
        T = at("T", 164, [P, 2, S])
        vec = at("vec", 204, [P, NVEC])
        cols = at("cols", 204 + 1.25, [P, 16])
        sqf = at("sqf", 204 + 1.3125, [P, 4, P])
        identb = at("identb", 204 + 3.3125, [P, P], BF16)
        aheadb = at("aheadb", 204 + 3.5625, [P, P], BF16)
        zero = at("zero", 204 + 3.8125, [P, 1])
        assert NVEC * 4 <= 1.25 * KB
        ident, ones, upto, rope_sum = (sqf[:, n, :] for n in range(4))
        aheadf = at("aheadf", 152, [P, P])
        ZS = at("ZS", 172, [P, 2, S])
        XBC = at("XBC", 180, [P, 6, S])
        DR = at("DR", 64, [P, S])
        selA = at("selA", 70.5, [P, P])
        DTC = at("DTC", 71, [P, TT, SSD_HEADS])
        NAC = at("NAC", 71.125, [P, TT, SSD_HEADS])
        XD = at("XD", 72, [P, TT, 2, P])
        AB = at("AB", 80, [P, 2, S])
        DD = at("DD", 88, [P, 2, S])
        PP = at("PP", 96, [P, 2, S])
        YS = at("YS", 104, [P, 2, S])
        TAB = at("TAB", 112, [P, S])
        ANG = at("ANG", 116, [P, S])
        KK = at("KK", 120, [P, S])
        KR = at("KR", 124, [P, S])
        POSI = at("POSI", 32 + 28, [P, S], I32)
        ROWS = at("ROWS", 152, [4, 5, S])
        QNH = at("QNH", 64, [P, 2, S], F32R)
        QNL = at("QNL", 72, [P, 2, S], F32R)
        KNH = at("KNH", 80, [P, 1, S], F32R)
        KNL = at("KNL", 84, [P, 1, S], F32R)
        QOP = at("QOP", 88, [P, 2, S])
        KOP = at("KOP", 96, [P, 2, S])
        VP = at("VP", 104, [P, 2, TT, P])
        PR = at("PR", 172, [P, 2, S])
        PTB = at("PTB", 180, [P, TT, HALF])
        KV = at("KV", 196, [P, S])
        ROPE_T = at("ROPE_T", 200, [P, S])
        GH = at("GH", 172, [P, 2, S], F32R)
        GL = at("GL", 180, [P, 2, S], F32R)
        VG = at("VG", 188, [P, S])
        VU = at("VU", 192, [P, S])
        SG = at("SG", 196, [P, S])
        PRD = at("PRD", 200, [P, S])
        DQ = at("DQ", 0, [P, 2, S])
        DK = at("DK", 8, [P, 2, S])
        DVT = at("DVT", 16, [P, S])
        DV = at("DV", 20, [P, TT, P])
        DZ = at("DZ", 24, [P, S])
        DO = at("DO", 28, [P, S])
        DP = at("DP", 172, [P, 2, 2, S])
        DPT = at("DPT", 188, [P, TT, HALF])
        GR = at("GR", 0, [P, S])
        GROWS = at("GROWS", 172, [4, 7, S])
        ACOL = at("ACOL", 4, [P, TT, ML_HEADS])
        selM = at("selM", 5, [P, 2, P])
        MQ = at("MQ", 8, [P, S])
        MK = at("MK", 12, [P, S])
        MVT = at("MVT", 16, [P, S])
        MV = at("MV", 20, [P, TT, P])
        MO = at("MO", 24, [P, S])
        MZ = at("MZ", 28, [P, S])
        MC = at("MC", 172, [P, S])
        MN = at("MN", 176, [P, S])
        ME = at("ME", 180, [P, S])
        MD = at("MD", 184, [P, 2, S])
        MP = at("MP", 192, [P, 2, S])
        MH = at("MH", 200, [P, S])
        lam_sb = at("lam_sb", 172, [P, 4 * 64])
        YH = at("YH", 0, [P, KT, S], F32R)
        YL = at("YL", 172, [P, KT, S], F32R)
        MS = at("MS", 160, [P, S])
        MS2 = at("MS2", 164, [P, S])
        MA = at("MA", 168, [P, S])
        OUT2 = at("OUT2", 172, [P, KT, S])
        OUTB = at("OUTB", 64, [P, 4, S])

        PG = ctx.enter_context(nc.psum_tensor("PG", [P, 2, S], F32))
        PT = ctx.enter_context(nc.psum_tensor("PT", [P, 2, HALF], F32))
        PO = ctx.enter_context(nc.psum_tensor("PO", [P, 2, HALF], F32))
        POf = PO[:, :, :].rearrange("p a n -> p (a n)")
        PTf = PT[:, :, :].rearrange("p a n -> p (a n)")

        w_loaded = [sem("w_loaded0"), sem("w_loaded1")]
        w_hi = sem("w_hi")
        w_split = sem("w_split")
        w_used = sem("w_used")
        zero_set = sem("zero_set")
        g_ready = sem("g_ready")
        g_free = [sem("g_free0"), sem("g_free1")]
        dve_step = sem("dve_step")
        act_step = sem("act_step")
        const_in = sem("const_in")
        x_loaded = [sem(f"x_loaded{i}") for i in range(TT)]
        consts_ready = sem("consts_ready")
        x_act, x_dve = sem("x_act"), sem("x_dve")
        n_sq, n_sq_used = sem("n_sq"), sem("n_sq_used")
        n_sum, n_root = sem("n_sum"), sem("n_root")
        s_raw, s_hi, s_lo = sem("s_raw"), sem("s_hi"), sem("s_lo")
        n_done = sem("n_done")
        in_act, in_dve = sem("in_act"), sem("in_dve")
        xbc_ready = sem("xbc_ready")
        rows_act, rows_dve = sem("rows_act"), sem("rows_dve")
        pos_in, tab_r, tab_sin = sem("pos_in"), sem("tab_r"), sem("tab_sin")
        tab_done = sem("tab_done")
        ssd_rows, sel_set = sem("ssd_rows"), sem("sel_set")
        ab_ready, dd_ready, e_ready = sem("ab_ready"), sem("dd_ready"), sem("e_ready")
        pp_ready, pv_used, ssd_x = sem("pp_ready"), sem("pv_used"), sem("ssd_x")
        ssd_acc, ssd_y = sem("ssd_acc"), sem("ssd_y")
        krot_t, krot_done, vp_zero = sem("krot_t"), sem("krot_done"), sem("vp_zero")
        q_op, k_op, v_op, kv_cp = sem("q_op"), sem("k_op"), sem("v_op"), sem("kv_cp")
        m_neg, m_exp, m_prob = sem("m_neg"), sem("m_exp"), sem("m_prob")
        t_ready = sem("t_ready")
        t_free = sem("t_free")
        pv_half, att_free = sem("pv_half"), sem("att_free")
        out_act, out_dve = sem("out_act"), sem("out_dve")
        acc_zero = sem("acc_zero")
        f_act, f_silu, f_prod, f_hi, f_lo, f_down = (sem(n) for n in (
            "f_act", "f_silu", "f_prod", "f_hi", "f_lo", "f_down"))
        ffn_done = sem("ffn_done")
        spilled, aug_set, aug_k, lam_loaded, lam_prod, lam_exp, lam_ready = (sem(n) for n in (
            "spilled", "aug_set", "aug_k", "lam_loaded", "lam_prod", "lam_exp", "lam_ready"))
        d_q, d_k, d_v, d_z, d_vop = (sem(n) for n in ("d_q", "d_k", "d_v", "d_z", "d_vop"))
        d_neg, d_exp, d_prob, d_tready, d_tfree, d_half = (sem(n) for n in (
            "d_neg", "d_exp", "d_prob", "d_tready", "d_tfree", "d_half"))
        d_o, d_sq, d_root, d_y = (sem(n) for n in ("d_o", "d_sq", "d_root", "d_y"))
        aug_loaded = sem("aug_loaded")
        gate_rows, gates_ready = sem("gate_rows"), sem("gates_ready")
        a_cols, m_sel = sem("a_cols"), sem("m_sel")
        m_conv, m_taps, m_q, m_v, m_o, m_z, m_vop = (sem(n) for n in (
            "m_conv", "m_taps", "m_q", "m_v", "m_o", "m_z", "m_vop"))
        m_mn, m_me, m_dd, m_e, m_pp, m_used, m_acc, m_abs, m_h, m_sq, m_root, m_y = (
            sem(n) for n in ("m_mn", "m_me", "m_dd", "m_e", "m_pp", "m_used", "m_acc", "m_abs",
                             "m_h", "m_sq", "m_root", "m_y"))
        g_sig, g_prod, g_done = sem("g_sig"), sem("g_prod"), sem("g_done")
        o2_act, o2_dve, x_back = sem("o2_act"), sem("o2_dve"), sem("x_back")
        y_act, y_dve = sem("y_act"), sem("y_dve")
        y_stored = [sem(f"y_stored{i}") for i in range(4)]

        PRIMED = {"pe": [pv_half, d_half, m_used],
                  "act": [att_free, d_o],
                  "dve": [m_y, d_y, m_pp, g_done, d_prob, m_prob]}

        def primed(eng, semaphore, value):
            eng.wait_ge(semaphore, value + 1)

        def v(name, k=0):
            return vec[:, VEC0[name] + k:VEC0[name] + k + 1]

        class Groups:

            def __init__(self, stage, i=0, stride=0, first=0):
                self.base, self.i, self.stride = GROUP0[stage] + first, i, stride
                assert stride % 2 == 0

            def slot(self, k):
                return (self.base + k) % 2

            def psum(self, k):
                return PG[:, self.slot(k), :]

            def before(self, pe, k):
                n = (self.base + k) // 2
                if n or not isinstance(self.i, int):
                    pe.wait_ge(g_free[self.slot(k)], self.i * (self.stride // 2) + n)

            def ready(self, eng, k):
                eng.wait_ge(g_ready, self.i * self.stride + (self.base + k + 1))

            def free(self, k):
                return g_free[self.slot(k)]

            def wait_free(self, eng, k):
                eng.wait_ge(g_free[self.slot(k)],
                            self.i * (self.stride // 2) + ((self.base + k) // 2 + 1))

        class Steps:

            def __init__(self, eng, semaphore):
                self.eng, self.sem, self.n, self.off = eng, semaphore, 0, 0

            def __call__(self, ins):
                ins.then_inc(self.sem, 1)
                self.n += 1
                self.eng.wait_ge(self.sem, self.off + self.n)

            @contextmanager
            def loop(self, start, end, per):
                n0 = self.n
                with self.eng.Fori(start, end) as i:
                    self.off = i * per - start * per
                    yield i
                assert self.n - n0 == per, (self.n - n0, per)
                self.off, self.n = 0, n0 + per * (end - start)

        def unit_slot(stage, k):
            return (UNIT0[stage] + k) % 2

        NDONE, total = {}, 0
        for name, tiles in NORMS:
            if name in ("ssd", "mix_post", "ffn_post", "post2"):
                total += tiles
                NDONE[name] = total

        def attention(pe, g, k0, comps, operands, probs, ptb, vals, head, sems, opens, closes, acc):
            prob_ready, tr_ready, tr_free, half_done = sems

            def scores(t):
                for c in range(comps):
                    q, k = operands(c)
                    n = k0 + comps * t + c
                    g.before(pe, n)
                    for h in range(t // 4 + 1):
                        end = min((h + 1) * HALF, (t + 1) * P)
                        pe.matmul(g.psum(n)[:, h * HALF:end], q[:, t * P:(t + 1) * P],
                                  k[:, h * HALF:end], start=True, stop=end != (t + 1) * P)
                    pe.matmul(g.psum(n)[:, t * P:(t + 1) * P], identb[:, :], aheadb[:, :],
                              start=False, stop=True).then_inc(g_ready, 1)

            def transposes(t):
                primed(pe, prob_ready, head * TT + (t + 1))
                for q in range(t // 4 + 1):
                    n = t if t < 4 else 4 + 2 * (t - 4) + q
                    if n >= 2:
                        pe.wait_ge(tr_free, head * 12 + (n - 1))
                    for b in range(4 * q, min(4 * q + 4, t + 1)):
                        m = pe.transpose(PT[:, n % 2, (b - 4 * q) * P:(b - 4 * q + 1) * P],
                                         probs(t)[:, b * P:(b + 1) * P], ident)
                    m.then_inc(tr_ready, 1)

            def values(h):
                pe.wait_ge(tr_free, head * 12 + (4 if h == 0 else 12))
                if acc is not None and h == 0:
                    primed(pe, acc[0], acc[1])
                for j in range(4 * h + 4):
                    a = max(0, j * P - h * HALF)
                    m = pe.matmul(PO[:, h, a:HALF], vals[:, j, :], ptb[:, j, a:HALF],
                                  start=opens and j == 0, stop=closes and j == 4 * h + 3)
                m.then_inc(half_done, 1)

            scores(0)
            for t in range(TT):
                if t + 1 < TT:
                    scores(t + 1)
                if t == 4:
                    values(0)
                transposes(t)
            values(1)

        def evacuate(act, exp, ptb, head, tr_ready, tr_free, half_done):
            exp(0)
            for t in range(TT):
                if t + 1 < TT:
                    exp(t + 1)
                for q in range(t // 4 + 1):
                    n = t if t < 4 else 4 + 2 * (t - 4) + q
                    act.wait_ge(tr_ready, head * 12 + (n + 1))
                    if t == 4 and q == 0:
                        primed(act, half_done, head * 2 + 1)
                    if t == 0:
                        primed(act, half_done, head * 2)
                    m = min(4, t + 1 - 4 * q)
                    act.activation(ptb[:, 4 * q:4 * q + m, (t % 4) * P:(t % 4 + 1) * P],
                                   PT[:, n % 2, 0:m * P].rearrange("p (b n) -> p b n", b=m),
                                   ACT.Copy).then_inc(tr_free, 1)

        block = ctx.enter_context(nc.Block())

        @block.sync
        def _(sp):
            sp.dma_start(vec[:, :], vec_in).then_inc(const_in, 16)
            sp.dma_start(sqf[:, :, :], sq_in[:, 0:4, :]).then_inc(const_in, 16)
            sp.dma_start(aheadf[:, :], sq_in[:, 4, :]).then_inc(const_in, 16)
            for t in range(TT):
                sp.dma_start(RAW[:, t, :], x_in[t * P:(t + 1) * P, :]).then_inc(x_loaded[t], 16)

            def load(u, s):
                sp.dma_start(WR[:, s, :], u).then_inc(w_loaded[s], 16)

            load(wts[0], 0)
            load(wts[1], 1)
            with sp.Fori(1, UNITS // 2) as i:
                for s in range(2):
                    sp.wait_ge(w_split, 2 * i + (s - 1))
                    load(wts[bass.ds(2 * i + s, 1)].rearrange("a p n -> p (a n)"), s)
            sp.wait_ge(w_split, UNITS - 2)
            load(wts[UNITS - 1], 0)

        @block.gpsimd
        def _(pool):
            pool.memset(zero[:, :], 0.0).then_inc(zero_set, 1)
            pool.wait_ge(zero_set, 1)

            def split(i, s, reused):
                pool.wait_ge(w_loaded[s], 16 * i + 16)
                if reused:
                    pool.wait_ge(w_used, 2 * i + s)
                pool.tensor_tensor(WH[:, s, :], WR[:, s, :], zero[:, :].to_broadcast([P, KT * P]),
                                   ALU.add).then_inc(w_hi, 1)
                pool.wait_ge(w_hi, 2 * i + (s + 1))
                pool.tensor_tensor(WL[:, s, :], WR[:, s, :], WH[:, s, :].bitcast(F32),
                                   ALU.subtract).then_inc(w_split, 1)

            split(0, 0, False)
            split(0, 1, False)
            with pool.Fori(1, UNITS // 2) as i:
                for s in range(2):
                    split(i, s, True)
            split(UNITS // 2, 0, True)

        @block.tensor
        def _(pe):
            for semaphore in PRIMED["pe"]:
                pe.sem_inc(semaphore, 1)

            def product(out, blocks, first=None):
                for h in range(2):
                    cut = slice(h * HALF, (h + 1) * HALF)
                    for n, (slot, b, hi, lo) in enumerate(blocks):
                        w = slice(b * P, (b + 1) * P)
                        last = n == len(blocks) - 1
                        m = pe.matmul(out[:, cut], WH[:, slot, w], hi[:, cut], start=n == 0, stop=False)
                        if first is not None and h == 0 and n == 0:
                            m.then_inc(first, 1)
                        pe.matmul(out[:, cut], WH[:, slot, w], lo[:, cut], start=False, stop=False)
                        m = pe.matmul(out[:, cut], WL[:, slot, w], hi[:, cut], start=False, stop=last)
                return m

            def unit(stage, k, i=0, stride=0):
                pe.wait_ge(w_split, i * stride + (UNIT0[stage] + k + 1))
                return unit_slot(stage, k)

            def projection(stage, g, k, u, hi, lo, i=0, stride=0):
                slot = unit(stage, u, i, stride)
                g.before(pe, k)
                product(g.psum(k), [(slot, b, hi[:, b, :], lo[:, b, :]) for b in range(KT)],
                        w_used).then_inc(g_ready, 1)

            def norm(name):
                tiles, t0, n = dict(NORMS)[name], NORM_TILES0[name], NORM_INDEX[name]
                for k in range(tiles):
                    pe.wait_ge(n_sq, t0 + k + 1)
                    for h in range(2):
                        m = pe.matmul(PO[:, h, :], ones, SQ[:, k % 2, h * HALF:(h + 1) * HALF],
                                      start=k == 0, stop=k == tiles - 1)
                        if h == 1:
                            m.then_inc(n_sq_used, 1)

            def wait_split(name):
                pe.wait_ge(s_lo, SPLIT0[name] + dict(SPLITS)[name])

            def turn(out, src, g=None, k=None):
                for t in range(TT):
                    m = pe.transpose(out[:, t * P:(t + 1) * P], src[:, t * P:(t + 1) * P], ident)
                return m

            pe.wait_ge(consts_ready, 1)
            g = Groups("x")
            for t in range(TT):
                pe.wait_ge(x_loaded[t], 16)
                g.before(pe, t)
                turn(g.psum(t), RAW[:, t, :]).then_inc(g_ready, 1)
            norm("mix_pre")

            wait_split("mix_pre")
            with pe.Fori(0, 9) as i:
                g = Groups("in", i, 2)
                for k in range(2):
                    projection("in", g, k, k, HH, HL, i, 2)

            g = Groups("krot")
            pe.wait_ge(krot_t, 1)
            g.before(pe, 0)
            for h in range(2):
                m = pe.matmul(g.psum(0)[:, h * HALF:(h + 1) * HALF], rope_sum,
                              RAW[:, 3, h * HALF:(h + 1) * HALF], start=True, stop=True)
            m.then_inc(g_ready, 1)
            g = Groups("cols")
            pe.wait_ge(ssd_rows, 1)
            g.before(pe, 0)
            turn(g.psum(0), DR[:, :]).then_inc(g_ready, 1)

            pe.wait_ge(xbc_ready, 6)
            for grp in range(2):
                g = Groups("ssd", first=11 * grp)
                g.before(pe, 0)
                turn(g.psum(0), XBC[:, grp, :]).then_inc(g_ready, 1)
                for hh in range(2):
                    pe.wait_ge(sel_set, 2 * grp + hh + 1)
                    g.before(pe, 1 + hh)
                    for h in range(2):
                        m = pe.matmul(g.psum(1 + hh)[:, h * HALF:(h + 1) * HALF], selA[:, :],
                                      DR[:, h * HALF:(h + 1) * HALF], start=True, stop=True)
                    m.then_inc(g_ready, 1)

                def scores(j):
                    g.before(pe, 3 + j)
                    for h in range(j // 4, 2):
                        a = max(h * HALF, j * P)
                        m = pe.matmul(g.psum(3 + j)[:, a:(h + 1) * HALF],
                                      XBC[:, 2 + grp, j * P:(j + 1) * P],
                                      XBC[:, 4 + grp, a:(h + 1) * HALF], start=True, stop=True)
                    m.then_inc(g_ready, 1)

                def values(j):
                    for hh in range(2):
                        pe.wait_ge(pp_ready, 16 * grp + 2 * j + hh + 1)
                        for h in range(j // 4, 2):
                            a = max(h * HALF, j * P)
                            m = pe.matmul(PO[:, h, a - h * HALF:HALF], XD[:, j, hh, :],
                                          PP[:, hh, a:(h + 1) * HALF],
                                          start=j == 0 and hh == 0,
                                          stop=hh == 1 and j == 4 * h + 3)
                        m.then_inc(pv_used, 1)

                pe.wait_ge(ssd_x, grp + 1)
                if grp:
                    pe.wait_ge(ssd_acc, grp)
                for j in range(TT):
                    scores(j)
                    if j:
                        values(j - 1)
                values(TT - 1)
            pe.wait_ge(ssd_acc, 2)
            norm("ssd")
            norm("q")
            norm("kv")

            wait_split("kv")
            pe.wait_ge(krot_done, 2)
            with pe.Fori(0, MLA_HEADS // 2) as i:
                g = Groups("mla", i, 22)
                for hh in range(2):
                    o = 11 * hh
                    slot = unit("mla", hh, i, 2)
                    g.before(pe, o)
                    product(g.psum(o), [(slot, b, QNH[:, b, :], QNL[:, b, :]) for b in range(2)],
                            w_used).then_inc(g_ready, 1)
                    g.before(pe, o + 1)
                    product(g.psum(o + 1), [(slot, 2, KNH[:, 0, :], KNL[:, 0, :])]).then_inc(g_ready, 1)
                    pe.wait_ge(kv_cp, 2 * i + (hh + 1))
                    g.before(pe, o + 2)
                    turn(g.psum(o + 2), KV[:, :]).then_inc(g_ready, 1)
                    pe.wait_ge(q_op, 2 * i + (hh + 1))
                    pe.wait_ge(k_op, 2 * i + (hh + 1))
                    pe.wait_ge(v_op, 2 * i + (hh + 1))
                    attention(pe, g, o + 3, 1, lambda c: (QOP[:, hh, :], KOP[:, hh, :]),
                              lambda t: PR[:, t % 2, :], PTB, VP[:, hh, :, :], i * 2 + hh,
                              (m_prob, t_ready, t_free, pv_half), hh == 0, hh == 1,
                              (att_free, i) if hh == 0 else None)

            wait_split("mix")
            with pe.Fori(0, KT // 2) as i:
                g = Groups("out", i, 2)
                for k in range(2):
                    projection("out", g, k, k, HH, HL, i, 2)
            norm("mix_post")
            norm("ffn_pre")

            wait_split("ffn_pre")
            DOWN = 8

            def gate_up(g, k, u, i=0, stride=0):
                for n in range(2):
                    projection("ffn", g, k + n, u + n, HH, HL, i, stride)

            def down(g, k, u, pair, i=0, stride=0):
                pe.wait_ge(f_lo, 2 * pair + 2)
                for m in range(DOWN):
                    if m % 4 == 0:
                        slot = unit("ffn", u + m // 4, i, stride)
                    g.before(pe, k + m)
                    last = product(g.psum(k + m), [(slot, 2 * (m % 4) + b, GH[:, b, :], GL[:, b, :])
                                                   for b in range(2)], w_used if m % 4 == 0 else None)
                    last.then_inc(g_ready, 1)

            g = Groups("ffn_first")
            gate_up(g, 0, 0)
            gate_up(g, 2, 2)
            with pe.Fori(0, FFN_PAIRS - 1) as i:
                g = Groups("ffn", i, 12)
                gate_up(g, 0, 4, i, 6)
                down(g, 2, 6, i, i, 6)
                gate_up(g, 10, 8, i, 6)
            g = Groups("ffn_last")
            down(g, 0, 4 + 6 * (FFN_PAIRS - 1), FFN_PAIRS - 1)
            norm("ffn_post")
            norm("pre2")

            wait_split("pre2")
            pe.wait_ge(aug_set, 1)
            with pe.Fori(0, DIFF_HEADS) as i:
                g = Groups("diff", i, 22)
                for k in range(4):
                    projection("diff", g, k, k, HH, HL, i, 4)
                pe.wait_ge(d_v, i + 1)
                g.before(pe, 4)
                turn(g.psum(4), DVT[:, :]).then_inc(g_ready, 1)
                pe.wait_ge(d_q, i + 1)
                pe.wait_ge(d_k, i + 1)
                pe.wait_ge(d_vop, i + 1)
                attention(pe, g, 5, 2, lambda c: (DQ[:, c, :], DK[:, c, :]),
                          lambda t: DP[:, t % 2, 0, :], DPT, DV[:, :, :], i,
                          (d_prob, d_tready, d_tfree, d_half), True, True, (d_o, i))
                g.before(pe, 21)
                pe.wait_ge(d_sq, i + 1)
                for h in range(2):
                    m = pe.matmul(g.psum(21)[:, h * HALF:(h + 1) * HALF], ones,
                                  SQ[:, 0, h * HALF:(h + 1) * HALF], start=True, stop=True)
                m.then_inc(g_ready, 1)

            g = Groups("gates")
            projection("gates", g, 0, 0, HH, HL)
            pe.wait_ge(gate_rows, 1)
            g.before(pe, 1)
            turn(g.psum(1), GR[:, :]).then_inc(g_ready, 1)
            with pe.Fori(0, ML_HEADS // 2) as i:
                g = Groups("mlstm", i, 34)
                for hh in range(2):
                    o, head = 17 * hh, 2 * i + hh
                    for k in range(5):
                        projection("mlstm", g, o + k, 5 * hh + k, HH, HL, i, 10)
                    pe.wait_ge(m_v, head + 1)
                    g.before(pe, o + 5)
                    turn(g.psum(o + 5), MVT[:, :]).then_inc(g_ready, 1)
                    pe.wait_ge(m_sel, head + 1)
                    for n in range(2):
                        g.before(pe, o + 6 + n)
                        for h in range(2):
                            m = pe.matmul(g.psum(o + 6 + n)[:, h * HALF:(h + 1) * HALF],
                                          selM[:, n, :], GR[:, h * HALF:(h + 1) * HALF],
                                          start=True, stop=True)
                        m.then_inc(g_ready, 1)
                    pe.wait_ge(m_q, 2 * head + 2)
                    pe.wait_ge(m_vop, head + 1)

                    def scores(j):
                        g.before(pe, o + 8 + j)
                        for h in range(j // 4, 2):
                            a = max(h * HALF, j * P)
                            m = pe.matmul(g.psum(o + 8 + j)[:, a:(h + 1) * HALF],
                                          MK[:, j * P:(j + 1) * P], MQ[:, a:(h + 1) * HALF],
                                          start=True, stop=True)
                        m.then_inc(g_ready, 1)

                    def values(j):
                        primed(pe, m_pp, 8 * head + j + 1)
                        for lhs, acc in ((MV[:, j, :], PO), (ones, PT)):
                            for h in range(j // 4, 2):
                                a = max(h * HALF, j * P)
                                m = pe.matmul(acc[:, h, a - h * HALF:HALF], lhs,
                                              MP[:, j % 2, a:(h + 1) * HALF],
                                              start=j == 0, stop=j == 4 * h + 3)
                        m.then_inc(m_used, 1)

                    primed(pe, m_y, head)
                    for j in range(TT):
                        scores(j)
                        if j:
                            values(j - 1)
                    values(TT - 1)
                    pe.wait_ge(m_sq, head + 1)
                    g.before(pe, o + 16)
                    for h in range(2):
                        m = pe.matmul(g.psum(o + 16)[:, h * HALF:(h + 1) * HALF], ones,
                                      SQ[:, 0, h * HALF:(h + 1) * HALF], start=True, stop=True)
                    m.then_inc(g_ready, 1)

            wait_split("y")
            with pe.Fori(0, KT // 2) as i:
                g = Groups("merge", i, 8)
                for n in range(2):
                    for k in range(2):
                        projection("merge", g, 4 * n + k, 3 * n + k, HH, HL, i, 6)
                    slot = unit("merge", 3 * n + 2, i, 6)
                    for k in range(2):
                        g.before(pe, 4 * n + 2 + k)
                        product(g.psum(4 * n + 2 + k),
                                [(slot, 4 * k + b, YH[:, 4 * k + b, :], YL[:, 4 * k + b, :])
                                 for b in range(4)], w_used if k == 0 else None).then_inc(g_ready, 1)
            wait_split("merged")
            with pe.Fori(0, KT // 2) as i:
                g = Groups("out2", i, 2)
                for k in range(2):
                    projection("out2", g, k, k, HH, HL, i, 2)
            norm("post2")
            pe.wait_ge(n_done, NDONE["post2"])
            g = Groups("y")
            for t in range(TT):
                g.before(pe, t)
                for k in range(KT):
                    m = pe.transpose(g.psum(t)[:, k * P:(k + 1) * P], X[:, k, t * P:(t + 1) * P], ident)
                m.then_inc(g_ready, 1)

        @block.scalar
        def _(act):
            for semaphore in PRIMED["act"]:
                act.sem_inc(semaphore, 1)

            step = Steps(act, act_step)

            def norm(name, src, width):
                tiles, t0, n = dict(NORMS)[name], NORM_TILES0[name], NORM_INDEX[name]
                for k in range(tiles):
                    if t0 + k >= 2:
                        act.wait_ge(n_sq_used, t0 + k - 1)
                    act.activation(SQ[:, k % 2, :], src(k), ACT.Square).then_inc(n_sq, 1)
                act.wait_ge(n_sq_used, t0 + tiles)
                act.activation(RS[:, :], POf, ACT.Sqrt, bias=v("eps"), scale=1.0 / width)\
                   .then_inc(n_root, 1)

            def split(name, hi):
                t0 = SPLIT0[name]
                for k in range(dict(SPLITS)[name]):
                    act.wait_ge(s_raw, t0 + k + 1)
                    raw = RAW[:, k, :] if name in ("mix", "y", "merged") else T[:, (t0 + k) % 2, :]
                    act.activation(hi[:, k, :], raw, ACT.Copy).then_inc(s_hi, 1)

            act.wait_ge(consts_ready, 1)
            g = Groups("x")
            for t in range(0, TT, 2):
                g.ready(act, t)
                act.activation(X[:, :, t * P:(t + 1) * P], g.psum(t).rearrange("p (k n) -> p k n", k=KT),
                               ACT.Copy).then_inc(g.free(t), 1)
            g.wait_free(act, TT - 2)
            g.wait_free(act, TT - 1)
            act.dma_start(POSI[:, :], pos.to_broadcast([P, S])).then_inc(pos_in, 16)
            norm("mix_pre", lambda k: X[:, k, :], D)
            split("mix_pre", HH)

            g = Groups("in")
            for k in range(4):
                g.ready(act, k)
                act.activation(RAW[:, k, :], g.psum(k), ACT.Copy).then_inc(g.free(k), 1)
            for j in range(2):
                k = 4 + 3 * j
                g.ready(act, k)
                if j:
                    act.wait_ge(in_dve, 3)
                else:
                    act.wait_ge(s_lo, 8)
                act.activation(T[:, 0, :], g.psum(k), ACT.Copy).then_inc(g.free(k), 1)
                g.wait_free(act, k + 1)
                act.activation(SQ[:, 0, :], T[:, 1, :], ACT.Copy, scale=v("sc_conv", 3 * j + 2))\
                   .then_inc(in_act, 1)
            for j in range(2):
                g.ready(act, 10 + j)
                act.activation(ZS[:, j, :], g.psum(10 + j), ACT.Silu).then_inc(g.free(10 + j), 1)
            for j in range(6):
                k = 12 + j
                g.ready(act, k)
                act.activation(XBC[:, j, :], g.psum(k), ACT.Identity, bias=v("ssd_conv", 5 * j + 4),
                               scale=v("ssd_conv", 5 * j + 3)).then_inc(in_act, 1)
                g.wait_free(act, k)
                act.activation(XBC[:, j, :], XBC[:, j, :], ACT.Silu).then_inc(xbc_ready, 1)

            def log1p_rows(base, rows, n_dve):
                act.wait_ge(rows_dve, n_dve + 1)
                act.activation(rows[:, 1, :], rows[:, 1, :], ACT.Exp, scale=-1.0).then_inc(rows_act, 1)
                act.wait_ge(rows_dve, n_dve + 2)
                act.activation(rows[:, 3, :], rows[:, 2, :], ACT.Ln).then_inc(rows_act, 1)

            act.activation(cols[0:4, 0:1], vec[0:4, VEC0["a_log"]:VEC0["a_log"] + 1], ACT.Exp)\
               .then_inc(rows_act, 1)
            log1p_rows(0, ROWS, 0)
            act.wait_ge(tab_r, 1)
            act.activation(TAB[:, :], KK[:, :], ACT.Sin).then_inc(tab_sin, 1)
            g = Groups("krot")
            g.ready(act, 0)
            act.activation(KR[64:128, :], g.psum(0)[64:128, :], ACT.Copy)\
               .then_inc(g.free(0), 1)

            for grp in range(2):
                g = Groups("ssd", first=11 * grp)
                for hh in range(2):
                    g.ready(act, 1 + hh)
                    if grp:
                        act.wait_ge(dd_ready, 16 * grp)
                    act.activation(AB[:, hh, :], g.psum(1 + hh), ACT.Copy).then_inc(g.free(1 + hh), 1)
                for j in range(TT):
                    for hh in range(2):
                        n = 16 * grp + 2 * j + hh
                        act.wait_ge(dd_ready, n + 1)
                        act.activation(DD[:, hh, j * P:], DD[:, hh, j * P:], ACT.Exp).then_inc(e_ready, 1)
            act.wait_ge(ssd_y, 2)
            norm("ssd", lambda k: YS[:, k, :], 256)
            act.wait_ge(n_done, NDONE["ssd"])
            norm("q", lambda k: RAW[:, k, :], 256)
            split("q", QNH)
            norm("kv", lambda k: RAW[:, 2, :], 128)
            split("kv", KNH)

            act.wait_ge(krot_done, 1)
            for hh in range(2):
                m = act.activation(KOP[64:128, hh, :], KR[64:128, :], ACT.Copy)
            m.then_inc(krot_done, 1)
            with act.Fori(0, MLA_HEADS // 2) as i:
                g = Groups("mla", i, 22)
                for hh in range(2):
                    o = 11 * hh
                    head = 2 * i + hh
                    g.ready(act, o + 1)
                    act.activation(KOP[0:64, hh, :], g.psum(o + 1)[0:64, :], ACT.Copy).then_inc(k_op, 1)
                    act.wait_ge(k_op, head + 1)
                    act.activation(KV[:, :], g.psum(o + 1), ACT.Copy).then_inc(kv_cp, 1)
                    act.wait_ge(kv_cp, head + 1)
                    act.sem_inc(g.free(o + 1), 1)

                    def exp(t):
                        act.wait_ge(m_neg, head * TT + (t + 1))
                        act.activation(PR[:, t % 2, 0:(t + 1) * P], g.psum(o + 3 + t)[:, 0:(t + 1) * P],
                                       ACT.Exp, bias=cols[:, 4 + t % 2:5 + t % 2],
                                       scale=float(QK_DIM) ** -0.5,
                                       accum_out=cols[:, 6 + t % 2:7 + t % 2]).then_inc(m_exp, 1)
                        act.wait_ge(m_exp, head * TT + (t + 1))
                        act.sem_inc(g.free(o + 3 + t), 1)

                    evacuate(act, exp, PTB, head, t_ready, t_free, pv_half)
                primed(act, pv_half, 4 * i + 4)
                act.activation(RAW[:, bass.ds(i, 1), :], POf, ACT.Copy).then_inc(att_free, 1)

            split("mix", HH)
            with act.Fori(0, KT // 2) as i:
                g = Groups("out", i, 2)
                g.ready(act, 0)
                act.activation(RAW[:, bass.ds(2 * i, 1), :], g.psum(0), ACT.Copy).then_inc(g.free(0), 1)
            g = Groups("out")
            g.wait_free(act, 6)
            g.wait_free(act, 7)
            norm("mix_post", lambda k: RAW[:, k, :], D)
            act.wait_ge(n_done, NDONE["mix_post"])
            norm("ffn_pre", lambda k: X[:, k, :], D)
            split("ffn_pre", HH)

            def ffn_vec(part, tap, j, x):
                c = VEC0["ffn_conv"] + 8 * x + 4 * part + tap
                if isinstance(j, int):
                    return vec[:, c + 16 * j:c + 16 * j + 1]
                return vec[:, bass.ds(16 * j + c, 1)]

            def tile(g, k, pair, x):
                tile_no = 2 * pair + x
                for part, buf in ((0, VG), (1, VU)):
                    g.ready(act, k + part)
                    if not (isinstance(tile_no, int) and tile_no == 0):
                        act.wait_ge(f_prod, tile_no)
                    act.activation(buf[:, :], g.psum(k + part), ACT.Identity,
                                   bias=ffn_vec(part, 3, pair, x),
                                   scale=ffn_vec(part, 2, pair, x)).then_inc(f_act, 1)
                    if part == 0:
                        g.wait_free(act, k)
                        act.activation(SG[:, :], VG[:, :], ACT.Silu).then_inc(f_silu, 1)

            def hi(pair, x, downs):
                tile_no = 2 * pair + x
                act.wait_ge(f_prod, tile_no + 1)
                if downs is not None:
                    downs()
                act.activation(GH[:, x, :], PRD[:, :], ACT.Copy).then_inc(f_hi, 1)

            g = Groups("ffn_first")
            tile(g, 0, 0, 0)
            hi(0, 0, None)
            tile(g, 2, 0, 1)
            hi(0, 1, None)
            with act.Fori(1, FFN_PAIRS) as i:
                g = Groups("ffn", i, 12, first=-12)
                tile(g, 0, i, 0)
                hi(i, 0, lambda: g.ready(act, 9))
                tile(g, 10, i, 1)
                hi(i, 1, None)
            act.wait_ge(ffn_done, 1)
            act.dma_start(lam_sb[:, :], lam_in.to_broadcast([P, 4 * 64])).then_inc(lam_loaded, 16)
            norm("ffn_post", lambda k: RAW[:, k, :], D)
            act.wait_ge(n_done, NDONE["ffn_post"])
            norm("pre2", lambda k: X[:, k, :], D)
            act.dma_start(spill, X[:, :, :].rearrange("p k n -> p (k n)")).then_inc(spilled, 16)
            split("pre2", HH)

            act.wait_ge(lam_loaded, 16)
            act.wait_ge(lam_prod, 1)
            act.activation(cols[:, 8:10], cols[:, 8:10], ACT.Exp).then_inc(lam_exp, 1)
            act.wait_ge(spilled, 16)
            act.wait_ge(aug_k, 1)
            for rows, c in ((slice(64, 66), 0), (slice(0, 2), 1)):
                act.dma_start(DQ[rows, c, :], aug_in[0]).then_inc(aug_loaded, 16)
                act.dma_start(DK[rows, c, :], aug_in[1]).then_inc(aug_loaded, 16)
            act.wait_ge(aug_set, 1)
            with act.Fori(0, DIFF_HEADS) as i:
                g = Groups("diff", i, 22)
                g.ready(act, 1)
                act.activation(DK[0:64, 0, :], g.psum(1)[0:64, :], ACT.Copy)
                act.activation(DK[64:128, 1, :], g.psum(1)[64:128, :], ACT.Copy).then_inc(d_k, 1)
                act.wait_ge(d_k, i + 1)
                act.sem_inc(g.free(1), 1)
                g.ready(act, 2)
                act.activation(DVT[:, :], g.psum(2), ACT.Copy).then_inc(d_v, 1)
                act.wait_ge(d_v, i + 1)
                act.sem_inc(g.free(2), 1)
                g.ready(act, 3)
                primed(act, d_y, i)
                act.activation(DZ[:, :], g.psum(3), ACT.Silu).then_inc(g.free(3), 1)

                def exp(t):
                    act.wait_ge(d_neg, i * TT + (t + 1))
                    for c in range(2):
                        act.activation(DP[:, t % 2, c, 0:(t + 1) * P],
                                       g.psum(5 + 2 * t + c)[:, 0:(t + 1) * P], ACT.Exp,
                                       bias=cols[:, 4 + 2 * (t % 2) + c:5 + 2 * (t % 2) + c],
                                       scale=0.125,
                                       accum_out=cols[:, 10 + 2 * (t % 2) + c:11 + 2 * (t % 2) + c])\
                           .then_inc(d_exp, 1)
                        act.wait_ge(d_exp, i * (2 * TT) + (2 * t + c + 1))
                        act.sem_inc(g.free(5 + 2 * t + c), 1)

                evacuate(act, exp, DPT, i, d_tready, d_tfree, d_half)
                primed(act, d_half, 2 * i + 2)
                act.activation(SQ[:, 0, :], POf, ACT.Square).then_inc(d_sq, 1)
                act.wait_ge(d_sq, i + 1)
                act.activation(DO[:, :], POf, ACT.Copy).then_inc(d_o, 1)
                g.ready(act, 21)
                act.activation(RS[:, :], g.psum(21), ACT.Sqrt, bias=v("eps"), scale=1.0 / P)\
                   .then_inc(d_root, 1)
                act.wait_ge(d_root, i + 1)
                act.sem_inc(g.free(21), 1)

            g = Groups("gates")
            g.ready(act, 0)
            primed(act, d_y, DIFF_HEADS)
            gb = VEC0["gate_bias"]
            act.activation(GROWS[:, 5, :], g.psum(0)[0:4, :], ACT.Identity, bias=vec[0:4, gb:gb + 1])
            act.activation(GROWS[:, 0, :], g.psum(0)[32:36, :], ACT.Identity,
                           bias=vec[32:36, gb:gb + 1]).then_inc(g.free(0), 1)
            log1p_rows(1, GROWS, 2)
            with act.Fori(0, ML_HEADS // 2) as i:
                g = Groups("mlstm", i, 34)
                for hh in range(2):
                    o, head = 17 * hh, 2 * i + hh
                    primed(act, m_y, head)
                    for n, buf in ((0, MQ), (1, MK)):
                        g.ready(act, o + n)
                        c = VEC0["ml_conv"] + 4 * n + 8 * hh + 3
                        act.activation(MC[:, :], g.psum(o + n), ACT.Copy,
                                       scale=vec[:, bass.ds(16 * i + c, 1)]).then_inc(m_conv, 1)
                        g.wait_free(act, o + n)
                        act.activation(buf[:, :], MC[:, :], ACT.Silu).then_inc(m_q, 1)
                        act.wait_ge(m_q, 2 * head + (n + 1))
                    g.ready(act, o + 2)
                    act.activation(MVT[:, :], g.psum(o + 2), ACT.Copy).then_inc(m_v, 1)
                    act.wait_ge(m_v, head + 1)
                    act.sem_inc(g.free(o + 2), 1)
                    g.ready(act, o + 3)
                    act.activation(MO[:, :], g.psum(o + 3), ACT.Sigmoid).then_inc(g.free(o + 3), 1)
                    g.ready(act, o + 4)
                    act.activation(MZ[:, :], g.psum(o + 4), ACT.Silu).then_inc(g.free(o + 4), 1)
                    g.ready(act, o + 6)
                    act.activation(MN[:, :], g.psum(o + 6), ACT.Copy).then_inc(m_mn, 1)
                    act.wait_ge(m_mn, head + 1)
                    act.sem_inc(g.free(o + 6), 1)
                    g.ready(act, o + 7)
                    act.activation(ME[:, :], g.psum(o + 7), ACT.Exp).then_inc(m_me, 1)
                    act.wait_ge(m_me, head + 1)
                    act.sem_inc(g.free(o + 7), 1)
                    for j in range(TT):
                        act.wait_ge(m_dd, head * TT + (j + 1))
                        act.activation(MD[:, j % 2, j * P:], MD[:, j % 2, j * P:], ACT.Exp)\
                           .then_inc(m_e, 1)
                    primed(act, m_used, head * TT + TT)
                    act.activation(MC[:, :], PTf, ACT.Abs).then_inc(m_abs, 1)
                    act.wait_ge(m_h, head + 1)
                    act.activation(SQ[:, 0, :], MH[:, :], ACT.Square).then_inc(m_sq, 1)
                    g.ready(act, o + 16)
                    act.activation(RS[:, :], g.psum(o + 16), ACT.Sqrt, bias=v("eps"),
                                   scale=1.0 / P).then_inc(m_root, 1)
                    act.wait_ge(m_root, head + 1)
                    act.sem_inc(g.free(o + 16), 1)

            split("y", YH)
            with act.Fori(0, KT // 2) as i:
                g = Groups("merge", i, 8)
                for n in range(2):
                    tile_no = 2 * i + n
                    primed(act, g_done, tile_no)
                    g.ready(act, 4 * n)
                    act.activation(MS[:, :], g.psum(4 * n), ACT.Sigmoid).then_inc(g.free(4 * n), 1)
                    g.ready(act, 4 * n + 1)
                    act.activation(MS2[:, :], g.psum(4 * n + 1), ACT.Sigmoid)\
                       .then_inc(g.free(4 * n + 1), 1)
            split("merged", HH)
            with act.Fori(0, KT // 2) as i:
                g = Groups("out2", i, 2)
                g.ready(act, 0)
                act.activation(OUT2[:, bass.ds(2 * i, 1), :], g.psum(0), ACT.Copy).then_inc(g.free(0), 1)
            act.wait_ge(spilled, 16)
            act.wait_ge(g_ready, GROUP0["out2"])
            act.dma_start(X[:, :, :].rearrange("p k n -> p (k n)"), spill).then_inc(x_back, 16)
            g = Groups("out2")
            g.wait_free(act, 6)
            g.wait_free(act, 7)
            norm("post2", lambda k: OUT2[:, k, :], D)
            g = Groups("y")
            for t in range(TT):
                if t % 2 == 0:
                    g.ready(act, t)
                    if t >= 4:
                        act.wait_ge(y_stored[t % 4], 16)
                    act.activation(OUTB[:, t % 4, :], g.psum(t), ACT.Copy).then_inc(g.free(t), 1)
                g.wait_free(act, t)
                act.dma_start(y_out[t * P:(t + 1) * P, :], OUTB[:, t % 4, :]).then_inc(y_stored[t % 4], 16)
            for n in range(4):
                act.wait_ge(y_stored[n], 32)

        @block.vector
        def _(dve):
            for semaphore in PRIMED["dve"]:
                dve.sem_inc(semaphore, 1)

            step = Steps(dve, dve_step)

            def reciprocal_root(name):
                dve.wait_ge(n_root, NORM_INDEX[name] + 1)
                step(dve.reciprocal(RS[:, :], RS[:, :]))

            def norm_split(name, vname, src, lo):
                reciprocal_root(name)
                split(name, lambda k, out: dve.scalar_tensor_tensor(
                    out, src(k), v(vname, k), RS[:, :], ALU.mult, ALU.mult), lo)

            def split(name, make, lo):
                t0, n = SPLIT0[name], dict(SPLITS)[name]

                def low(k):
                    dve.wait_ge(s_hi, t0 + k + 1)
                    raw = RAW[:, k, :] if make is None else T[:, (t0 + k) % 2, :]
                    dve.tensor_tensor(lo[:, k, :], raw, HI[name][:, k, :].bitcast(F32),
                                      ALU.subtract).then_inc(s_lo, 1)

                if make is None:
                    for k in range(n):
                        dve.sem_inc(s_raw, 1)
                    for k in range(n):
                        low(k)
                    return
                for k in range(n):
                    if t0 + k >= 2:
                        dve.wait_ge(s_lo, t0 + k - 1)
                    make(k, T[:, (t0 + k) % 2, :]).then_inc(s_raw, 1)
                    if k:
                        low(k - 1)
                low(n - 1)

            HI = {"mix_pre": HH, "q": QNH, "kv": KNH, "mix": HH, "ffn_pre": HH, "pre2": HH,
                  "y": YH, "merged": HH}

            def norm_residual(name, vname, src):
                reciprocal_root(name)
                done = NDONE[name] - KT
                for k in range(KT):
                    if k >= 2:
                        dve.wait_ge(n_done, done + k - 1)
                    step(dve.scalar_tensor_tensor(T[:, k % 2, :], src(k), v(vname, k), RS[:, :],
                                                  ALU.mult, ALU.mult))
                    dve.tensor_tensor(X[:, k, :], X[:, k, :], T[:, k % 2, :], ALU.add)\
                       .then_inc(n_done, 1)
                dve.wait_ge(n_done, NDONE[name])

            def taps(g, k, out, weights, then):
                for d, w in enumerate(weights, 1):
                    ins = dve.scalar_tensor_tensor(out[:, d:], g.psum(k)[:, 0:S - d], w, out[:, d:],
                                                   ALU.mult, ALU.add)
                    if d < len(weights):
                        step(ins)
                    else:
                        ins.then_inc(g.free(k), 1)

            dve.wait_ge(const_in, 48)
            step(dve.tensor_copy(identb[:, :], ident))
            dve.tensor_copy(aheadb[:, :], aheadf[:, :]).then_inc(consts_ready, 1)
            dve.wait_ge(consts_ready, 1)

            g = Groups("x")
            for t in range(1, TT, 2):
                g.ready(dve, t)
                dve.tensor_copy(X[:, :, t * P:(t + 1) * P],
                                g.psum(t).rearrange("p (k n) -> p k n", k=KT)).then_inc(g.free(t), 1)
            g.wait_free(dve, TT - 2)
            g.wait_free(dve, TT - 1)
            norm_split("mix_pre", "norm_mix_pre", lambda k: X[:, k, :], HL)

            g = Groups("in")
            for j in range(2):
                k = 4 + 3 * j
                g.wait_free(dve, k)
                g.ready(dve, k + 1)
                dve.tensor_tensor(T[:, 1, :], g.psum(k + 1), T[:, 0, :], ALU.mult)\
                   .then_inc(g.free(k + 1), 1)
                dve.wait_ge(in_act, 1 if j == 0 else 2)
                g.wait_free(dve, k + 1)
                for d in (1, 2):
                    if d == 2:
                        dve.wait_ge(in_dve, 3 * j + 1)
                    dve.scalar_tensor_tensor(SQ[:, 0, d:], T[:, 1, 0:S - d], v("sc_conv", 3 * j + 2 - d),
                                             SQ[:, 0, d:], ALU.mult, ALU.add).then_inc(in_dve, 1)
                dve.wait_ge(in_dve, 3 * j + 2)
                g.ready(dve, k + 2)
                dve.tensor_tensor(RAW[:, 4 + j, :], g.psum(k + 2), SQ[:, 0, :], ALU.mult)\
                   .then_inc(g.free(k + 2), 1)
                g.wait_free(dve, k + 2)
                dve.sem_inc(in_dve, 1)
            for j in range(6):
                k = 12 + j
                dve.wait_ge(in_act, 2 + j + 1)
                g.ready(dve, k)
                taps(g, k, XBC[:, j, :], [v("ssd_conv", 5 * j + 3 - d) for d in (1, 2, 3)], None)

            def softplus(rows, raw, bias, n_act):
                x0, y, u, l, s = (rows[:, n, :] for n in range(5))
                if raw is not None:
                    step(dve.tensor_scalar(x0, raw, bias, None, ALU.add))
                dve.scalar_tensor_tensor(y, x0, -1.0, x0, ALU.mult, ALU.max).then_inc(rows_dve, 1)
                dve.wait_ge(rows_act, n_act + 1)
                dve.tensor_scalar(u, y, 1.0, None, ALU.add).then_inc(rows_dve, 1)
                step(dve.tensor_scalar(s, y, -0.25, 1.0 / 3.0, ALU.mult, ALU.add))
                step(dve.tensor_tensor(s, s, y, ALU.mult))
                step(dve.tensor_scalar(s, s, -0.5, None, ALU.add))
                step(dve.tensor_tensor(s, s, y, ALU.mult))
                step(dve.tensor_scalar(s, s, 1.0, None, ALU.add))
                step(dve.tensor_tensor(s, s, y, ALU.mult))
                dve.wait_ge(rows_act, n_act + 2)
                step(dve.tensor_tensor(s, s, l, ALU.subtract))
                step(dve.tensor_scalar(u, y, 1.0 / 64, None, ALU.is_lt))
                step(dve.tensor_tensor(s, s, u, ALU.mult))
                step(dve.tensor_tensor(l, l, s, ALU.add))
                step(dve.scalar_tensor_tensor(x0, x0, 0.0, l, ALU.max, ALU.add))

            g.wait_free(dve, 3)
            g.wait_free(dve, 17)
            g.ready(dve, 17)
            step(dve.memset(DR[:, :], 0.0))
            db = VEC0["dt_bias"]
            softplus(ROWS, RAW[0:4, 3, :], vec[0:4, db:db + 1], 1)
            step(dve.tensor_copy(DR[0:4, :], ROWS[:, 0, :]))
            dve.wait_ge(rows_act, 1)
            step(dve.tensor_scalar(ROWS[:, 1, :], ROWS[:, 0, :], cols[0:4, 0:1], -1.0, ALU.mult, ALU.mult))
            step(dve.memset(ROWS[:, 2, :], 1.0))
            dve.tensor_tensor_scan(DR[32:36, :], ROWS[:, 2, :], ROWS[:, 1, :], 0.0, ALU.mult, ALU.add)\
               .then_inc(ssd_rows, 1)

            dve.wait_ge(pos_in, 16)
            step(dve.tensor_copy(KK[:, :], POSI[:, :]))
            step(dve.tensor_scalar(ANG[:, :], KK[:, :], v("inv_freq"), None, ALU.mult))
            step(dve.tensor_scalar(KK[:, :], ANG[:, :], 1.0 / (2 * np.pi), v("turn"), ALU.mult, ALU.add))
            step(dve.tensor_scalar(KK[:, :], KK[:, :], 12582912.0, None, ALU.add))
            step(dve.tensor_scalar(KK[:, :], KK[:, :], 12582912.0, None, ALU.subtract))
            c1, c2 = 6.25, 0.033203125
            for c in (c1, c2, 2 * np.pi - c1 - c2):
                step(dve.scalar_tensor_tensor(ANG[:, :], KK[:, :], -float(c), ANG[:, :],
                                              ALU.mult, ALU.add))
            step(dve.tensor_scalar(KK[:, :], ANG[:, :], v("phase"), None, ALU.add))
            dve.tensor_scalar(KK[:, :], KK[:, :], 3.1415925, -3.1415925, ALU.min, ALU.max)\
               .then_inc(tab_r, 1)
            dve.wait_ge(tab_sin, 1)
            step(dve.tensor_scalar(TAB[:, :], TAB[:, :], v("sign"), None, ALU.mult))
            step(dve.memset(TAB[0:64, :], 1.0))
            dve.tensor_tensor(RAW[:, 3, :], RAW[:, 3, :], TAB[:, :], ALU.mult).then_inc(krot_t, 1)

            g = Groups("cols")
            g.ready(dve, 0)
            turned = g.psum(0).rearrange("p (t n) -> p t n", t=TT)
            step(dve.tensor_copy(DTC[:, :, :], turned[:, :, 0:4]))
            dve.tensor_scalar(NAC[:, :, :], turned[:, :, 32:36], -1.0, None, ALU.mult)\
               .then_inc(g.free(0), 1)
            g.wait_free(dve, 0)

            dve.wait_ge(xbc_ready, 6)
            step(dve.memset(XD[:, :, :, :].rearrange("p a b c -> p (a b c)"), 0.0))
            for grp in range(2):
                g = Groups("ssd", first=11 * grp)
                g.ready(dve, 0)
                if grp:
                    dve.wait_ge(pv_used, 16)
                xt = g.psum(0).rearrange("p (t n) -> p t n", t=TT)
                for hh in range(2):
                    c = 2 * grp + hh
                    ins = dve.tensor_tensor(XD[:, :, hh, hh * 64:(hh + 1) * 64],
                                            xt[:, :, hh * 64:(hh + 1) * 64],
                                            DTC[:, :, c:c + 1].to_broadcast([P, TT, 64]), ALU.mult)
                    if hh == 0:
                        step(ins)
                    else:
                        ins.then_inc(ssd_x, 1)
                dve.wait_ge(ssd_x, grp + 1)
                dve.sem_inc(g.free(0), 1)
                for hh in range(2):
                    c = 2 * grp + hh
                    if c:
                        prev = Groups("ssd", first=11 * ((c - 1) // 2))
                        prev.ready(dve, 1 + (c - 1) % 2)
                    dve.tensor_copy(selA[:, :], ident[:, 32 + c:33 + c].to_broadcast([P, P]))\
                       .then_inc(sel_set, 1)

                def exponents(j):
                    for hh in range(2):
                        n = 16 * grp + 2 * j + hh
                        c = 2 * grp + hh
                        if j == 0:
                            g.wait_free(dve, 1 + hh)
                        if n >= 2:
                            dve.wait_ge(pp_ready, n - 1)
                        dve.tensor_scalar(DD[:, hh, j * P:], AB[:, hh, j * P:],
                                          NAC[:, j, c:c + 1], 0.0, ALU.add, ALU.min)\
                           .then_inc(dd_ready, 1)

                def decayed(j):
                    g.ready(dve, 3 + j)
                    for hh in range(2):
                        n = 16 * grp + 2 * j + hh
                        dve.wait_ge(e_ready, n + 1)
                        if n >= 2:
                            dve.wait_ge(pv_used, n - 1)
                        step(dve.tensor_tensor(DD[:, hh, j * P:(j + 1) * P],
                                               DD[:, hh, j * P:(j + 1) * P], upto, ALU.mult))
                        dve.tensor_tensor(PP[:, hh, j * P:], g.psum(3 + j)[:, j * P:],
                                          DD[:, hh, j * P:], ALU.mult).then_inc(pp_ready, 1)
                    dve.wait_ge(pp_ready, 16 * grp + 2 * j + 2)
                    dve.sem_inc(g.free(3 + j), 1)

                for j in range(TT):
                    exponents(j)
                    decayed(j)
                dve.wait_ge(pv_used, 16 * grp + 16)
                dve.scalar_tensor_tensor(YS[:, grp, :], XBC[:, grp, :], v("ssd_d", grp), POf,
                                         ALU.mult, ALU.add).then_inc(ssd_acc, 1)
                dve.wait_ge(ssd_acc, grp + 1)
                dve.tensor_tensor(YS[:, grp, :], YS[:, grp, :], ZS[:, grp, :], ALU.mult)\
                   .then_inc(ssd_y, 1)
            reciprocal_root("ssd")
            for k in range(2):
                dve.scalar_tensor_tensor(RAW[:, 6 + k, :], YS[:, k, :], v("ssd_norm", k), RS[:, :],
                                         ALU.mult, ALU.mult).then_inc(n_done, 1)
            dve.wait_ge(n_done, NDONE["ssd"])
            norm_split("q", "mla_q_norm", lambda k: RAW[:, k, :], QNL)
            norm_split("kv", "mla_kv_norm", lambda k: RAW[:, 2, :], KNL)

            Groups("krot").wait_free(dve, 0)
            step(dve.memset(VP[:, :, :, :].rearrange("p a b c -> p (a b c)"), 0.0))
            dve.sem_inc(krot_done, 1)

            with step.loop(0, MLA_HEADS // 2, 2 * (TT + TT)) as i:
                g = Groups("mla", i, 22)
                for hh in range(2):
                    o, head = 11 * hh, 2 * i + hh
                    g.ready(dve, o)
                    dve.tensor_tensor(QOP[:, hh, :], g.psum(o), TAB[:, :], ALU.mult).then_inc(q_op, 1)
                    dve.wait_ge(q_op, head + 1)
                    dve.sem_inc(g.free(o), 1)
                    g.ready(dve, o + 2)
                    dve.tensor_copy(VP[:, hh, :, hh * 64:(hh + 1) * 64],
                                    g.psum(o + 2).rearrange("p (t n) -> p t n", t=TT)[:, :, 64:128])\
                       .then_inc(v_op, 1)
                    dve.wait_ge(v_op, head + 1)
                    dve.sem_inc(g.free(o + 2), 1)

                    def maximum(t):
                        g.ready(dve, o + 3 + t)
                        step(dve.reduce_max(cols[:, 2 + t % 2:3 + t % 2],
                                            g.psum(o + 3 + t)[:, 0:(t + 1) * P], AX.X))
                        if t >= 2:
                            dve.wait_ge(m_exp, head * TT + (t - 1))
                        dve.tensor_scalar(cols[:, 4 + t % 2:5 + t % 2], cols[:, 2 + t % 2:3 + t % 2],
                                          -float(QK_DIM) ** -0.5, None, ALU.mult).then_inc(m_neg, 1)

                    def normalise(t):
                        dve.wait_ge(m_exp, head * TT + (t + 1))
                        n = (t + 1) * P
                        c = 8 + t % 2
                        step(dve.reciprocal(cols[:, c:c + 1], cols[:, 6 + t % 2:7 + t % 2]))
                        dve.tensor_scalar(PR[:, t % 2, 0:n], PR[:, t % 2, 0:n], cols[:, c:c + 1], None,
                                          ALU.mult).then_inc(m_prob, 1)

                    maximum(0)
                    for t in range(TT):
                        if t + 1 < TT:
                            maximum(t + 1)
                        normalise(t)
            primed(dve, att_free, MLA_HEADS // 2)
            split("mix", None, HL)
            with dve.Fori(0, KT // 2) as i:
                g = Groups("out", i, 2)
                g.ready(dve, 1)
                dve.tensor_copy(RAW[:, bass.ds(2 * i + 1, 1), :], g.psum(1)).then_inc(g.free(1), 1)
            g = Groups("out")
            g.wait_free(dve, 6)
            g.wait_free(dve, 7)
            norm_residual("mix_post", "norm_mix_post", lambda k: RAW[:, k, :])
            step(dve.memset(RAW[:, :, :].rearrange("p k n -> p (k n)"), 0.0))
            norm_split("ffn_pre", "norm_ffn_pre", lambda k: X[:, k, :], HL)

            def ffn_vec(part, tap, j, x):
                c = VEC0["ffn_conv"] + 8 * x + 4 * part + tap
                if isinstance(j, int):
                    return vec[:, c + 16 * j:c + 16 * j + 1]
                return vec[:, bass.ds(16 * j + c, 1)]

            def tile(g, k, pair, x):
                tile_no = 2 * pair + x
                for part, buf in ((0, VG), (1, VU)):
                    dve.wait_ge(f_act, 2 * tile_no + (part + 1))
                    g.ready(dve, k + part)
                    taps(g, k + part, buf, [ffn_vec(part, 2 - d, pair, x) for d in (1, 2)], None)
                g.wait_free(dve, k + 1)
                dve.wait_ge(f_silu, tile_no + 1)
                if not (isinstance(tile_no, int) and tile_no == 0):
                    dve.wait_ge(f_lo, tile_no)
                dve.tensor_tensor(PRD[:, :], SG[:, :], VU[:, :], ALU.mult).then_inc(f_prod, 1)

            def low(pair, x):
                tile_no = 2 * pair + x
                dve.wait_ge(f_hi, tile_no + 1)
                dve.tensor_tensor(GL[:, x, :], PRD[:, :], GH[:, x, :].bitcast(F32),
                                  ALU.subtract).then_inc(f_lo, 1)

            def accumulate(g, k):
                for m in range(KT):
                    g.ready(dve, k + m)
                    dve.tensor_tensor(RAW[:, m, :], RAW[:, m, :], g.psum(k + m), ALU.add)\
                       .then_inc(g.free(k + m), 1)

            g = Groups("ffn_first")
            tile(g, 0, 0, 0)
            low(0, 0)
            tile(g, 2, 0, 1)
            low(0, 1)
            with step.loop(1, FFN_PAIRS, 4) as i:
                g = Groups("ffn", i, 12, first=-12)
                tile(g, 0, i, 0)
                accumulate(g, 2)
                g.wait_free(dve, 8)
                g.wait_free(dve, 9)
                low(i, 0)
                tile(g, 10, i, 1)
                low(i, 1)
            g = Groups("ffn_last")
            accumulate(g, 0)
            g.wait_free(dve, 6)
            g.wait_free(dve, 7)
            dve.sem_inc(ffn_done, 1)
            norm_residual("ffn_post", "norm_ffn_post", lambda k: RAW[:, k, :])
            norm_split("pre2", "norm_pre_2", lambda k: X[:, k, :], HL)

            dve.wait_ge(lam_loaded, 16)
            lam4 = lam_sb[:, :].rearrange("p (a b n) -> p a b n", a=2, b=2)
            step(dve.tensor_tensor(lam4[:, :, 0, :], lam4[:, :, 0, :], lam4[:, :, 1, :], ALU.mult))
            dve.reduce_sum(cols[:, 8:10], lam4[:, :, 0, :], AX.X).then_inc(lam_prod, 1)
            dve.wait_ge(lam_exp, 1)
            step(dve.tensor_tensor(cols[:, 8:9], cols[:, 8:9], cols[:, 9:10], ALU.subtract))
            dve.tensor_scalar(cols[:, 14:15], cols[:, 8:9], LAM_INIT, -1.0, ALU.add, ALU.mult)\
               .then_inc(lam_ready, 1)
            dve.wait_ge(lam_ready, 1)
            dve.wait_ge(spilled, 16)
            step(dve.memset(DQ[:, :, :], 0.0))
            step(dve.memset(DK[:, :, :], 0.0))
            dve.sem_inc(aug_k, 1)
            dve.wait_ge(aug_loaded, 64)
            dve.sem_inc(aug_set, 1)
            with step.loop(0, DIFF_HEADS, 3 + 2 * TT + 3 * TT + 2) as i:
                g = Groups("diff", i, 22)
                step(dve.tensor_scalar(DK[64:66, 0, :], DK[64:66, 0, :], 0.25, None, ALU.mult))
                step(dve.tensor_scalar(DK[0:2, 1, :], DK[0:2, 1, :], 0.25, None, ALU.mult))
                g.ready(dve, 0)
                step(dve.tensor_copy(DQ[0:64, 0, :], g.psum(0)[0:64, :]))
                dve.tensor_copy(DQ[64:128, 1, :], g.psum(0)[64:128, :]).then_inc(d_q, 1)
                dve.wait_ge(d_q, i + 1)
                dve.sem_inc(g.free(0), 1)
                g.ready(dve, 4)
                dve.tensor_copy(DV[:, :, :], g.psum(4).rearrange("p (t n) -> p t n", t=TT))\
                   .then_inc(d_vop, 1)
                dve.wait_ge(d_vop, i + 1)
                dve.sem_inc(g.free(4), 1)

                def maximum(t):
                    b = 4 + 2 * (t % 2)
                    for c in range(2):
                        g.ready(dve, 5 + 2 * t + c)
                        step(dve.reduce_max(cols[:, c:c + 1],
                                            g.psum(5 + 2 * t + c)[:, 0:(t + 1) * P], AX.X))
                    if t >= 2:
                        dve.wait_ge(d_exp, i * (2 * TT) + 2 * (t - 1))
                    dve.tensor_scalar(cols[:, b:b + 2], cols[:, 0:2], -0.125, None, ALU.mult)\
                       .then_inc(d_neg, 1)

                def normalise(t):
                    b = 10 + 2 * (t % 2)
                    n = (t + 1) * P
                    dve.wait_ge(d_exp, i * (2 * TT) + (2 * t + 2))
                    primed(dve, d_prob, i * TT + t)
                    step(dve.reciprocal(cols[:, 2:4], cols[:, b:b + 2]))
                    step(dve.tensor_tensor(cols[:, 3:4], cols[:, 3:4], cols[:, 14:15], ALU.mult))
                    step(dve.tensor_scalar(DP[:, t % 2, 0, 0:n], DP[:, t % 2, 0, 0:n],
                                           cols[:, 2:3], None, ALU.mult))
                    dve.scalar_tensor_tensor(DP[:, t % 2, 0, 0:n], DP[:, t % 2, 1, 0:n], cols[:, 3:4],
                                             DP[:, t % 2, 0, 0:n], ALU.mult, ALU.add)\
                       .then_inc(d_prob, 1)

                maximum(0)
                for t in range(TT):
                    if t + 1 < TT:
                        maximum(t + 1)
                    normalise(t)
                dve.wait_ge(d_root, i + 1)
                primed(dve, d_o, i + 1)
                step(dve.reciprocal(RS[:, :], RS[:, :]))
                step(dve.scalar_tensor_tensor(DO[:, :], DO[:, :], vec[:, bass.ds(i + VEC0["norm_a"], 1)],
                                              RS[:, :], ALU.mult, ALU.mult))
                dve.scalar_tensor_tensor(RAW[:, bass.ds(i, 1), :], DO[:, :], 1.0 - LAM_INIT, DZ[:, :],
                                         ALU.mult, ALU.mult).then_inc(d_y, 1)

            primed(dve, d_y, DIFF_HEADS)
            step(dve.memset(GR[:, :], 0.0))
            Groups("gates").wait_free(dve, 0)
            step(dve.tensor_scalar(GROWS[:, 0, :], GROWS[:, 0, :], -1.0, None, ALU.mult))
            softplus(GROWS, None, None, 3)
            step(dve.tensor_scalar(GROWS[:, 2, :], GROWS[:, 0, :], -1.0, None, ALU.mult))
            step(dve.memset(GROWS[:, 1, :], 1.0))
            step(dve.tensor_tensor_scan(GROWS[:, 3, :], GROWS[:, 1, :], GROWS[:, 2, :], 0.0,
                                        ALU.mult, ALU.add))
            step(dve.tensor_tensor(GROWS[:, 5, :], GROWS[:, 5, :], GROWS[:, 3, :], ALU.subtract))
            step(dve.tensor_tensor_scan(GROWS[:, 4, :], GROWS[:, 5, :], GROWS[:, 5, :], 0.0,
                                        ALU.max, ALU.max))
            step(dve.tensor_copy(GR[64:68, :], GROWS[:, 5, :]))
            step(dve.tensor_scalar(GR[0:4, :], GROWS[:, 4, :], -1.0, None, ALU.mult))
            step(dve.tensor_tensor(GROWS[:, 3, :], GROWS[:, 3, :], GROWS[:, 4, :], ALU.add))
            dve.tensor_scalar(GR[32:36, :], GROWS[:, 3, :], -1.0, None, ALU.mult).then_inc(gate_rows, 1)
            g = Groups("gates")
            g.ready(dve, 1)
            dve.tensor_copy(ACOL[:, :, :], g.psum(1).rearrange("p (t n) -> p t n", t=TT)[:, :, 64:68])\
               .then_inc(g.free(1), 1)
            g.wait_free(dve, 1)
            with step.loop(0, ML_HEADS // 2, 2 * (4 + 1 + TT + 5)) as i:
                g = Groups("mlstm", i, 34)
                for hh in range(2):
                    o, head = 17 * hh, 2 * i + hh
                    for n in range(2):
                        dve.wait_ge(m_conv, 2 * head + (n + 1))
                        c = VEC0["ml_conv"] + 4 * n + 8 * hh
                        taps(g, o + n, MC, [vec[:, bass.ds(16 * i + (c + 3 - d), 1)] for d in (1, 2, 3)],
                             None)
                    g.ready(dve, o + 5)
                    dve.tensor_copy(MV[:, :, :], g.psum(o + 5).rearrange("p (t n) -> p t n", t=TT))\
                       .then_inc(m_vop, 1)
                    dve.wait_ge(m_vop, head + 1)
                    dve.sem_inc(g.free(o + 5), 1)
                    step(dve.tensor_copy(selM[:, 0, :],
                                         ident[:, bass.ds(2 * i + hh, 1)].to_broadcast([P, P])))
                    dve.tensor_copy(selM[:, 1, :],
                                    ident[:, bass.ds(2 * i + (32 + hh), 1)].to_broadcast([P, P]))\
                       .then_inc(m_sel, 1)
                    def decayed(j):
                        g.ready(dve, o + 8 + j)
                        dve.wait_ge(m_e, head * TT + (j + 1))
                        primed(dve, m_used, head * TT + max(j - 1, 0))
                        step(dve.tensor_tensor(MD[:, j % 2, j * P:(j + 1) * P],
                                               MD[:, j % 2, j * P:(j + 1) * P], upto, ALU.mult))
                        dve.scalar_tensor_tensor(MP[:, j % 2, j * P:], g.psum(o + 8 + j)[:, j * P:],
                                                 float(P) ** -0.5, MD[:, j % 2, j * P:],
                                                 ALU.mult, ALU.mult).then_inc(m_pp, 1)
                        primed(dve, m_pp, head * TT + (j + 1))
                        dve.sem_inc(g.free(o + 8 + j), 1)

                    dve.wait_ge(m_mn, head + 1)
                    for j in range(TT):
                        acol = ACOL[:, j, bass.ds(2 * i + hh, 1)]
                        if j >= 2:
                            primed(dve, m_pp, head * TT + (j - 1))
                        else:
                            primed(dve, m_pp, head * TT)
                        dve.tensor_scalar(MD[:, j % 2, j * P:], MN[:, j * P:], acol, 0.0,
                                          ALU.add, ALU.min).then_inc(m_dd, 1)
                        if j:
                            decayed(j - 1)
                    decayed(TT - 1)
                    dve.wait_ge(m_abs, head + 1)
                    dve.wait_ge(m_me, head + 1)
                    step(dve.tensor_tensor(MC[:, :], MC[:, :], ME[:, :], ALU.max))
                    step(dve.reciprocal(MC[:, :], MC[:, :]))
                    step(dve.tensor_tensor(MH[:, :], POf, MC[:, :], ALU.mult))
                    g.wait_free(dve, o + 3)
                    dve.tensor_tensor(MH[:, :], MH[:, :], MO[:, :], ALU.mult).then_inc(m_h, 1)
                    dve.wait_ge(m_root, head + 1)
                    step(dve.reciprocal(RS[:, :], RS[:, :]))
                    dve.wait_ge(m_h, head + 1)
                    step(dve.scalar_tensor_tensor(MH[:, :], MH[:, :],
                                                  vec[:, bass.ds(2 * i + (hh + VEC0["norm_b"]), 1)],
                                                  RS[:, :], ALU.mult, ALU.mult))
                    g.wait_free(dve, o + 4)
                    dve.tensor_tensor(RAW[:, bass.ds(2 * i + (4 + hh), 1), :], MH[:, :], MZ[:, :],
                                      ALU.mult).then_inc(m_y, 1)

            primed(dve, m_y, ML_HEADS)
            split("y", None, YL)
            with step.loop(0, KT // 2, 2) as i:
                g = Groups("merge", i, 8)
                for n in range(2):
                    tile_no = 2 * i + n
                    g.wait_free(dve, 4 * n)
                    g.ready(dve, 4 * n + 2)
                    dve.tensor_tensor(MA[:, :], g.psum(4 * n + 2), MS[:, :], ALU.mult)\
                       .then_inc(g.free(4 * n + 2), 1)
                    g.wait_free(dve, 4 * n + 2)
                    g.wait_free(dve, 4 * n + 1)
                    g.ready(dve, 4 * n + 3)
                    step(dve.tensor_tensor(MS2[:, :], g.psum(4 * n + 3), MS2[:, :], ALU.mult))
                    dve.sem_inc(g.free(4 * n + 3), 1)
                    dve.tensor_tensor(RAW[:, bass.ds(2 * i + n, 1), :], MA[:, :], MS2[:, :], ALU.add)\
                       .then_inc(g_done, 1)
            primed(dve, g_done, KT)
            split("merged", None, HL)
            with dve.Fori(0, KT // 2) as i:
                g = Groups("out2", i, 2)
                g.ready(dve, 1)
                dve.tensor_copy(OUT2[:, bass.ds(2 * i + 1, 1), :], g.psum(1)).then_inc(g.free(1), 1)
            g = Groups("out2")
            g.wait_free(dve, 6)
            g.wait_free(dve, 7)
            dve.wait_ge(x_back, 16)
            norm_residual("post2", "norm_post_2", lambda k: OUT2[:, k, :])
            g = Groups("y")
            for t in range(1, TT, 2):
                g.ready(dve, t)
                if t >= 4:
                    dve.wait_ge(y_stored[t % 4], 16)
                dve.tensor_copy(OUTB[:, t % 4, :], g.psum(t)).then_inc(g.free(t), 1)


_VECTORS_P = ("norm_mix_pre", "norm_mix_post", "norm_ffn_pre", "norm_ffn_post", "norm_pre_2",
              "norm_post_2", "mla_q_norm", "mla_kv_norm", "ssd_norm")


def _blocks(w, columns):
    out = np.zeros((len(columns), P, KT, P), w.dtype)
    for u, c in enumerate(columns):
        part = w[:, c].reshape(w.shape[0] // P, P, len(c))
        out[u, :, :part.shape[0], :len(c)] = part.transpose(1, 0, 2)
    return out


def _weights(a):
    tile = lambda at: list(range(at, at + P))
    w_in = a["w_in"][0]
    c, h, z = 672, 928, 1184
    order = [tile(0), tile(128), tile(256), None]
    for j in range(2):
        order += [tile(c + j * P), tile(h + j * P), tile(416 + j * P)]
    order += [tile(z), tile(z + P)] + [tile(1440 + j * P) for j in range(6)]
    parts = _blocks(w_in, [o if o is not None else [] for o in order])
    odd = w_in.reshape(KT, P, -1).transpose(1, 0, 2)
    kr = 384
    parts[3, :, :, 0:4] = odd[:, :, 2208:2212]
    parts[3, :, :, 64:96] = odd[:, :, kr:kr + 32]
    parts[3, :, :, 96:112] = odd[:, :, kr + 16:kr + 32]
    parts[3, :, :, 112:128] = odd[:, :, kr:kr + 16]
    units = [parts]
    wq, wkv = a["mla_w_q_up"][0], a["mla_w_kv_up"][0]
    mla = np.zeros((MLA_HEADS, P, KT, P), wq.dtype)
    for n in range(MLA_HEADS):
        q = n * QK_DIM
        cols = list(range(q, q + 96)) + list(range(q + 80, q + 96)) + list(range(q + 64, q + 80))
        mla[n, :, 0:2, :] = wq[:, cols].reshape(2, P, P).transpose(1, 0, 2)
        mla[n, :, 2, :] = wkv[:, n * P:(n + 1) * P]
    units.append(mla)
    units.append(_blocks(a["w_out"][0], [tile(m * P) for m in range(KT)]))
    up, down = a["ffn_w_up"][0], a["ffn_w_down"][0]

    def gate_up(pair):
        return _blocks(up, [tile(part * FFN + (2 * pair + x) * P) for x in range(2) for part in range(2)])

    def down_of(pair):
        w = down[2 * pair * P:(2 * pair + 2) * P].reshape(2, P, 2, 4, P)
        return w.transpose(2, 1, 3, 0, 4).reshape(2, P, KT, P)

    units.append(gate_up(0))
    for pair in range(1, FFN_PAIRS):
        first = gate_up(pair)
        units += [first[0:2], down_of(pair - 1), first[2:4]]
    units.append(down_of(FFN_PAIRS - 1))
    w2 = a["w_in_2"][0]
    units.append(_blocks(w2, [tile(part * 512 + n * P) for n in range(4) for part in range(4)]))
    gates = np.zeros((1, P, KT, P), w2.dtype)
    g8 = w2[:, 4608:4616].reshape(KT, P, 8).transpose(1, 0, 2)
    gates[0, :, :, 0:4] = g8[:, :, 0:4]
    gates[0, :, :, 32:36] = g8[:, :, 4:8]
    units.append(gates)
    units.append(_blocks(w2, [tile(2048 + part * 512 + n * P) for n in range(4) for part in range(5)]))
    wa, wb = a["w_a_2"][0], a["w_b_2"][0]
    for m in range(KT):
        units.append(_blocks(w2, [tile(4616 + m * P), tile(5640 + m * P)]))
        units.append(_blocks(np.concatenate([wa, wb]), [tile(m * P)]))
    units.append(_blocks(a["w_out_2"][0], [tile(m * P) for m in range(KT)]))
    return np.concatenate(units).reshape(-1, P, KT * P)


def _vectors(a):
    out = np.zeros((P, NVEC), np.float32)

    def put(name, k, column, at=0):
        out[at:at + len(column), VEC0[name] + k] = column

    for name in _VECTORS_P:
        for k, column in enumerate(a[name][0].reshape(-1, P)):
            put(name, k, column)
    for j in range(2):
        for i in range(3):
            put("sc_conv", 3 * j + i, a["sc_conv_w"][0, i, j * P:(j + 1) * P])
    for j in range(6):
        for i in range(4):
            put("ssd_conv", 5 * j + i, a["ssd_conv_w"][0, i, j * P:(j + 1) * P])
        put("ssd_conv", 5 * j + 4, a["ssd_conv_b"][0, j * P:(j + 1) * P])
    put("dt_bias", 0, a["ssd_dt_bias"][0])
    put("a_log", 0, a["ssd_a_log"][0])
    for j in range(2):
        put("ssd_d", j, np.repeat(a["ssd_d"][0, 2 * j:2 * j + 2], 64))
    for t in range(FT):
        for part in range(2):
            at = part * FFN + t * P
            for i in range(3):
                put("ffn_conv", 8 * t + 4 * part + i, a["ffn_conv_w"][0, i, at:at + P])
            put("ffn_conv", 8 * t + 4 * part + 3, a["ffn_conv_b"][0, at:at + P])
    put("gate_bias", 0, a["b_if_2"][0, 0:4])
    put("gate_bias", 0, a["b_if_2"][0, 4:8], 32)
    for n in range(ML_HEADS):
        for part in range(2):
            for i in range(4):
                at = part * 512 + n * P
                put("ml_conv", 8 * n + 4 * part + i, a["conv_qk_2"][0, i, at:at + P])
        put("norm_a", n, a["norm_a_2"][0, n * P:(n + 1) * P])
        put("norm_b", n, a["norm_b_2"][0, n * P:(n + 1) * P])
    freq = (1.0 / 10000.0 ** (np.arange(0, ROPE, 2) / ROPE)).astype(np.float32)
    put("inv_freq", 0, np.tile(freq, 4), 64)
    put("phase", 0, np.full(32, np.pi / 2, np.float32), 64)
    put("turn", 0, np.full(32, 0.25, np.float32), 64)
    put("sign", 0, np.ones(P, np.float32))
    put("sign", 0, -np.ones(16, np.float32), 96)
    put("eps", 0, np.full(P, EPS, np.float32))
    return out


def _squares():
    rows, columns = np.indices((P, P))
    rope_sum = ((columns >= 64) & (rows >= 64) & (rows % 32 == columns % 32)).astype(np.float32)
    ahead = np.where(columns > rows, np.float32(-1e30), np.float32(0))
    made = {"ident": rows == columns, "ones": np.ones((P, P)), "upto": rows <= columns,
            "rope_sum": rope_sum, "ahead": ahead}
    return np.stack([made[n].astype(np.float32) for n in SQUARES], axis=1)


def _aug_rows():
    t = np.arange(S, dtype=np.float32)
    one = np.ones(S, np.float32)
    return np.stack([np.stack([t, one]), np.stack([-8 * one, 8 * t])])


def kernel(**inputs):
    import concourse.bacc as bacc
    from concourse.bass_utils import run_bass_kernel_spmd

    a = {k: np.asarray(x) for k, x in inputs.items()}
    arrays = {
        "weights": _weights(a),
        "x": a["x"].reshape(S, D),
        "positions": a["positions"].reshape(1, S),
        "vectors": _vectors(a),
        "squares": _squares(),
        "aug_rows": _aug_rows(),
        "lambda_qk": a["lambda_qk_2"].reshape(1, 4 * 64),
    }
    arrays = {k: np.ascontiguousarray(x) for k, x in arrays.items()}
    nc = bacc.Bacc("TRN2", target_bir_lowering=False, num_devices=1)
    args = [nc.dram_tensor(k, x.shape, mybir.dt.from_np(x.dtype), kind="ExternalInput").ap()
            for k, x in arrays.items()]
    args.append(nc.dram_tensor("y", (S, D), F32, kind="ExternalOutput").ap())
    program(nc, *args)
    r = run_bass_kernel_spmd(nc, [arrays], core_ids=[0])
    return np.asarray(r.results[0]["y"]).reshape(1, S, D)
```

```python
from contextlib import ExitStack, contextmanager

import numpy as np

import concourse.bass as bass
from concourse import mybir

ALU = mybir.AluOpType
ACT = mybir.ActivationFunctionType
AX = mybir.AxisListType
F32 = mybir.dt.float32
F32R = mybir.dt.float32r
BF16 = mybir.dt.bfloat16
I32 = mybir.dt.int32

P = 128
S = 1024
D = 1024
KT = D // P
TT = S // P
HALF = 512
MLA_HEADS, QK_DIM, NOPE, ROPE = 8, 96, 64, 32
FFN = 2816
FT = FFN // P
SSD_HEADS = 4
DIFF_HEADS = 4
ML_HEADS = 4
EPS = 1e-6
LAM_INIT = 0.8 - 0.6 * float(np.exp(-0.3 * 0))

STAGE_UNITS = [("in", 18), ("mla", MLA_HEADS), ("out", KT), ("ffn", 3 * FT),
               ("diff", 4 * DIFF_HEADS), ("gates", 1), ("mlstm", 5 * ML_HEADS),
               ("merge", 3 * KT), ("out2", KT)]
FFN_PAIRS = FT // 2
STAGE_GROUPS = [("x", TT), ("in", 18), ("krot", 1), ("cols", 1), ("ssd", 2 * 11), ("mla", 11 * MLA_HEADS),
                ("out", KT), ("ffn_first", 4), ("ffn", 12 * (FFN_PAIRS - 1)), ("ffn_last", 8),
                ("diff", 5), ("gates", 2), ("mlstm", 17 * ML_HEADS),
                ("merge", 4 * KT), ("out2", KT), ("y", TT)]


def starts(stages):
    at, out = 0, {}
    for name, n in stages:
        out[name] = at
        at += n
    return out, at


UNIT0, UNITS = starts(STAGE_UNITS)
GROUP0, GROUPS = starts(STAGE_GROUPS)

NORMS = [("mix_pre", 8), ("ssd", 2), ("q", 2), ("kv", 1), ("mix_post", 1), ("ffn_pre", 8),
         ("ffn_post", 1), ("pre2", 8), ("post2", 1)]
POST_NORMS = ["mix_post", "ffn_post", "post2"]
NORM_TILES0, _ = starts(NORMS)
NORM_INDEX = {name: i for i, (name, _) in enumerate(NORMS)}
SPLITS = [("mix_pre", 8), ("q", 2), ("kv", 1), ("mix", 8), ("ffn_pre", 8), ("pre2", 8), ("y", 8),
          ("merged", 8)]
SPLIT0, _ = starts(SPLITS)

VECTORS = [("norm_mix_pre", 8), ("norm_mix_post", 8), ("norm_ffn_pre", 8), ("norm_ffn_post", 8),
           ("norm_pre_2", 8), ("norm_post_2", 8), ("mla_q_norm", 2), ("mla_kv_norm", 1),
           ("ssd_norm", 2), ("sc_conv", 2 * 3), ("ssd_conv", 6 * 5), ("dt_bias", 1), ("a_log", 1),
           ("ssd_d", 2), ("ffn_conv", FT * 2 * 4), ("gate_bias", 1), ("ml_conv", ML_HEADS * 2 * 4),
           ("norm_a", 4), ("norm_b", 4), ("inv_freq", 1), ("phase", 1), ("turn", 1), ("sign", 1),
           ("eps", 1)]
VEC0, NVEC = starts(VECTORS)
SQUARES = ["ident", "ones", "upto", "rope_sum", "ahead"]


def program(nc, wts, x_in, pos, vec_in, sq_in, aug_in, lam_in, y_out):
    spill = nc.dram_tensor("x_spill", (P, KT * S), F32).ap()
    with ExitStack() as ctx:
        KB = 1024
        base = nc.sbuf_base
        base += (-base) % 64

        def at(name, kb, shape, dt=F32):
            return nc.alloc_sbuf_tensor_at(name, shape, dt, offset=base + int(kb * KB))

        def sem(name):
            return ctx.enter_context(nc.semaphore(name))

        X = at("X", 0, [P, KT, S])
        RAW = at("RAW", 32, [P, KT, S])
        HH = at("HH", 64, [P, KT, S], F32R)
        HL = at("HL", 96, [P, KT, S], F32R)
        WR = at("WR", 128, [P, 2, KT * P])
        WH = at("WH", 136, [P, 2, KT * P], F32R)
        WL = at("WL", 144, [P, 2, KT * P], F32R)
        SQ = at("SQ", 152, [P, 2, S])
        RS = at("RS", 160, [P, S])
        T = at("T", 164, [P, 2, S])
        vec = at("vec", 204, [P, NVEC])
        cols = at("cols", 204 + 1.25, [P, 16])
        sqf = at("sqf", 204 + 1.3125, [P, 4, P])
        identb = at("identb", 204 + 3.3125, [P, P], BF16)
        aheadb = at("aheadb", 204 + 3.5625, [P, P], BF16)
        zero = at("zero", 204 + 3.8125, [P, 1])
        assert NVEC * 4 <= 1.25 * KB
        ident, ones, upto, rope_sum = (sqf[:, n, :] for n in range(4))
        aheadf = at("aheadf", 152, [P, P])
        ZS = at("ZS", 172, [P, 2, S])
        XBC = at("XBC", 180, [P, 6, S])
        DR = at("DR", 64, [P, S])
        selA = at("selA", 70.5, [P, P])
        DTC = at("DTC", 71, [P, TT, SSD_HEADS])
        NAC = at("NAC", 71.125, [P, TT, SSD_HEADS])
        XD = at("XD", 72, [P, TT, 2, P])
        AB = at("AB", 80, [P, 2, S])
        DD = at("DD", 88, [P, 2, S])
        PP = at("PP", 96, [P, 2, S])
        YS = at("YS", 104, [P, 2, S])
        TAB = at("TAB", 112, [P, S])
        ANG = at("ANG", 116, [P, S])
        KK = at("KK", 120, [P, S])
        KR = at("KR", 124, [P, S])
        POSI = at("POSI", 32 + 28, [P, S], I32)
        ROWS = at("ROWS", 152, [4, 5, S])
        QNH = at("QNH", 64, [P, 2, S], F32R)
        QNL = at("QNL", 72, [P, 2, S], F32R)
        KNH = at("KNH", 80, [P, 1, S], F32R)
        KNL = at("KNL", 84, [P, 1, S], F32R)
        QOP = at("QOP", 88, [P, 2, S])
        KOP = at("KOP", 96, [P, 2, S])
        VP = at("VP", 104, [P, 2, TT, P])
        KV = at("KV", 116, [P, 2, S])
        PR = at("PR", 152, [P, 2, S])
        PTB = at("PTB", 172, [P, 2, TT, HALF])
        GH = at("GH", 172, [P, 2, S], F32R)
        GL = at("GL", 180, [P, 2, S], F32R)
        VG = at("VG", 188, [P, S])
        VU = at("VU", 192, [P, S])
        SG = at("SG", 196, [P, S])
        PRD = at("PRD", 200, [P, S])
        DQ = at("DQ", 0, [P, 2, S])
        DK = at("DK", 8, [P, 2, S])
        DVT = at("DVT", 16, [P, S])
        DV = at("DV", 20, [P, TT, P])
        NQ = at("NQ", 164, [P, S])
        NK = at("NK", 168, [P, S])
        DO = at("DO", 28, [P, S])
        DP = at("DP", 172, [P, 2, 2, S])
        DPT = at("DPT", 188, [P, TT, HALF])
        GR = at("GR", 0, [P, S])
        GROWS = at("GROWS", 172, [4, 7, S])
        ACOL = at("ACOL", 4, [P, TT, ML_HEADS])
        selM = at("selM", 5, [P, 2, P])
        MQ = at("MQ", 8, [P, S])
        MK = at("MK", 12, [P, S])
        MVT = at("MVT", 16, [P, S])
        MV = at("MV", 20, [P, TT, P])
        MO = at("MO", 24, [P, S])
        MZ = at("MZ", 28, [P, S])
        MC = at("MC", 172, [P, S])
        MN = at("MN", 176, [P, S])
        ME = at("ME", 180, [P, S])
        MD = at("MD", 184, [P, 2, S])
        MP = at("MP", 192, [P, 2, S])
        MH = at("MH", 200, [P, S])
        lam_sb = at("lam_sb", 172, [P, 4 * 64])
        YH = at("YH", 0, [P, KT, S], F32R)
        YL = at("YL", 172, [P, KT, S], F32R)
        MS = at("MS", 160, [P, S])
        MS2 = at("MS2", 164, [P, S])
        MA = at("MA", 168, [P, S])
        OUT2 = at("OUT2", 172, [P, KT, S])
        OUTB = at("OUTB", 64, [P, 4, S])

        PG = ctx.enter_context(nc.psum_tensor("PG", [P, 2, S], F32))
        PT = ctx.enter_context(nc.psum_tensor("PT", [P, 2, HALF], F32))
        PO = ctx.enter_context(nc.psum_tensor("PO", [P, 2, HALF], F32))
        POf = PO[:, :, :].rearrange("p a n -> p (a n)")
        PTf = PT[:, :, :].rearrange("p a n -> p (a n)")

        w_loaded = [sem("w_loaded0"), sem("w_loaded1")]
        w_hi = sem("w_hi")
        w_split = sem("w_split")
        w_used = sem("w_used")
        zero_set = sem("zero_set")
        g_ready = sem("g_ready")
        g_free = [sem("g_free0"), sem("g_free1")]
        dve_step = sem("dve_step")
        act_step = sem("act_step")
        const_in = sem("const_in")
        x_loaded = [sem(f"x_loaded{i}") for i in range(TT)]
        consts_ready = sem("consts_ready")
        x_act, x_dve = sem("x_act"), sem("x_dve")
        n_sq, n_sq_used = sem("n_sq"), sem("n_sq_used")
        n_sum, n_root = sem("n_sum"), sem("n_root")
        sq_new, sq_sum = sem("sq_new"), sem("sq_sum")
        s_raw, s_hi, s_lo = sem("s_raw"), sem("s_hi"), sem("s_lo")
        n_done = sem("n_done")
        in_act, in_dve = sem("in_act"), sem("in_dve")
        xbc_ready = sem("xbc_ready")
        rows_act, rows_dve = sem("rows_act"), sem("rows_dve")
        pos_in, tab_r, tab_sin = sem("pos_in"), sem("tab_r"), sem("tab_sin")
        tab_done = sem("tab_done")
        ssd_rows, sel_set = sem("ssd_rows"), sem("sel_set")
        ab_ready, dd_ready, e_ready = sem("ab_ready"), sem("dd_ready"), sem("e_ready")
        pp_ready, pv_used, ssd_x = sem("pp_ready"), sem("pv_used"), sem("ssd_x")
        ssd_acc, ssd_y = sem("ssd_acc"), sem("ssd_y")
        krot_t, krot_done, vp_zero = sem("krot_t"), sem("krot_done"), sem("vp_zero")
        q_op, k_op, v_op, kv_cp = sem("q_op"), sem("k_op"), sem("v_op"), sem("kv_cp")
        m_neg, m_exp, m_prob = sem("m_neg"), sem("m_exp"), sem("m_prob")
        t_ready = sem("t_ready")
        t_free = sem("t_free")
        pv_half, att_free = sem("pv_half"), sem("att_free")
        out_act, out_dve = sem("out_act"), sem("out_dve")
        acc_zero = sem("acc_zero")
        f_act, f_silu, f_prod, f_hi, f_lo, f_down = (sem(n) for n in (
            "f_act", "f_silu", "f_prod", "f_hi", "f_lo", "f_down"))
        spilled, aug_set, aug_k, lam_loaded, lam_prod, lam_exp, lam_ready = (sem(n) for n in (
            "spilled", "aug_set", "aug_k", "lam_loaded", "lam_prod", "lam_exp", "lam_ready"))
        d_q, d_k, d_v, d_z, d_vop = (sem(n) for n in ("d_q", "d_k", "d_v", "d_z", "d_vop"))
        d_scores, d_neg, d_exp, d_prob, d_tready, d_tfree, d_half = (sem(n) for n in (
            "d_scores", "d_neg", "d_exp", "d_prob", "d_tready", "d_tfree", "d_half"))
        hb_ready = sem("hb_ready")
        hb_free = [sem("hb_free0"), sem("hb_free1")]
        d_o, d_sq, d_root, d_y = (sem(n) for n in ("d_o", "d_sq", "d_root", "d_y"))
        aug_loaded = sem("aug_loaded")
        gate_rows, gates_ready = sem("gate_rows"), sem("gates_ready")
        a_cols, m_sel = sem("a_cols"), sem("m_sel")
        m_conv, m_taps, m_q, m_v, m_o, m_z, m_vop = (sem(n) for n in (
            "m_conv", "m_taps", "m_q", "m_v", "m_o", "m_z", "m_vop"))
        m_mn, m_me, m_dd, m_e, m_pp, m_used, m_acc, m_abs, m_h, m_sq, m_root, m_y = (
            sem(n) for n in ("m_mn", "m_me", "m_dd", "m_e", "m_pp", "m_used", "m_acc", "m_abs",
                             "m_h", "m_sq", "m_root", "m_y"))
        g_sig, g_prod, g_done = sem("g_sig"), sem("g_prod"), sem("g_done")
        o2_act, o2_dve, x_back = sem("o2_act"), sem("o2_dve"), sem("x_back")
        y_act, y_dve = sem("y_act"), sem("y_dve")
        y_stored = [sem(f"y_stored{i}") for i in range(4)]

        PRIMED = {"pe": [pv_half, d_half, m_used],
                  "act": [att_free, d_o, d_exp],
                  "dve": [hb_free[0], hb_free[1], sq_sum, m_y, d_y, m_pp, g_done, d_prob, m_prob]}

        def primed(eng, semaphore, value):
            eng.wait_ge(semaphore, value + 1)

        def v(name, k=0):
            return vec[:, VEC0[name] + k:VEC0[name] + k + 1]

        class Groups:

            def __init__(self, stage, i=0, stride=0, first=0):
                self.base, self.i, self.stride = GROUP0[stage] + first, i, stride
                assert stride % 2 == 0

            def slot(self, k):
                return (self.base + k) % 2

            def psum(self, k):
                return PG[:, self.slot(k), :]

            def before(self, pe, k):
                n = (self.base + k) // 2
                if n or not isinstance(self.i, int):
                    pe.wait_ge(g_free[self.slot(k)], self.i * (self.stride // 2) + n)

            def ready(self, eng, k):
                eng.wait_ge(g_ready, self.i * self.stride + (self.base + k + 1))

            def free(self, k):
                return g_free[self.slot(k)]

            def wait_free(self, eng, k):
                eng.wait_ge(g_free[self.slot(k)],
                            self.i * (self.stride // 2) + ((self.base + k) // 2 + 1))

        class Steps:

            def __init__(self, eng, semaphore):
                self.eng, self.sem, self.n, self.off = eng, semaphore, 0, 0

            def __call__(self, ins):
                ins.then_inc(self.sem, 1)
                self.n += 1
                self.eng.wait_ge(self.sem, self.off + self.n)

            @contextmanager
            def loop(self, start, end, per):
                n0 = self.n
                with self.eng.Fori(start, end) as i:
                    self.off = i * per - start * per
                    yield i
                assert self.n - n0 == per, (self.n - n0, per)
                self.off, self.n = 0, n0 + per * (end - start)

        def unit_slot(stage, k):
            return (UNIT0[stage] + k) % 2

        NDONE0 = {"ssd": 0, "mix_post": 2, "ffn_post": 2 + KT, "post2": 2 + 2 * KT}
        NDONE = {"ssd": 2, "mix_post": 2 + KT, "ffn_post": 2 + 2 * KT, "post2": 2 + 4 * KT}

        def mla_bank(t, hh, q):
            return 2 * t + hh if t < 4 else 8 + 4 * (t - 4) + 2 * hh + q

        def half_bank(m):
            return PG[:, 1, (m % 2) * HALF:(m % 2 + 1) * HALF]

        def halves(m):
            return slice((m % 2) * HALF, (m % 2 + 1) * HALF)

        block = ctx.enter_context(nc.Block())

        @block.sync
        def _(sp):
            sp.dma_start(vec[:, :], vec_in).then_inc(const_in, 16)
            sp.dma_start(sqf[:, :, :], sq_in[:, 0:4, :]).then_inc(const_in, 16)
            sp.dma_start(aheadf[:, :], sq_in[:, 4, :]).then_inc(const_in, 16)
            for t in range(TT):
                sp.dma_start(RAW[:, t, :], x_in[t * P:(t + 1) * P, :]).then_inc(x_loaded[t], 16)

            def load(u, s):
                sp.dma_start(WR[:, s, :], u).then_inc(w_loaded[s], 16)

            load(wts[0], 0)
            load(wts[1], 1)
            with sp.Fori(1, UNITS // 2) as i:
                for s in range(2):
                    sp.wait_ge(w_split, 2 * i + (s - 1))
                    load(wts[bass.ds(2 * i + s, 1)].rearrange("a p n -> p (a n)"), s)
            sp.wait_ge(w_split, UNITS - 2)
            load(wts[UNITS - 1], 0)

        @block.gpsimd
        def _(pool):
            pool.memset(zero[:, :], 0.0).then_inc(zero_set, 1)
            pool.wait_ge(zero_set, 1)

            def split(i, s, reused):
                pool.wait_ge(w_loaded[s], 16 * i + 16)
                if reused:
                    pool.wait_ge(w_used, 2 * i + s)
                pool.tensor_tensor(WH[:, s, :], WR[:, s, :], zero[:, :].to_broadcast([P, KT * P]),
                                   ALU.add).then_inc(w_hi, 1)
                pool.wait_ge(w_hi, 2 * i + (s + 1))
                pool.tensor_tensor(WL[:, s, :], WR[:, s, :], WH[:, s, :].bitcast(F32),
                                   ALU.subtract).then_inc(w_split, 1)

            split(0, 0, False)
            split(0, 1, False)
            with pool.Fori(1, UNITS // 2) as i:
                for s in range(2):
                    split(i, s, True)
            split(UNITS // 2, 0, True)

        @block.tensor
        def _(pe):
            for semaphore in PRIMED["pe"]:
                pe.sem_inc(semaphore, 1)

            def product(out, blocks, first=None):
                for h in range(2):
                    cut = slice(h * HALF, (h + 1) * HALF)
                    for n, (slot, b, hi, lo) in enumerate(blocks):
                        w = slice(b * P, (b + 1) * P)
                        last = n == len(blocks) - 1
                        m = pe.matmul(out[:, cut], WH[:, slot, w], hi[:, cut], start=n == 0, stop=False)
                        if first is not None and h == 0 and n == 0:
                            m.then_inc(first, 1)
                        pe.matmul(out[:, cut], WH[:, slot, w], lo[:, cut], start=False, stop=False)
                        m = pe.matmul(out[:, cut], WL[:, slot, w], hi[:, cut], start=False, stop=last)
                return m

            def unit(stage, k, i=0, stride=0):
                pe.wait_ge(w_split, i * stride + (UNIT0[stage] + k + 1))
                return unit_slot(stage, k)

            def projection(stage, g, k, u, hi, lo, i=0, stride=0):
                slot = unit(stage, u, i, stride)
                g.before(pe, k)
                product(g.psum(k), [(slot, b, hi[:, b, :], lo[:, b, :]) for b in range(KT)],
                        w_used).then_inc(g_ready, 1)

            def first_pair(stage, g, k, name, hi=HH, lo=HL):
                for b in range(KT):
                    pe.wait_ge(s_lo, SPLIT0[name] + b + 1)
                    w = slice(b * P, (b + 1) * P)
                    for n in range(2):
                        slot = unit(stage, n)
                        if b == 0:
                            g.before(pe, k + n)
                        for h in range(2):
                            cut = slice(h * HALF, (h + 1) * HALF)
                            out = g.psum(k + n)[:, cut]
                            m = pe.matmul(out, WH[:, slot, w], hi[:, b, cut], start=b == 0, stop=False)
                            if b == 0 and n == 0 and h == 0:
                                m.then_inc(w_used, 1)
                            m = pe.matmul(out, WH[:, slot, w], lo[:, b, cut], start=False, stop=False)
                            if b == KT - 1 and n == 1 and h == 1:
                                m.then_inc(w_used, 1)
                            m = pe.matmul(out, WL[:, slot, w], hi[:, b, cut], start=False,
                                          stop=b == KT - 1)
                        if b == KT - 1:
                            m.then_inc(g_ready, 1)

            def norm(name):
                tiles, t0, n = dict(NORMS)[name], NORM_TILES0[name], NORM_INDEX[name]
                for k in range(tiles):
                    pe.wait_ge(n_sq, t0 + k + 1)
                    for h in range(2):
                        m = pe.matmul(PO[:, h, :], ones, SQ[:, k % 2, h * HALF:(h + 1) * HALF],
                                      start=k == 0, stop=k == tiles - 1)
                        if h == 1:
                            m.then_inc(n_sq_used, 1)

            def wait_split(name):
                pe.wait_ge(s_lo, SPLIT0[name] + dict(SPLITS)[name])

            def turn(out, src, g=None, k=None):
                for t in range(TT):
                    m = pe.transpose(out[:, t * P:(t + 1) * P], src[:, t * P:(t + 1) * P], ident)
                return m

            pe.wait_ge(consts_ready, 1)
            g = Groups("x")
            for t in range(TT):
                pe.wait_ge(x_loaded[t], 16)
                g.before(pe, t)
                turn(g.psum(t), RAW[:, t, :]).then_inc(g_ready, 1)
            norm("mix_pre")

            first_pair("in", Groups("in"), 0, "mix_pre")
            with pe.Fori(1, 9) as i:
                g = Groups("in", i, 2)
                for k in range(2):
                    projection("in", g, k, k, HH, HL, i, 2)

            g = Groups("krot")
            pe.wait_ge(krot_t, 1)
            g.before(pe, 0)
            for h in range(2):
                m = pe.matmul(g.psum(0)[:, h * HALF:(h + 1) * HALF], rope_sum,
                              RAW[:, 3, h * HALF:(h + 1) * HALF], start=True, stop=True)
            m.then_inc(g_ready, 1)
            g = Groups("cols")
            pe.wait_ge(ssd_rows, 1)
            g.before(pe, 0)
            turn(g.psum(0), DR[:, :]).then_inc(g_ready, 1)

            pe.wait_ge(xbc_ready, 6)
            for grp in range(2):
                g = Groups("ssd", first=11 * grp)
                g.before(pe, 0)
                turn(g.psum(0), XBC[:, grp, :]).then_inc(g_ready, 1)
                for hh in range(2):
                    pe.wait_ge(sel_set, 2 * grp + hh + 1)
                    g.before(pe, 1 + hh)
                    for h in range(2):
                        m = pe.matmul(g.psum(1 + hh)[:, h * HALF:(h + 1) * HALF], selA[:, :],
                                      DR[:, h * HALF:(h + 1) * HALF], start=True, stop=True)
                    m.then_inc(g_ready, 1)

                def scores(j):
                    g.before(pe, 3 + j)
                    for h in range(j // 4, 2):
                        a = max(h * HALF, j * P)
                        m = pe.matmul(g.psum(3 + j)[:, a:(h + 1) * HALF],
                                      XBC[:, 2 + grp, j * P:(j + 1) * P],
                                      XBC[:, 4 + grp, a:(h + 1) * HALF], start=True, stop=True)
                    m.then_inc(g_ready, 1)

                def values(j):
                    for hh in range(2):
                        pe.wait_ge(pp_ready, 16 * grp + 2 * j + hh + 1)
                        for h in range(j // 4, 2):
                            a = max(h * HALF, j * P)
                            m = pe.matmul(PO[:, h, a - h * HALF:HALF], XD[:, j, hh, :],
                                          PP[:, hh, a:(h + 1) * HALF],
                                          start=j == 0 and hh == 0,
                                          stop=hh == 1 and j == 4 * h + 3)
                        m.then_inc(pv_used, 1)

                pe.wait_ge(ssd_x, grp + 1)
                if grp:
                    pe.wait_ge(ssd_acc, grp)
                for j in range(TT):
                    scores(j)
                    if j:
                        values(j - 1)
                values(TT - 1)
            pe.wait_ge(ssd_acc, 2)
            norm("ssd")
            norm("q")
            norm("kv")

            wait_split("kv")
            pe.wait_ge(krot_done, 2)
            with pe.Fori(0, MLA_HEADS // 2) as i:
                g = Groups("mla", i, 22)
                for hh in range(2):
                    slot = unit("mla", hh, i, 2)
                    g.before(pe, 2 * hh)
                    product(g.psum(2 * hh), [(slot, b, QNH[:, b, :], QNL[:, b, :]) for b in range(2)],
                            w_used).then_inc(g_ready, 1)
                    g.before(pe, 2 * hh + 1)
                    product(g.psum(2 * hh + 1), [(slot, 2, KNH[:, 0, :], KNL[:, 0, :])])\
                        .then_inc(g_ready, 1)
                for hh in range(2):
                    pe.wait_ge(kv_cp, 2 * i + (hh + 1))
                    g.before(pe, 4 + hh)
                    turn(g.psum(4 + hh), KV[:, hh, :]).then_inc(g_ready, 1)

                def scores(t, hh):
                    n = 6 + 2 * t + hh
                    g.before(pe, n)
                    for h in range(t // 4 + 1):
                        end = min((h + 1) * HALF, (t + 1) * P)
                        pe.matmul(g.psum(n)[:, h * HALF:end], QOP[:, hh, t * P:(t + 1) * P],
                                  KOP[:, hh, h * HALF:end], start=True, stop=end != (t + 1) * P)
                    pe.matmul(g.psum(n)[:, t * P:(t + 1) * P], identb[:, :], aheadb[:, :],
                              start=False, stop=True).then_inc(g_ready, 1)

                def transposes(t, hh):
                    primed(pe, m_prob, i * (2 * TT) + (2 * t + hh + 1))
                    for q in range(t // 4 + 1):
                        n = mla_bank(t, hh, q)
                        if n >= 2:
                            pe.wait_ge(t_free, i * 24 + (n - 1))
                        for b in range(4 * q, min(4 * q + 4, t + 1)):
                            m = pe.transpose(PT[:, n % 2, (b - 4 * q) * P:(b - 4 * q + 1) * P],
                                             PR[:, hh, b * P:(b + 1) * P], ident)
                        m.then_inc(t_ready, 1)

                def values(h, hh):
                    pe.wait_ge(t_free, i * 24 + (8 if h == 0 else 24) - (1 - hh) * (1 if h == 0 else 2))
                    if h == 0 and hh == 0:
                        primed(pe, att_free, i)
                    for j in range(4 * h + 4):
                        a = max(0, j * P - h * HALF)
                        m = pe.matmul(PO[:, h, a:HALF], VP[:, hh, j, :], PTB[:, hh, j, a:HALF],
                                      start=hh == 0 and j == 0, stop=hh == 1 and j == 4 * h + 3)
                    m.then_inc(pv_half, 1)

                for hh in range(2):
                    pe.wait_ge(q_op, 2 * i + (hh + 1))
                    pe.wait_ge(k_op, 2 * i + (hh + 1))
                    scores(0, hh)
                for t in range(TT):
                    for hh in range(2):
                        transposes(t, hh)
                        if t + 1 < TT:
                            scores(t + 1, hh)
                    if t == 3 or t == 7:
                        for hh in range(2):
                            pe.wait_ge(v_op, 2 * i + (hh + 1))
                            values(t // 4, hh)

            first_pair("out", Groups("out"), 0, "mix")
            with pe.Fori(1, KT // 2) as i:
                g = Groups("out", i, 2)
                for k in range(2):
                    projection("out", g, k, k, HH, HL, i, 2)
            norm("mix_post")
            norm("ffn_pre")

            DOWN = 8

            def gate_up(g, k, u, i=0, stride=0):
                for n in range(2):
                    projection("ffn", g, k + n, u + n, HH, HL, i, stride)

            def down(g, k, u, pair, i=0, stride=0):
                pe.wait_ge(f_lo, 2 * pair + 2)
                for m in range(DOWN):
                    if m % 4 == 0:
                        slot = unit("ffn", u + m // 4, i, stride)
                    g.before(pe, k + m)
                    last = product(g.psum(k + m), [(slot, 2 * (m % 4) + b, GH[:, b, :], GL[:, b, :])
                                                   for b in range(2)], w_used if m % 4 == 0 else None)
                    last.then_inc(g_ready, 1)

            g = Groups("ffn_first")
            first_pair("ffn", g, 0, "ffn_pre")
            gate_up(g, 2, 2)
            with pe.Fori(0, FFN_PAIRS - 1) as i:
                g = Groups("ffn", i, 12)
                gate_up(g, 0, 4, i, 6)
                down(g, 2, 6, i, i, 6)
                gate_up(g, 10, 8, i, 6)
            g = Groups("ffn_last")
            down(g, 0, 4 + 6 * (FFN_PAIRS - 1), FFN_PAIRS - 1)
            norm("ffn_post")
            norm("pre2")

            g = Groups("diff")
            first_pair("diff", g, 0, "pre2")
            projection("diff", g, 2, 2, HH, HL)
            projection("diff", g, 3, 3, HH, HL)
            pe.wait_ge(d_v, 1)
            g.before(pe, 4)
            turn(g.psum(4), DVT[:, :]).then_inc(g_ready, 1)
            for k in (3, 4):
                g.wait_free(pe, k)

            def diff_head(i, more):
                def bank(m):
                    primed(pe, hb_free[m % 2], 6 * i + m // 2)
                    return half_bank(m)

                def fill(n):
                    u, h, part = n // 4, (n // 2) % 2, n % 2
                    slot = unit("diff", 4 + u, i, 4)
                    out = bank(n // 2) if part == 0 else half_bank(n // 2)
                    cut = slice(h * HALF, (h + 1) * HALF)
                    for b in range(part * KT // 2, (part + 1) * KT // 2):
                        w = slice(b * P, (b + 1) * P)
                        m = pe.matmul(out, WH[:, slot, w], HH[:, b, cut], start=b == 0, stop=False)
                        if b == 0 and h == 0:
                            m.then_inc(w_used, 1)
                        pe.matmul(out, WH[:, slot, w], HL[:, b, cut], start=False, stop=False)
                        m = pe.matmul(out, WL[:, slot, w], HH[:, b, cut], start=False,
                                      stop=b == KT - 1)
                    if part == 1:
                        m.then_inc(hb_ready, 1)

                def scores(t, c):
                    primed(pe, d_exp, i * (2 * TT) + (2 * t + c))
                    for h in range(t // 4 + 1):
                        end = min((h + 1) * HALF, (t + 1) * P)
                        pe.matmul(PG[:, 0, h * HALF:end], DQ[:, c, t * P:(t + 1) * P],
                                  DK[:, c, h * HALF:end], start=True, stop=end != (t + 1) * P)
                    pe.matmul(PG[:, 0, t * P:(t + 1) * P], identb[:, :], aheadb[:, :],
                              start=False, stop=True).then_inc(d_scores, 1)

                def transposes(t):
                    primed(pe, d_prob, i * TT + (t + 1))
                    for q in range(t // 4 + 1):
                        n = t if t < 4 else 4 + 2 * (t - 4) + q
                        if n >= 2:
                            pe.wait_ge(d_tfree, i * 12 + (n - 1))
                        for b in range(4 * q, min(4 * q + 4, t + 1)):
                            m = pe.transpose(PT[:, n % 2, (b - 4 * q) * P:(b - 4 * q + 1) * P],
                                             DP[:, t % 2, 0, b * P:(b + 1) * P], ident)
                        m.then_inc(d_tready, 1)

                def values(h):
                    pe.wait_ge(d_tfree, i * 12 + (4 if h == 0 else 12))
                    if h == 0:
                        pe.wait_ge(d_vop, i + 1)
                        primed(pe, d_o, i)
                    for j in range(4 * h + 4):
                        a = max(0, j * P - h * HALF)
                        m = pe.matmul(PO[:, h, a:HALF], DV[:, j, :], DPT[:, j, a:HALF],
                                      start=j == 0, stop=j == 4 * h + 3)
                    m.then_inc(d_half, 1)

                pe.wait_ge(d_q, i + 1)
                pe.wait_ge(d_k, i + 1)
                for t in range(TT):
                    for c in range(2):
                        scores(t, c)
                        if more and 2 * t + c < 13:
                            fill(2 * t + c)
                        if t == 5 and c == 0:
                            values(0)
                    if t:
                        transposes(t - 1)
                if more:
                    fill(13)
                    fill(14)
                transposes(TT - 1)
                if more:
                    fill(15)
                    pe.wait_ge(d_v, i + 2)
                    for m in (8, 9):
                        out = bank(m)
                        for b in range(4):
                            t = 4 * (m % 2) + b
                            ins = pe.transpose(out[:, b * P:(b + 1) * P], DVT[:, t * P:(t + 1) * P],
                                               ident)
                        ins.then_inc(hb_ready, 1)
                values(1)
                pe.wait_ge(d_sq, i + 1)
                for m in (10, 11) if more else (0, 1):
                    pe.matmul(bank(m), ones, SQ[:, 0, halves(m)], start=True, stop=True)\
                      .then_inc(hb_ready, 1)

            with pe.Fori(0, DIFF_HEADS - 1) as i:
                diff_head(i, True)
            diff_head(DIFF_HEADS - 1, False)
            primed(pe, d_exp, DIFF_HEADS * 2 * TT)
            for b in hb_free:
                primed(pe, b, 6 * (DIFF_HEADS - 1) + 1)

            g = Groups("gates")
            projection("gates", g, 0, 0, HH, HL)
            pe.wait_ge(gate_rows, 1)
            g.before(pe, 1)
            turn(g.psum(1), GR[:, :]).then_inc(g_ready, 1)
            with pe.Fori(0, ML_HEADS // 2) as i:
                g = Groups("mlstm", i, 34)
                for hh in range(2):
                    o, head = 17 * hh, 2 * i + hh
                    for k in range(5):
                        projection("mlstm", g, o + k, 5 * hh + k, HH, HL, i, 10)
                    pe.wait_ge(m_v, head + 1)
                    g.before(pe, o + 5)
                    turn(g.psum(o + 5), MVT[:, :]).then_inc(g_ready, 1)
                    pe.wait_ge(m_sel, head + 1)
                    for n in range(2):
                        g.before(pe, o + 6 + n)
                        for h in range(2):
                            m = pe.matmul(g.psum(o + 6 + n)[:, h * HALF:(h + 1) * HALF],
                                          selM[:, n, :], GR[:, h * HALF:(h + 1) * HALF],
                                          start=True, stop=True)
                        m.then_inc(g_ready, 1)
                    pe.wait_ge(m_q, 2 * head + 2)
                    pe.wait_ge(m_vop, head + 1)

                    def scores(j):
                        g.before(pe, o + 8 + j)
                        for h in range(j // 4, 2):
                            a = max(h * HALF, j * P)
                            m = pe.matmul(g.psum(o + 8 + j)[:, a:(h + 1) * HALF],
                                          MK[:, j * P:(j + 1) * P], MQ[:, a:(h + 1) * HALF],
                                          start=True, stop=True)
                        m.then_inc(g_ready, 1)

                    def values(j):
                        primed(pe, m_pp, 8 * head + j + 1)
                        for lhs, acc in ((MV[:, j, :], PO), (ones, PT)):
                            for h in range(j // 4, 2):
                                a = max(h * HALF, j * P)
                                m = pe.matmul(acc[:, h, a - h * HALF:HALF], lhs,
                                              MP[:, j % 2, a:(h + 1) * HALF],
                                              start=j == 0, stop=j == 4 * h + 3)
                        m.then_inc(m_used, 1)

                    primed(pe, m_y, head)
                    for j in range(TT):
                        scores(j)
                        if j:
                            values(j - 1)
                    values(TT - 1)
                    pe.wait_ge(m_sq, head + 1)
                    g.before(pe, o + 16)
                    for h in range(2):
                        m = pe.matmul(g.psum(o + 16)[:, h * HALF:(h + 1) * HALF], ones,
                                      SQ[:, 0, h * HALF:(h + 1) * HALF], start=True, stop=True)
                    m.then_inc(g_ready, 1)

            with pe.Fori(0, KT // 2) as i:
                g = Groups("merge", i, 8)
                for n in range(2):
                    for k in range(2):
                        projection("merge", g, 4 * n + k, 3 * n + k, HH, HL, i, 6)
                    slot = unit("merge", 3 * n + 2, i, 6)
                    wait_split("y")
                    for k in range(2):
                        g.before(pe, 4 * n + 2 + k)
                        product(g.psum(4 * n + 2 + k),
                                [(slot, 4 * k + b, YH[:, 4 * k + b, :], YL[:, 4 * k + b, :])
                                 for b in range(4)], w_used if k == 0 else None).then_inc(g_ready, 1)
            first_pair("out2", Groups("out2"), 0, "merged")
            with pe.Fori(1, KT // 2) as i:
                g = Groups("out2", i, 2)
                for k in range(2):
                    projection("out2", g, k, k, HH, HL, i, 2)
            norm("post2")
            g = Groups("y")
            for t in range(TT):
                pe.wait_ge(n_done, NDONE["post2"] - (KT if t < TT // 2 else 0))
                g.before(pe, t)
                for k in range(KT):
                    m = pe.transpose(g.psum(t)[:, k * P:(k + 1) * P], X[:, k, t * P:(t + 1) * P], ident)
                m.then_inc(g_ready, 1)

        @block.scalar
        def _(act):
            for semaphore in PRIMED["act"]:
                act.sem_inc(semaphore, 1)

            step = Steps(act, act_step)

            def square(src, k):
                act.activation(T[:, k % 2, :], src, ACT.Square).then_inc(sq_new, 1)

            def root(name, width):
                act.wait_ge(n_sq_used, NORM_TILES0[name] + dict(NORMS)[name])
                act.activation(RS[:, :], POf, ACT.Sqrt, bias=v("eps"), scale=1.0 / width)\
                   .then_inc(n_root, 1)

            def norm(name, src, width, after=None):
                tiles, t0, n = dict(NORMS)[name], NORM_TILES0[name], NORM_INDEX[name]
                for k in range(tiles):
                    if after is not None:
                        act.wait_ge(n_done, NDONE0[after] + k + 1)
                    if t0 + k >= 2:
                        act.wait_ge(n_sq_used, t0 + k - 1)
                    act.activation(SQ[:, k % 2, :], src(k), ACT.Square).then_inc(n_sq, 1)
                root(name, width)

            def out_tiles(stage, post, dst):
                with act.Fori(0, KT // 2) as i:
                    g = Groups(stage, i, 2)
                    for k in range(2):
                        g.ready(act, k)
                        primed(act, sq_sum, 2 * i + KT * POST_NORMS.index(post))
                        act.activation(dst[:, bass.ds(2 * i + k, 1), :], g.psum(k), ACT.Copy)
                        m = act.activation(T[:, k, :], g.psum(k), ACT.Square)
                        m.then_inc(sq_new, 1)
                        act.wait_ge(sq_new, 2 * i + (KT * POST_NORMS.index(post) + k + 1))
                        act.sem_inc(g.free(k), 1)

            def split(name, hi):
                t0 = SPLIT0[name]
                for k in range(dict(SPLITS)[name]):
                    act.wait_ge(s_raw, t0 + k + 1)
                    raw = RAW[:, k, :] if name in ("mix", "y", "merged") else T[:, (t0 + k) % 2, :]
                    act.activation(hi[:, k, :], raw, ACT.Copy).then_inc(s_hi, 1)

            act.wait_ge(consts_ready, 1)
            g = Groups("x")
            for t in range(0, TT, 2):
                g.ready(act, t)
                act.activation(X[:, :, t * P:(t + 1) * P], g.psum(t).rearrange("p (k n) -> p k n", k=KT),
                               ACT.Copy).then_inc(g.free(t), 1)
            g.wait_free(act, TT - 2)
            g.wait_free(act, TT - 1)
            act.dma_start(POSI[:, :], pos.to_broadcast([P, S])).then_inc(pos_in, 16)
            norm("mix_pre", lambda k: X[:, k, :], D)
            split("mix_pre", HH)

            g = Groups("in")
            for k in range(4):
                g.ready(act, k)
                act.activation(RAW[:, k, :], g.psum(k), ACT.Copy).then_inc(g.free(k), 1)
            for j in range(2):
                k = 4 + 3 * j
                g.ready(act, k)
                if j:
                    act.wait_ge(in_dve, 3)
                else:
                    act.wait_ge(s_lo, 8)
                act.activation(T[:, 0, :], g.psum(k), ACT.Copy).then_inc(g.free(k), 1)
                g.wait_free(act, k + 1)
                act.activation(SQ[:, 0, :], T[:, 1, :], ACT.Copy, scale=v("sc_conv", 3 * j + 2))\
                   .then_inc(in_act, 1)
            for j in range(2):
                g.ready(act, 10 + j)
                act.activation(ZS[:, j, :], g.psum(10 + j), ACT.Silu).then_inc(g.free(10 + j), 1)
            for j in range(6):
                k = 12 + j
                g.ready(act, k)
                act.activation(XBC[:, j, :], g.psum(k), ACT.Identity, bias=v("ssd_conv", 5 * j + 4),
                               scale=v("ssd_conv", 5 * j + 3)).then_inc(in_act, 1)
                g.wait_free(act, k)
                act.activation(XBC[:, j, :], XBC[:, j, :], ACT.Silu).then_inc(xbc_ready, 1)

            def log1p_rows(base, rows, n_dve):
                act.wait_ge(rows_dve, n_dve + 1)
                act.activation(rows[:, 1, :], rows[:, 1, :], ACT.Exp, scale=-1.0).then_inc(rows_act, 1)
                act.wait_ge(rows_dve, n_dve + 2)
                act.activation(rows[:, 3, :], rows[:, 2, :], ACT.Ln).then_inc(rows_act, 1)

            act.activation(cols[0:4, 0:1], vec[0:4, VEC0["a_log"]:VEC0["a_log"] + 1], ACT.Exp)\
               .then_inc(rows_act, 1)
            log1p_rows(0, ROWS, 0)
            act.wait_ge(tab_r, 1)
            act.activation(TAB[:, :], KK[:, :], ACT.Sin).then_inc(tab_sin, 1)
            g = Groups("krot")
            g.ready(act, 0)
            act.activation(KR[64:128, :], g.psum(0)[64:128, :], ACT.Copy)\
               .then_inc(g.free(0), 1)

            for grp in range(2):
                g = Groups("ssd", first=11 * grp)
                for hh in range(2):
                    g.ready(act, 1 + hh)
                    if grp:
                        act.wait_ge(dd_ready, 16 * grp)
                    act.activation(AB[:, hh, :], g.psum(1 + hh), ACT.Copy).then_inc(g.free(1 + hh), 1)
                for j in range(TT):
                    for hh in range(2):
                        n = 16 * grp + 2 * j + hh
                        act.wait_ge(dd_ready, n + 1)
                        act.activation(DD[:, hh, j * P:], DD[:, hh, j * P:], ACT.Exp).then_inc(e_ready, 1)
            act.wait_ge(ssd_y, 2)
            norm("ssd", lambda k: YS[:, k, :], 256)
            act.wait_ge(n_done, NDONE["ssd"])
            norm("q", lambda k: RAW[:, k, :], 256)
            split("q", QNH)
            norm("kv", lambda k: RAW[:, 2, :], 128)
            split("kv", KNH)

            act.wait_ge(krot_done, 1)
            for hh in range(2):
                m = act.activation(KOP[64:128, hh, :], KR[64:128, :], ACT.Copy)
            m.then_inc(krot_done, 1)
            with act.Fori(0, MLA_HEADS // 2) as i:
                g = Groups("mla", i, 22)
                for hh in range(2):
                    g.ready(act, 2 * hh + 1)
                    act.activation(KV[:, hh, :], g.psum(2 * hh + 1), ACT.Copy).then_inc(kv_cp, 1)
                    act.activation(KOP[0:64, hh, :], g.psum(2 * hh + 1)[0:64, :], ACT.Copy)\
                       .then_inc(k_op, 1)
                    act.wait_ge(k_op, 2 * i + (hh + 1))
                    act.sem_inc(g.free(2 * hh + 1), 1)

                def exp(t, hh):
                    act.wait_ge(m_neg, i * (2 * TT) + (2 * t + hh + 1))
                    act.activation(PR[:, hh, 0:(t + 1) * P], g.psum(6 + 2 * t + hh)[:, 0:(t + 1) * P],
                                   ACT.Exp, bias=cols[:, 2 + hh:3 + hh], scale=float(QK_DIM) ** -0.5,
                                   accum_out=cols[:, 4 + hh:5 + hh]).then_inc(m_exp, 1)
                    act.wait_ge(m_exp, i * (2 * TT) + (2 * t + hh + 1))
                    act.sem_inc(g.free(6 + 2 * t + hh), 1)

                def evacuate_pair(t, hh):
                    for q in range(t // 4 + 1):
                        n = mla_bank(t, hh, q)
                        act.wait_ge(t_ready, i * 24 + (n + 1))
                        if t % 4 == 0 and q == 0:
                            primed(act, pv_half, i * 4 + (1 + hh if t else 0))
                        m = min(4, t + 1 - 4 * q)
                        act.activation(PTB[:, hh, 4 * q:4 * q + m, (t % 4) * P:(t % 4 + 1) * P],
                                       PT[:, n % 2, 0:m * P].rearrange("p (b n) -> p b n", b=m),
                                       ACT.Copy).then_inc(t_free, 1)

                exp(0, 0)
                exp(0, 1)
                for t in range(TT):
                    evacuate_pair(t, 0)
                    evacuate_pair(t, 1)
                    if t + 1 < TT:
                        exp(t + 1, 0)
                        exp(t + 1, 1)
                primed(act, pv_half, 4 * i + 4)
                act.activation(RAW[:, bass.ds(i, 1), :], POf, ACT.Copy).then_inc(att_free, 1)

            split("mix", HH)
            out_tiles("out", "mix_post", RAW)
            root("mix_post", D)
            norm("ffn_pre", lambda k: X[:, k, :], D, "mix_post")
            split("ffn_pre", HH)

            def ffn_vec(part, tap, j, x):
                c = VEC0["ffn_conv"] + 8 * x + 4 * part + tap
                if isinstance(j, int):
                    return vec[:, c + 16 * j:c + 16 * j + 1]
                return vec[:, bass.ds(16 * j + c, 1)]

            def tile(g, k, pair, x):
                tile_no = 2 * pair + x
                for part, buf in ((0, VG), (1, VU)):
                    g.ready(act, k + part)
                    if not (isinstance(tile_no, int) and tile_no == 0):
                        act.wait_ge(f_prod, tile_no)
                    act.activation(buf[:, :], g.psum(k + part), ACT.Identity,
                                   bias=ffn_vec(part, 3, pair, x),
                                   scale=ffn_vec(part, 2, pair, x)).then_inc(f_act, 1)
                    if part == 0:
                        g.wait_free(act, k)
                        act.activation(SG[:, :], VG[:, :], ACT.Silu).then_inc(f_silu, 1)

            def hi(pair, x, downs):
                tile_no = 2 * pair + x
                act.wait_ge(f_prod, tile_no + 1)
                if downs is not None:
                    downs()
                act.activation(GH[:, x, :], PRD[:, :], ACT.Copy).then_inc(f_hi, 1)

            g = Groups("ffn_first")
            tile(g, 0, 0, 0)
            hi(0, 0, None)
            tile(g, 2, 0, 1)
            hi(0, 1, None)
            with act.Fori(1, FFN_PAIRS) as i:
                g = Groups("ffn", i, 12, first=-12)
                tile(g, 0, i, 0)
                hi(i, 0, lambda: g.ready(act, 9))
                tile(g, 10, i, 1)
                hi(i, 1, None)
            g = Groups("ffn_last")
            for k in range(KT):
                g.wait_free(act, k)
                primed(act, sq_sum, KT + max(k - 1, 0))
                square(RAW[:, k, :], k)
            act.dma_start(lam_sb[:, :], lam_in.to_broadcast([P, 4 * 64])).then_inc(lam_loaded, 16)
            root("ffn_post", D)
            norm("pre2", lambda k: X[:, k, :], D, "ffn_post")
            act.dma_start(spill, X[:, :, :].rearrange("p k n -> p (k n)")).then_inc(spilled, 16)
            split("pre2", HH)

            act.wait_ge(lam_loaded, 16)
            act.wait_ge(lam_prod, 1)
            act.activation(cols[:, 8:10], cols[:, 8:10], ACT.Exp).then_inc(lam_exp, 1)
            act.wait_ge(spilled, 16)
            act.wait_ge(aug_k, 1)
            for rows, c in ((slice(64, 66), 0), (slice(0, 2), 1)):
                act.dma_start(DQ[rows, c, :], aug_in[0]).then_inc(aug_loaded, 16)
                act.dma_start(DK[rows, c, :], aug_in[1]).then_inc(aug_loaded, 16)
            act.wait_ge(aug_set, 1)
            g = Groups("diff")
            g.ready(act, 1)
            act.activation(DK[0:64, 0, :], g.psum(1)[0:64, :], ACT.Copy)
            act.activation(DK[64:128, 1, :], g.psum(1)[64:128, :], ACT.Copy).then_inc(d_k, 1)
            act.wait_ge(d_k, 1)
            act.sem_inc(g.free(1), 1)
            g.ready(act, 2)
            act.activation(DVT[:, :], g.psum(2), ACT.Copy).then_inc(d_v, 1)
            act.wait_ge(d_v, 1)
            act.sem_inc(g.free(2), 1)
            g.ready(act, 3)
            act.activation(RAW[:, 4, :], g.psum(3), ACT.Silu).then_inc(g.free(3), 1)

            def diff_head(i, more):
                def half_ready(m):
                    act.wait_ge(hb_ready, i * 12 + (m + 1))

                def exp(t, c):
                    act.wait_ge(d_neg, i * (2 * TT) + (2 * t + c + 1))
                    act.activation(DP[:, t % 2, c, 0:(t + 1) * P], PG[:, 0, 0:(t + 1) * P], ACT.Exp,
                                   bias=cols[:, 4 + 2 * (t % 2) + c:5 + 2 * (t % 2) + c], scale=0.125,
                                   accum_out=cols[:, 10 + 2 * (t % 2) + c:11 + 2 * (t % 2) + c])\
                       .then_inc(d_exp, 1)

                def transposed(t):
                    for q in range(t // 4 + 1):
                        n = t if t < 4 else 4 + 2 * (t - 4) + q
                        act.wait_ge(d_tready, i * 12 + (n + 1))
                        if t == 4 and q == 0:
                            primed(act, d_half, i * 2 + 1)
                        if t == 0:
                            primed(act, d_half, i * 2)
                        m = min(4, t + 1 - 4 * q)
                        act.activation(DPT[:, 4 * q:4 * q + m, (t % 4) * P:(t % 4 + 1) * P],
                                       PT[:, n % 2, 0:m * P].rearrange("p (b n) -> p b n", b=m),
                                       ACT.Copy).then_inc(d_tfree, 1)

                def next_half(m):
                    half_ready(m)
                    cut, src = halves(m), half_bank(m)
                    if m < 4:
                        act.activation(NK[:, cut], src, ACT.Copy).then_inc(hb_free[m % 2], 1)
                    elif m < 6:
                        act.activation(DVT[:, cut], src, ACT.Copy).then_inc(hb_free[m % 2], 1)
                    else:
                        act.activation(RAW[:, bass.ds(i + 5, 1), cut], src, ACT.Silu)\
                           .then_inc(hb_free[m % 2], 1)
                    if m == 5:
                        for b in range(2):
                            primed(act, hb_free[b], 6 * i + 3)
                        act.sem_inc(d_v, 1)

                for t in range(TT):
                    exp(t, 0)
                    exp(t, 1)
                    if more and 2 <= t < 6:
                        next_half(t)
                    if t:
                        transposed(t - 1)
                if more:
                    act.wait_ge(d_scores, i * (2 * TT) + 2 * TT)
                    act.activation(DK[0:64, 0, :], NK[0:64, :], ACT.Copy)
                    act.activation(DK[64:128, 1, :], NK[64:128, :], ACT.Copy).then_inc(d_k, 1)
                    next_half(6)
                transposed(TT - 1)
                if more:
                    next_half(7)
                primed(act, d_half, 2 * i + 2)
                act.activation(SQ[:, 0, :], POf, ACT.Square).then_inc(d_sq, 1)
                act.wait_ge(d_sq, i + 1)
                primed(act, d_y, i)
                act.activation(DO[:, :], POf, ACT.Copy).then_inc(d_o, 1)
                for m in (10, 11) if more else (0, 1):
                    half_ready(m)
                    act.activation(RS[:, halves(m)], half_bank(m), ACT.Sqrt, bias=v("eps"),
                                   scale=1.0 / P).then_inc(d_root, 1)
                    act.wait_ge(d_root, i * 2 + (m % 2 + 1))
                    act.sem_inc(hb_free[m % 2], 1)

            with act.Fori(0, DIFF_HEADS - 1) as i:
                diff_head(i, True)
            diff_head(DIFF_HEADS - 1, False)

            g = Groups("gates")
            g.ready(act, 0)
            primed(act, d_y, DIFF_HEADS)
            gb = VEC0["gate_bias"]
            act.activation(GROWS[:, 5, :], g.psum(0)[0:4, :], ACT.Identity, bias=vec[0:4, gb:gb + 1])
            act.activation(GROWS[:, 0, :], g.psum(0)[32:36, :], ACT.Identity,
                           bias=vec[32:36, gb:gb + 1]).then_inc(g.free(0), 1)
            log1p_rows(1, GROWS, 2)
            with act.Fori(0, ML_HEADS // 2) as i:
                g = Groups("mlstm", i, 34)
                for hh in range(2):
                    o, head = 17 * hh, 2 * i + hh
                    primed(act, m_y, head)
                    for n, buf in ((0, MQ), (1, MK)):
                        g.ready(act, o + n)
                        c = VEC0["ml_conv"] + 4 * n + 8 * hh + 3
                        act.activation(MC[:, :], g.psum(o + n), ACT.Copy,
                                       scale=vec[:, bass.ds(16 * i + c, 1)]).then_inc(m_conv, 1)
                        g.wait_free(act, o + n)
                        act.activation(buf[:, :], MC[:, :], ACT.Silu).then_inc(m_q, 1)
                        act.wait_ge(m_q, 2 * head + (n + 1))
                    g.ready(act, o + 2)
                    act.activation(MVT[:, :], g.psum(o + 2), ACT.Copy).then_inc(m_v, 1)
                    act.wait_ge(m_v, head + 1)
                    act.sem_inc(g.free(o + 2), 1)
                    g.ready(act, o + 3)
                    act.activation(MO[:, :], g.psum(o + 3), ACT.Sigmoid).then_inc(g.free(o + 3), 1)
                    g.ready(act, o + 4)
                    act.activation(MZ[:, :], g.psum(o + 4), ACT.Silu).then_inc(g.free(o + 4), 1)
                    g.ready(act, o + 6)
                    act.activation(MN[:, :], g.psum(o + 6), ACT.Copy).then_inc(m_mn, 1)
                    act.wait_ge(m_mn, head + 1)
                    act.sem_inc(g.free(o + 6), 1)
                    g.ready(act, o + 7)
                    act.activation(ME[:, :], g.psum(o + 7), ACT.Exp).then_inc(m_me, 1)
                    act.wait_ge(m_me, head + 1)
                    act.sem_inc(g.free(o + 7), 1)
                    for j in range(TT):
                        act.wait_ge(m_dd, head * TT + (j + 1))
                        act.activation(MD[:, j % 2, j * P:], MD[:, j % 2, j * P:], ACT.Exp)\
                           .then_inc(m_e, 1)
                    primed(act, m_used, head * TT + TT)
                    act.activation(MC[:, :], PTf, ACT.Abs).then_inc(m_abs, 1)
                    act.wait_ge(m_h, head + 1)
                    act.activation(SQ[:, 0, :], MH[:, :], ACT.Square).then_inc(m_sq, 1)
                    g.ready(act, o + 16)
                    act.activation(RS[:, :], g.psum(o + 16), ACT.Sqrt, bias=v("eps"),
                                   scale=1.0 / P).then_inc(m_root, 1)
                    act.wait_ge(m_root, head + 1)
                    act.sem_inc(g.free(o + 16), 1)

            split("y", YH)
            with act.Fori(0, KT // 2) as i:
                g = Groups("merge", i, 8)
                for n in range(2):
                    tile_no = 2 * i + n
                    primed(act, g_done, tile_no)
                    g.ready(act, 4 * n)
                    act.activation(MS[:, :], g.psum(4 * n), ACT.Sigmoid).then_inc(g.free(4 * n), 1)
                    g.ready(act, 4 * n + 1)
                    act.activation(MS2[:, :], g.psum(4 * n + 1), ACT.Sigmoid)\
                       .then_inc(g.free(4 * n + 1), 1)
            split("merged", HH)
            out_tiles("out2", "post2", OUT2)
            act.wait_ge(spilled, 16)
            act.wait_ge(g_ready, GROUP0["out2"])
            act.dma_start(X[:, :, :].rearrange("p k n -> p (k n)"), spill).then_inc(x_back, 16)
            root("post2", D)
            g = Groups("y")
            for t in range(TT):
                if t % 2 == 0 or t < TT // 2:
                    g.ready(act, t)
                    if t >= 4:
                        act.wait_ge(y_stored[t % 4], 16)
                    act.activation(OUTB[:, t % 4, :], g.psum(t), ACT.Copy).then_inc(g.free(t), 1)
                g.wait_free(act, t)
                act.dma_start(y_out[t * P:(t + 1) * P, :], OUTB[:, t % 4, :]).then_inc(y_stored[t % 4], 16)
            for n in range(4):
                act.wait_ge(y_stored[n], 32)

        @block.vector
        def _(dve):
            for semaphore in PRIMED["dve"]:
                dve.sem_inc(semaphore, 1)

            step = Steps(dve, dve_step)

            def reciprocal_root(name):
                dve.wait_ge(n_root, NORM_INDEX[name] + 1)
                step(dve.reciprocal(RS[:, :], RS[:, :]))

            def norm_split(name, vname, src, lo):
                reciprocal_root(name)
                split(name, lambda k, out: dve.scalar_tensor_tensor(
                    out, src(k), v(vname, k), RS[:, :], ALU.mult, ALU.mult), lo)

            def split(name, make, lo):
                t0, n = SPLIT0[name], dict(SPLITS)[name]

                def low(k):
                    dve.wait_ge(s_hi, t0 + k + 1)
                    raw = RAW[:, k, :] if make is None else T[:, (t0 + k) % 2, :]
                    dve.tensor_tensor(lo[:, k, :], raw, HI[name][:, k, :].bitcast(F32),
                                      ALU.subtract).then_inc(s_lo, 1)

                if make is None:
                    for k in range(n):
                        dve.sem_inc(s_raw, 1)
                    for k in range(n):
                        low(k)
                    return
                for k in range(n):
                    if t0 + k >= 2:
                        dve.wait_ge(s_lo, t0 + k - 1)
                    make(k, T[:, (t0 + k) % 2, :]).then_inc(s_raw, 1)
                    if k:
                        low(k - 1)
                low(n - 1)

            HI = {"mix_pre": HH, "q": QNH, "kv": KNH, "mix": HH, "ffn_pre": HH, "pre2": HH,
                  "y": YH, "merged": HH}

            def norm_residual(name, vname, src, parts=1):
                reciprocal_root(name)
                for n in range(parts):
                    cut = slice(n * S // parts, (n + 1) * S // parts)
                    for k in range(KT):
                        done = NDONE0[name] + n * KT + k
                        if n * KT + k >= 2:
                            dve.wait_ge(n_done, done - 1)
                        step(dve.scalar_tensor_tensor(T[:, k % 2, cut], src(k)[:, cut], v(vname, k),
                                                      RS[:, cut], ALU.mult, ALU.mult))
                        dve.tensor_tensor(X[:, k, cut], X[:, k, cut], T[:, k % 2, cut], ALU.add)\
                           .then_inc(n_done, 1)
                dve.wait_ge(n_done, NDONE[name])

            def zero_sum():
                step(dve.memset(SQ[:, 0, :], 0.0))

            def add_square(n, k):
                dve.wait_ge(sq_new, n + 1)
                primed(dve, sq_sum, n)
                dve.tensor_tensor(SQ[:, 0, :], SQ[:, 0, :], T[:, k, :], ALU.add).then_inc(sq_sum, 1)

            def end_sum(post):
                primed(dve, sq_sum, KT * (POST_NORMS.index(post) + 1))
                dve.sem_inc(n_sq, 1)

            def sum_squares(post):
                zero_sum()
                with dve.Fori(0, KT // 2) as i:
                    for k in range(2):
                        add_square(2 * i + (KT * POST_NORMS.index(post) + k), k)
                end_sum(post)

            def taps(g, k, out, weights, then):
                for d, w in enumerate(weights, 1):
                    ins = dve.scalar_tensor_tensor(out[:, d:], g.psum(k)[:, 0:S - d], w, out[:, d:],
                                                   ALU.mult, ALU.add)
                    if d < len(weights):
                        step(ins)
                    else:
                        ins.then_inc(g.free(k), 1)

            dve.wait_ge(const_in, 48)
            step(dve.tensor_copy(identb[:, :], ident))
            dve.tensor_copy(aheadb[:, :], aheadf[:, :]).then_inc(consts_ready, 1)
            dve.wait_ge(consts_ready, 1)

            g = Groups("x")
            for t in range(1, TT, 2):
                g.ready(dve, t)
                dve.tensor_copy(X[:, :, t * P:(t + 1) * P],
                                g.psum(t).rearrange("p (k n) -> p k n", k=KT)).then_inc(g.free(t), 1)
            g.wait_free(dve, TT - 2)
            g.wait_free(dve, TT - 1)
            norm_split("mix_pre", "norm_mix_pre", lambda k: X[:, k, :], HL)

            g = Groups("in")
            for j in range(2):
                k = 4 + 3 * j
                g.wait_free(dve, k)
                g.ready(dve, k + 1)
                dve.tensor_tensor(T[:, 1, :], g.psum(k + 1), T[:, 0, :], ALU.mult)\
                   .then_inc(g.free(k + 1), 1)
                dve.wait_ge(in_act, 1 if j == 0 else 2)
                g.wait_free(dve, k + 1)
                for d in (1, 2):
                    if d == 2:
                        dve.wait_ge(in_dve, 3 * j + 1)
                    dve.scalar_tensor_tensor(SQ[:, 0, d:], T[:, 1, 0:S - d], v("sc_conv", 3 * j + 2 - d),
                                             SQ[:, 0, d:], ALU.mult, ALU.add).then_inc(in_dve, 1)
                dve.wait_ge(in_dve, 3 * j + 2)
                g.ready(dve, k + 2)
                dve.tensor_tensor(RAW[:, 4 + j, :], g.psum(k + 2), SQ[:, 0, :], ALU.mult)\
                   .then_inc(g.free(k + 2), 1)
                g.wait_free(dve, k + 2)
                dve.sem_inc(in_dve, 1)
            for j in range(6):
                k = 12 + j
                dve.wait_ge(in_act, 2 + j + 1)
                g.ready(dve, k)
                taps(g, k, XBC[:, j, :], [v("ssd_conv", 5 * j + 3 - d) for d in (1, 2, 3)], None)

            def softplus(rows, raw, bias, n_act):
                x0, y, u, l, s = (rows[:, n, :] for n in range(5))
                if raw is not None:
                    step(dve.tensor_scalar(x0, raw, bias, None, ALU.add))
                dve.scalar_tensor_tensor(y, x0, -1.0, x0, ALU.mult, ALU.max).then_inc(rows_dve, 1)
                dve.wait_ge(rows_act, n_act + 1)
                dve.tensor_scalar(u, y, 1.0, None, ALU.add).then_inc(rows_dve, 1)
                step(dve.tensor_scalar(s, y, -0.25, 1.0 / 3.0, ALU.mult, ALU.add))
                step(dve.tensor_tensor(s, s, y, ALU.mult))
                step(dve.tensor_scalar(s, s, -0.5, None, ALU.add))
                step(dve.tensor_tensor(s, s, y, ALU.mult))
                step(dve.tensor_scalar(s, s, 1.0, None, ALU.add))
                step(dve.tensor_tensor(s, s, y, ALU.mult))
                dve.wait_ge(rows_act, n_act + 2)
                step(dve.tensor_tensor(s, s, l, ALU.subtract))
                step(dve.tensor_scalar(u, y, 1.0 / 64, None, ALU.is_lt))
                step(dve.tensor_tensor(s, s, u, ALU.mult))
                step(dve.tensor_tensor(l, l, s, ALU.add))
                step(dve.scalar_tensor_tensor(x0, x0, 0.0, l, ALU.max, ALU.add))

            g.wait_free(dve, 3)
            g.wait_free(dve, 17)
            g.ready(dve, 17)
            step(dve.memset(DR[:, :], 0.0))
            db = VEC0["dt_bias"]
            softplus(ROWS, RAW[0:4, 3, :], vec[0:4, db:db + 1], 1)
            step(dve.tensor_copy(DR[0:4, :], ROWS[:, 0, :]))
            dve.wait_ge(rows_act, 1)
            step(dve.tensor_scalar(ROWS[:, 1, :], ROWS[:, 0, :], cols[0:4, 0:1], -1.0, ALU.mult, ALU.mult))
            step(dve.memset(ROWS[:, 2, :], 1.0))
            dve.tensor_tensor_scan(DR[32:36, :], ROWS[:, 2, :], ROWS[:, 1, :], 0.0, ALU.mult, ALU.add)\
               .then_inc(ssd_rows, 1)

            dve.wait_ge(pos_in, 16)
            step(dve.tensor_copy(KK[:, :], POSI[:, :]))
            step(dve.tensor_scalar(ANG[:, :], KK[:, :], v("inv_freq"), None, ALU.mult))
            step(dve.tensor_scalar(KK[:, :], ANG[:, :], 1.0 / (2 * np.pi), v("turn"), ALU.mult, ALU.add))
            step(dve.tensor_scalar(KK[:, :], KK[:, :], 12582912.0, None, ALU.add))
            step(dve.tensor_scalar(KK[:, :], KK[:, :], 12582912.0, None, ALU.subtract))
            c1, c2 = 6.25, 0.033203125
            for c in (c1, c2, 2 * np.pi - c1 - c2):
                step(dve.scalar_tensor_tensor(ANG[:, :], KK[:, :], -float(c), ANG[:, :],
                                              ALU.mult, ALU.add))
            step(dve.tensor_scalar(KK[:, :], ANG[:, :], v("phase"), None, ALU.add))
            dve.tensor_scalar(KK[:, :], KK[:, :], 3.1415925, -3.1415925, ALU.min, ALU.max)\
               .then_inc(tab_r, 1)
            dve.wait_ge(tab_sin, 1)
            step(dve.tensor_scalar(TAB[:, :], TAB[:, :], v("sign"), None, ALU.mult))
            step(dve.memset(TAB[0:64, :], 1.0))
            dve.tensor_tensor(RAW[:, 3, :], RAW[:, 3, :], TAB[:, :], ALU.mult).then_inc(krot_t, 1)

            g = Groups("cols")
            g.ready(dve, 0)
            turned = g.psum(0).rearrange("p (t n) -> p t n", t=TT)
            step(dve.tensor_copy(DTC[:, :, :], turned[:, :, 0:4]))
            dve.tensor_scalar(NAC[:, :, :], turned[:, :, 32:36], -1.0, None, ALU.mult)\
               .then_inc(g.free(0), 1)
            g.wait_free(dve, 0)

            dve.wait_ge(xbc_ready, 6)
            step(dve.memset(XD[:, :, :, :].rearrange("p a b c -> p (a b c)"), 0.0))
            for grp in range(2):
                g = Groups("ssd", first=11 * grp)
                g.ready(dve, 0)
                if grp:
                    dve.wait_ge(pv_used, 16)
                xt = g.psum(0).rearrange("p (t n) -> p t n", t=TT)
                for hh in range(2):
                    c = 2 * grp + hh
                    ins = dve.tensor_tensor(XD[:, :, hh, hh * 64:(hh + 1) * 64],
                                            xt[:, :, hh * 64:(hh + 1) * 64],
                                            DTC[:, :, c:c + 1].to_broadcast([P, TT, 64]), ALU.mult)
                    if hh == 0:
                        step(ins)
                    else:
                        ins.then_inc(ssd_x, 1)
                dve.wait_ge(ssd_x, grp + 1)
                dve.sem_inc(g.free(0), 1)
                for hh in range(2):
                    c = 2 * grp + hh
                    if c:
                        prev = Groups("ssd", first=11 * ((c - 1) // 2))
                        prev.ready(dve, 1 + (c - 1) % 2)
                    dve.tensor_copy(selA[:, :], ident[:, 32 + c:33 + c].to_broadcast([P, P]))\
                       .then_inc(sel_set, 1)

                def exponents(j):
                    for hh in range(2):
                        n = 16 * grp + 2 * j + hh
                        c = 2 * grp + hh
                        if j == 0:
                            g.wait_free(dve, 1 + hh)
                        if n >= 2:
                            dve.wait_ge(pp_ready, n - 1)
                        dve.tensor_scalar(DD[:, hh, j * P:], AB[:, hh, j * P:],
                                          NAC[:, j, c:c + 1], 0.0, ALU.add, ALU.min)\
                           .then_inc(dd_ready, 1)

                def decayed(j):
                    g.ready(dve, 3 + j)
                    for hh in range(2):
                        n = 16 * grp + 2 * j + hh
                        dve.wait_ge(e_ready, n + 1)
                        if n >= 2:
                            dve.wait_ge(pv_used, n - 1)
                        step(dve.tensor_tensor(DD[:, hh, j * P:(j + 1) * P],
                                               DD[:, hh, j * P:(j + 1) * P], upto, ALU.mult))
                        dve.tensor_tensor(PP[:, hh, j * P:], g.psum(3 + j)[:, j * P:],
                                          DD[:, hh, j * P:], ALU.mult).then_inc(pp_ready, 1)
                    dve.wait_ge(pp_ready, 16 * grp + 2 * j + 2)
                    dve.sem_inc(g.free(3 + j), 1)

                for j in range(TT):
                    exponents(j)
                    decayed(j)
                dve.wait_ge(pv_used, 16 * grp + 16)
                dve.scalar_tensor_tensor(YS[:, grp, :], XBC[:, grp, :], v("ssd_d", grp), POf,
                                         ALU.mult, ALU.add).then_inc(ssd_acc, 1)
                dve.wait_ge(ssd_acc, grp + 1)
                dve.tensor_tensor(YS[:, grp, :], YS[:, grp, :], ZS[:, grp, :], ALU.mult)\
                   .then_inc(ssd_y, 1)
            reciprocal_root("ssd")
            for k in range(2):
                dve.scalar_tensor_tensor(RAW[:, 6 + k, :], YS[:, k, :], v("ssd_norm", k), RS[:, :],
                                         ALU.mult, ALU.mult).then_inc(n_done, 1)
            dve.wait_ge(n_done, NDONE["ssd"])
            norm_split("q", "mla_q_norm", lambda k: RAW[:, k, :], QNL)
            norm_split("kv", "mla_kv_norm", lambda k: RAW[:, 2, :], KNL)

            Groups("krot").wait_free(dve, 0)
            step(dve.memset(VP[:, :, :, :].rearrange("p a b c -> p (a b c)"), 0.0))
            dve.sem_inc(krot_done, 1)

            with step.loop(0, MLA_HEADS // 2, 2 * (TT + TT)) as i:
                g = Groups("mla", i, 22)
                for hh in range(2):
                    g.ready(dve, 2 * hh)
                    dve.tensor_tensor(QOP[:, hh, :], g.psum(2 * hh), TAB[:, :], ALU.mult)\
                       .then_inc(q_op, 1)
                    dve.wait_ge(q_op, 2 * i + (hh + 1))
                    dve.sem_inc(g.free(2 * hh), 1)
                for hh in range(2):
                    g.ready(dve, 4 + hh)
                    dve.tensor_copy(VP[:, hh, :, hh * 64:(hh + 1) * 64],
                                    g.psum(4 + hh).rearrange("p (t n) -> p t n", t=TT)[:, :, 64:128])\
                       .then_inc(v_op, 1)
                    dve.wait_ge(v_op, 2 * i + (hh + 1))
                    dve.sem_inc(g.free(4 + hh), 1)

                def maximum(t, hh):
                    g.ready(dve, 6 + 2 * t + hh)
                    step(dve.reduce_max(cols[:, hh:hh + 1],
                                        g.psum(6 + 2 * t + hh)[:, 0:(t + 1) * P], AX.X))
                    dve.tensor_scalar(cols[:, 2 + hh:3 + hh], cols[:, hh:hh + 1],
                                      -float(QK_DIM) ** -0.5, None, ALU.mult).then_inc(m_neg, 1)

                def normalise(t, hh):
                    n = (t + 1) * P
                    dve.wait_ge(m_exp, i * (2 * TT) + (2 * t + hh + 1))
                    step(dve.reciprocal(cols[:, 6 + hh:7 + hh], cols[:, 4 + hh:5 + hh]))
                    dve.tensor_scalar(PR[:, hh, 0:n], PR[:, hh, 0:n], cols[:, 6 + hh:7 + hh], None,
                                      ALU.mult).then_inc(m_prob, 1)

                for t in range(TT):
                    maximum(t, 0)
                    maximum(t, 1)
                    normalise(t, 0)
                    normalise(t, 1)
            primed(dve, att_free, MLA_HEADS // 2)
            split("mix", None, HL)
            sum_squares("mix_post")
            norm_residual("mix_post", "norm_mix_post", lambda k: RAW[:, k, :])
            step(dve.memset(RAW[:, :, :].rearrange("p k n -> p (k n)"), 0.0))
            norm_split("ffn_pre", "norm_ffn_pre", lambda k: X[:, k, :], HL)

            def ffn_vec(part, tap, j, x):
                c = VEC0["ffn_conv"] + 8 * x + 4 * part + tap
                if isinstance(j, int):
                    return vec[:, c + 16 * j:c + 16 * j + 1]
                return vec[:, bass.ds(16 * j + c, 1)]

            def tile(g, k, pair, x):
                tile_no = 2 * pair + x
                for part, buf in ((0, VG), (1, VU)):
                    dve.wait_ge(f_act, 2 * tile_no + (part + 1))
                    g.ready(dve, k + part)
                    taps(g, k + part, buf, [ffn_vec(part, 2 - d, pair, x) for d in (1, 2)], None)
                g.wait_free(dve, k + 1)
                dve.wait_ge(f_silu, tile_no + 1)
                if not (isinstance(tile_no, int) and tile_no == 0):
                    dve.wait_ge(f_lo, tile_no)
                dve.tensor_tensor(PRD[:, :], SG[:, :], VU[:, :], ALU.mult).then_inc(f_prod, 1)

            def low(pair, x):
                tile_no = 2 * pair + x
                dve.wait_ge(f_hi, tile_no + 1)
                dve.tensor_tensor(GL[:, x, :], PRD[:, :], GH[:, x, :].bitcast(F32),
                                  ALU.subtract).then_inc(f_lo, 1)

            def accumulate(g, k, after=lambda m: None):
                for m in range(KT):
                    g.ready(dve, k + m)
                    dve.tensor_tensor(RAW[:, m, :], RAW[:, m, :], g.psum(k + m), ALU.add)\
                       .then_inc(g.free(k + m), 1)
                    after(m)

            g = Groups("ffn_first")
            tile(g, 0, 0, 0)
            low(0, 0)
            tile(g, 2, 0, 1)
            low(0, 1)
            with step.loop(1, FFN_PAIRS, 4) as i:
                g = Groups("ffn", i, 12, first=-12)
                tile(g, 0, i, 0)
                accumulate(g, 2)
                g.wait_free(dve, 8)
                g.wait_free(dve, 9)
                low(i, 0)
                tile(g, 10, i, 1)
                low(i, 1)
            g = Groups("ffn_last")
            zero_sum()
            accumulate(g, 0, lambda m: add_square(KT + m - 1, (m - 1) % 2) if m else None)
            add_square(2 * KT - 1, 1)
            end_sum("ffn_post")
            g.wait_free(dve, 6)
            g.wait_free(dve, 7)
            norm_residual("ffn_post", "norm_ffn_post", lambda k: RAW[:, k, :])
            norm_split("pre2", "norm_pre_2", lambda k: X[:, k, :], HL)

            dve.wait_ge(lam_loaded, 16)
            lam4 = lam_sb[:, :].rearrange("p (a b n) -> p a b n", a=2, b=2)
            step(dve.tensor_tensor(lam4[:, :, 0, :], lam4[:, :, 0, :], lam4[:, :, 1, :], ALU.mult))
            dve.reduce_sum(cols[:, 8:10], lam4[:, :, 0, :], AX.X).then_inc(lam_prod, 1)
            dve.wait_ge(lam_exp, 1)
            step(dve.tensor_tensor(cols[:, 8:9], cols[:, 8:9], cols[:, 9:10], ALU.subtract))
            dve.tensor_scalar(cols[:, 14:15], cols[:, 8:9], LAM_INIT, -1.0, ALU.add, ALU.mult)\
               .then_inc(lam_ready, 1)
            dve.wait_ge(lam_ready, 1)
            dve.wait_ge(spilled, 16)
            step(dve.memset(DQ[:, :, :], 0.0))
            step(dve.memset(DK[:, :, :], 0.0))
            dve.sem_inc(aug_k, 1)
            dve.wait_ge(aug_loaded, 64)

            def slopes():
                step(dve.tensor_scalar(DK[64:66, 0, :], DK[64:66, 0, :], 0.25, None, ALU.mult))
                step(dve.tensor_scalar(DK[0:2, 1, :], DK[0:2, 1, :], 0.25, None, ALU.mult))

            slopes()
            dve.sem_inc(aug_set, 1)
            g = Groups("diff")
            g.ready(dve, 0)
            step(dve.tensor_copy(DQ[0:64, 0, :], g.psum(0)[0:64, :]))
            dve.tensor_copy(DQ[64:128, 1, :], g.psum(0)[64:128, :]).then_inc(d_q, 1)
            dve.wait_ge(d_q, 1)
            dve.sem_inc(g.free(0), 1)
            g.ready(dve, 4)
            dve.tensor_copy(DV[:, :, :], g.psum(4).rearrange("p (t n) -> p t n", t=TT))\
               .then_inc(d_vop, 1)
            dve.wait_ge(d_vop, 1)
            dve.sem_inc(g.free(4), 1)

            def diff_head(i, more):
                def maximum(t, c):
                    b = 4 + 2 * (t % 2) + c
                    dve.wait_ge(d_scores, i * (2 * TT) + (2 * t + c + 1))
                    step(dve.reduce_max(cols[:, c:c + 1], PG[:, 0, 0:(t + 1) * P], AX.X))
                    dve.tensor_scalar(cols[:, b:b + 1], cols[:, c:c + 1], -0.125, None, ALU.mult)\
                       .then_inc(d_neg, 1)

                def normalise(t):
                    b = 10 + 2 * (t % 2)
                    n = (t + 1) * P
                    primed(dve, d_exp, i * (2 * TT) + (2 * t + 2))
                    primed(dve, d_prob, i * TT + t)
                    step(dve.reciprocal(cols[:, 2:4], cols[:, b:b + 2]))
                    step(dve.tensor_tensor(cols[:, 3:4], cols[:, 3:4], cols[:, 14:15], ALU.mult))
                    step(dve.tensor_scalar(DP[:, t % 2, 0, 0:n], DP[:, t % 2, 0, 0:n],
                                           cols[:, 2:3], None, ALU.mult))
                    dve.scalar_tensor_tensor(DP[:, t % 2, 0, 0:n], DP[:, t % 2, 1, 0:n], cols[:, 3:4],
                                             DP[:, t % 2, 0, 0:n], ALU.mult, ALU.add)\
                       .then_inc(d_prob, 1)

                for t in range(TT):
                    maximum(t, 0)
                    if t:
                        normalise(t - 1)
                    maximum(t, 1)
                    if more and t < 2:
                        dve.wait_ge(hb_ready, i * 12 + (t + 1))
                        dve.tensor_copy(NQ[:, halves(t)], half_bank(t)).then_inc(hb_free[t], 1)
                normalise(TT - 1)
                if more:
                    dve.wait_ge(d_k, i + 2)
                    slopes()
                    for b in hb_free:
                        primed(dve, b, 6 * i + 1)
                    step(dve.tensor_copy(DQ[0:64, 0, :], NQ[0:64, :]))
                    dve.tensor_copy(DQ[64:128, 1, :], NQ[64:128, :]).then_inc(d_q, 1)
                    primed(dve, d_half, 2 * i + 2)
                    for m in (8, 9):
                        dve.wait_ge(hb_ready, i * 12 + (m + 1))
                        ins = dve.tensor_copy(DV[:, 4 * (m % 2):4 * (m % 2) + 4, :],
                                              half_bank(m).rearrange("p (t n) -> p t n", t=4))
                        ins.then_inc(hb_free[m % 2], 1)
                    for b in hb_free:
                        primed(dve, b, 6 * i + 5)
                    dve.sem_inc(d_vop, 1)
                dve.wait_ge(d_root, 2 * i + 2)
                primed(dve, d_o, i + 1)
                step(dve.reciprocal(RS[:, :], RS[:, :]))
                head = (lambda n: bass.ds(i + n, 1)) if more else (lambda n: slice(i + n, i + n + 1))
                step(dve.scalar_tensor_tensor(DO[:, :], DO[:, :], vec[:, head(VEC0["norm_a"])],
                                              RS[:, :], ALU.mult, ALU.mult))
                dve.scalar_tensor_tensor(RAW[:, head(0), :], DO[:, :], 1.0 - LAM_INIT,
                                         RAW[:, head(4), :], ALU.mult, ALU.mult).then_inc(d_y, 1)

            shared = 2 * TT + 3 * TT + 2
            with step.loop(0, DIFF_HEADS - 1, shared + 3) as i:
                diff_head(i, True)
            diff_head(DIFF_HEADS - 1, False)

            primed(dve, d_y, DIFF_HEADS)
            step(dve.memset(GR[:, :], 0.0))
            Groups("gates").wait_free(dve, 0)
            step(dve.tensor_scalar(GROWS[:, 0, :], GROWS[:, 0, :], -1.0, None, ALU.mult))
            softplus(GROWS, None, None, 3)
            step(dve.tensor_scalar(GROWS[:, 2, :], GROWS[:, 0, :], -1.0, None, ALU.mult))
            step(dve.memset(GROWS[:, 1, :], 1.0))
            step(dve.tensor_tensor_scan(GROWS[:, 3, :], GROWS[:, 1, :], GROWS[:, 2, :], 0.0,
                                        ALU.mult, ALU.add))
            step(dve.tensor_tensor(GROWS[:, 5, :], GROWS[:, 5, :], GROWS[:, 3, :], ALU.subtract))
            step(dve.tensor_tensor_scan(GROWS[:, 4, :], GROWS[:, 5, :], GROWS[:, 5, :], 0.0,
                                        ALU.max, ALU.max))
            step(dve.tensor_copy(GR[64:68, :], GROWS[:, 5, :]))
            step(dve.tensor_scalar(GR[0:4, :], GROWS[:, 4, :], -1.0, None, ALU.mult))
            step(dve.tensor_tensor(GROWS[:, 3, :], GROWS[:, 3, :], GROWS[:, 4, :], ALU.add))
            dve.tensor_scalar(GR[32:36, :], GROWS[:, 3, :], -1.0, None, ALU.mult).then_inc(gate_rows, 1)
            g = Groups("gates")
            g.ready(dve, 1)
            dve.tensor_copy(ACOL[:, :, :], g.psum(1).rearrange("p (t n) -> p t n", t=TT)[:, :, 64:68])\
               .then_inc(g.free(1), 1)
            g.wait_free(dve, 1)
            with step.loop(0, ML_HEADS // 2, 2 * (4 + 1 + TT + 5)) as i:
                g = Groups("mlstm", i, 34)
                for hh in range(2):
                    o, head = 17 * hh, 2 * i + hh
                    for n in range(2):
                        dve.wait_ge(m_conv, 2 * head + (n + 1))
                        c = VEC0["ml_conv"] + 4 * n + 8 * hh
                        taps(g, o + n, MC, [vec[:, bass.ds(16 * i + (c + 3 - d), 1)] for d in (1, 2, 3)],
                             None)
                    g.ready(dve, o + 5)
                    dve.tensor_copy(MV[:, :, :], g.psum(o + 5).rearrange("p (t n) -> p t n", t=TT))\
                       .then_inc(m_vop, 1)
                    dve.wait_ge(m_vop, head + 1)
                    dve.sem_inc(g.free(o + 5), 1)
                    step(dve.tensor_copy(selM[:, 0, :],
                                         ident[:, bass.ds(2 * i + hh, 1)].to_broadcast([P, P])))
                    dve.tensor_copy(selM[:, 1, :],
                                    ident[:, bass.ds(2 * i + (32 + hh), 1)].to_broadcast([P, P]))\
                       .then_inc(m_sel, 1)
                    def decayed(j):
                        g.ready(dve, o + 8 + j)
                        dve.wait_ge(m_e, head * TT + (j + 1))
                        primed(dve, m_used, head * TT + max(j - 1, 0))
                        step(dve.tensor_tensor(MD[:, j % 2, j * P:(j + 1) * P],
                                               MD[:, j % 2, j * P:(j + 1) * P], upto, ALU.mult))
                        dve.scalar_tensor_tensor(MP[:, j % 2, j * P:], g.psum(o + 8 + j)[:, j * P:],
                                                 float(P) ** -0.5, MD[:, j % 2, j * P:],
                                                 ALU.mult, ALU.mult).then_inc(m_pp, 1)
                        primed(dve, m_pp, head * TT + (j + 1))
                        dve.sem_inc(g.free(o + 8 + j), 1)

                    dve.wait_ge(m_mn, head + 1)
                    for j in range(TT):
                        acol = ACOL[:, j, bass.ds(2 * i + hh, 1)]
                        if j >= 2:
                            primed(dve, m_pp, head * TT + (j - 1))
                        else:
                            primed(dve, m_pp, head * TT)
                        dve.tensor_scalar(MD[:, j % 2, j * P:], MN[:, j * P:], acol, 0.0,
                                          ALU.add, ALU.min).then_inc(m_dd, 1)
                        if j:
                            decayed(j - 1)
                    decayed(TT - 1)
                    dve.wait_ge(m_abs, head + 1)
                    dve.wait_ge(m_me, head + 1)
                    step(dve.tensor_tensor(MC[:, :], MC[:, :], ME[:, :], ALU.max))
                    step(dve.reciprocal(MC[:, :], MC[:, :]))
                    step(dve.tensor_tensor(MH[:, :], POf, MC[:, :], ALU.mult))
                    g.wait_free(dve, o + 3)
                    dve.tensor_tensor(MH[:, :], MH[:, :], MO[:, :], ALU.mult).then_inc(m_h, 1)
                    dve.wait_ge(m_root, head + 1)
                    step(dve.reciprocal(RS[:, :], RS[:, :]))
                    dve.wait_ge(m_h, head + 1)
                    step(dve.scalar_tensor_tensor(MH[:, :], MH[:, :],
                                                  vec[:, bass.ds(2 * i + (hh + VEC0["norm_b"]), 1)],
                                                  RS[:, :], ALU.mult, ALU.mult))
                    g.wait_free(dve, o + 4)
                    dve.tensor_tensor(RAW[:, bass.ds(2 * i + (4 + hh), 1), :], MH[:, :], MZ[:, :],
                                      ALU.mult).then_inc(m_y, 1)

            primed(dve, m_y, ML_HEADS)
            split("y", None, YL)
            with step.loop(0, KT // 2, 2) as i:
                g = Groups("merge", i, 8)
                for n in range(2):
                    tile_no = 2 * i + n
                    g.wait_free(dve, 4 * n)
                    g.ready(dve, 4 * n + 2)
                    dve.tensor_tensor(MA[:, :], g.psum(4 * n + 2), MS[:, :], ALU.mult)\
                       .then_inc(g.free(4 * n + 2), 1)
                    g.wait_free(dve, 4 * n + 2)
                    g.wait_free(dve, 4 * n + 1)
                    g.ready(dve, 4 * n + 3)
                    step(dve.tensor_tensor(MS2[:, :], g.psum(4 * n + 3), MS2[:, :], ALU.mult))
                    dve.sem_inc(g.free(4 * n + 3), 1)
                    dve.tensor_tensor(RAW[:, bass.ds(2 * i + n, 1), :], MA[:, :], MS2[:, :], ALU.add)\
                       .then_inc(g_done, 1)
            primed(dve, g_done, KT)
            split("merged", None, HL)
            sum_squares("post2")
            dve.wait_ge(x_back, 16)
            norm_residual("post2", "norm_post_2", lambda k: OUT2[:, k, :], 2)
            g = Groups("y")
            for t in range(TT // 2 + 1, TT, 2):
                g.ready(dve, t)
                if t >= 4:
                    dve.wait_ge(y_stored[t % 4], 16)
                dve.tensor_copy(OUTB[:, t % 4, :], g.psum(t)).then_inc(g.free(t), 1)


_VECTORS_P = ("norm_mix_pre", "norm_mix_post", "norm_ffn_pre", "norm_ffn_post", "norm_pre_2",
              "norm_post_2", "mla_q_norm", "mla_kv_norm", "ssd_norm")


def _blocks(w, columns):
    out = np.zeros((len(columns), P, KT, P), w.dtype)
    for u, c in enumerate(columns):
        part = w[:, c].reshape(w.shape[0] // P, P, len(c))
        out[u, :, :part.shape[0], :len(c)] = part.transpose(1, 0, 2)
    return out


def _weights(a):
    tile = lambda at: list(range(at, at + P))
    w_in = a["w_in"][0]
    c, h, z = 672, 928, 1184
    order = [tile(0), tile(128), tile(256), None]
    for j in range(2):
        order += [tile(c + j * P), tile(h + j * P), tile(416 + j * P)]
    order += [tile(z), tile(z + P)] + [tile(1440 + j * P) for j in range(6)]
    parts = _blocks(w_in, [o if o is not None else [] for o in order])
    odd = w_in.reshape(KT, P, -1).transpose(1, 0, 2)
    kr = 384
    parts[3, :, :, 0:4] = odd[:, :, 2208:2212]
    parts[3, :, :, 64:96] = odd[:, :, kr:kr + 32]
    parts[3, :, :, 96:112] = odd[:, :, kr + 16:kr + 32]
    parts[3, :, :, 112:128] = odd[:, :, kr:kr + 16]
    units = [parts]
    wq, wkv = a["mla_w_q_up"][0], a["mla_w_kv_up"][0]
    mla = np.zeros((MLA_HEADS, P, KT, P), wq.dtype)
    for n in range(MLA_HEADS):
        q = n * QK_DIM
        cols = list(range(q, q + 96)) + list(range(q + 80, q + 96)) + list(range(q + 64, q + 80))
        mla[n, :, 0:2, :] = wq[:, cols].reshape(2, P, P).transpose(1, 0, 2)
        mla[n, :, 2, :] = wkv[:, n * P:(n + 1) * P]
    units.append(mla)
    units.append(_blocks(a["w_out"][0], [tile(m * P) for m in range(KT)]))
    up, down = a["ffn_w_up"][0], a["ffn_w_down"][0]

    def gate_up(pair):
        return _blocks(up, [tile(part * FFN + (2 * pair + x) * P) for x in range(2) for part in range(2)])

    def down_of(pair):
        w = down[2 * pair * P:(2 * pair + 2) * P].reshape(2, P, 2, 4, P)
        return w.transpose(2, 1, 3, 0, 4).reshape(2, P, KT, P)

    units.append(gate_up(0))
    for pair in range(1, FFN_PAIRS):
        first = gate_up(pair)
        units += [first[0:2], down_of(pair - 1), first[2:4]]
    units.append(down_of(FFN_PAIRS - 1))
    w2 = a["w_in_2"][0]
    units.append(_blocks(w2, [tile(part * 512 + n * P) for n in range(4) for part in range(4)]))
    gates = np.zeros((1, P, KT, P), w2.dtype)
    g8 = w2[:, 4608:4616].reshape(KT, P, 8).transpose(1, 0, 2)
    gates[0, :, :, 0:4] = g8[:, :, 0:4]
    gates[0, :, :, 32:36] = g8[:, :, 4:8]
    units.append(gates)
    units.append(_blocks(w2, [tile(2048 + part * 512 + n * P) for n in range(4) for part in range(5)]))
    wa, wb = a["w_a_2"][0], a["w_b_2"][0]
    for m in range(KT):
        units.append(_blocks(w2, [tile(4616 + m * P), tile(5640 + m * P)]))
        units.append(_blocks(np.concatenate([wa, wb]), [tile(m * P)]))
    units.append(_blocks(a["w_out_2"][0], [tile(m * P) for m in range(KT)]))
    return np.concatenate(units).reshape(-1, P, KT * P)


def _vectors(a):
    out = np.zeros((P, NVEC), np.float32)

    def put(name, k, column, at=0):
        out[at:at + len(column), VEC0[name] + k] = column

    for name in _VECTORS_P:
        for k, column in enumerate(a[name][0].reshape(-1, P)):
            put(name, k, column)
    for j in range(2):
        for i in range(3):
            put("sc_conv", 3 * j + i, a["sc_conv_w"][0, i, j * P:(j + 1) * P])
    for j in range(6):
        for i in range(4):
            put("ssd_conv", 5 * j + i, a["ssd_conv_w"][0, i, j * P:(j + 1) * P])
        put("ssd_conv", 5 * j + 4, a["ssd_conv_b"][0, j * P:(j + 1) * P])
    put("dt_bias", 0, a["ssd_dt_bias"][0])
    put("a_log", 0, a["ssd_a_log"][0])
    for j in range(2):
        put("ssd_d", j, np.repeat(a["ssd_d"][0, 2 * j:2 * j + 2], 64))
    for t in range(FT):
        for part in range(2):
            at = part * FFN + t * P
            for i in range(3):
                put("ffn_conv", 8 * t + 4 * part + i, a["ffn_conv_w"][0, i, at:at + P])
            put("ffn_conv", 8 * t + 4 * part + 3, a["ffn_conv_b"][0, at:at + P])
    put("gate_bias", 0, a["b_if_2"][0, 0:4])
    put("gate_bias", 0, a["b_if_2"][0, 4:8], 32)
    for n in range(ML_HEADS):
        for part in range(2):
            for i in range(4):
                at = part * 512 + n * P
                put("ml_conv", 8 * n + 4 * part + i, a["conv_qk_2"][0, i, at:at + P])
        put("norm_a", n, a["norm_a_2"][0, n * P:(n + 1) * P])
        put("norm_b", n, a["norm_b_2"][0, n * P:(n + 1) * P])
    freq = (1.0 / 10000.0 ** (np.arange(0, ROPE, 2) / ROPE)).astype(np.float32)
    put("inv_freq", 0, np.tile(freq, 4), 64)
    put("phase", 0, np.full(32, np.pi / 2, np.float32), 64)
    put("turn", 0, np.full(32, 0.25, np.float32), 64)
    put("sign", 0, np.ones(P, np.float32))
    put("sign", 0, -np.ones(16, np.float32), 96)
    put("eps", 0, np.full(P, EPS, np.float32))
    return out


def _squares():
    rows, columns = np.indices((P, P))
    rope_sum = ((columns >= 64) & (rows >= 64) & (rows % 32 == columns % 32)).astype(np.float32)
    ahead = np.where(columns > rows, np.float32(-1e30), np.float32(0))
    made = {"ident": rows == columns, "ones": np.ones((P, P)), "upto": rows <= columns,
            "rope_sum": rope_sum, "ahead": ahead}
    return np.stack([made[n].astype(np.float32) for n in SQUARES], axis=1)


def _aug_rows():
    t = np.arange(S, dtype=np.float32)
    one = np.ones(S, np.float32)
    return np.stack([np.stack([t, one]), np.stack([-8 * one, 8 * t])])


def kernel(**inputs):
    import concourse.bacc as bacc
    from concourse.bass_utils import run_bass_kernel_spmd

    a = {k: np.asarray(x) for k, x in inputs.items()}
    arrays = {
        "weights": _weights(a),
        "x": a["x"].reshape(S, D),
        "positions": a["positions"].reshape(1, S),
        "vectors": _vectors(a),
        "squares": _squares(),
        "aug_rows": _aug_rows(),
        "lambda_qk": a["lambda_qk_2"].reshape(1, 4 * 64),
    }
    arrays = {k: np.ascontiguousarray(x) for k, x in arrays.items()}
    nc = bacc.Bacc("TRN2", target_bir_lowering=False, num_devices=1)
    args = [nc.dram_tensor(k, x.shape, mybir.dt.from_np(x.dtype), kind="ExternalInput").ap()
            for k, x in arrays.items()]
    args.append(nc.dram_tensor("y", (S, D), F32, kind="ExternalOutput").ap())
    program(nc, *args)
    r = run_bass_kernel_spmd(nc, [arrays], core_ids=[0])
    return np.asarray(r.results[0]["y"]).reshape(1, S, D)
```

```python
from contextlib import ExitStack, contextmanager

import numpy as np

import concourse.bass as bass
from concourse import mybir

ALU = mybir.AluOpType
ACT = mybir.ActivationFunctionType
AX = mybir.AxisListType
F32 = mybir.dt.float32
F32R = mybir.dt.float32r
BF16 = mybir.dt.bfloat16
I32 = mybir.dt.int32

P = 128
S = 1024
D = 1024
KT = D // P
TT = S // P
HALF = 512
MLA_HEADS, QK_DIM, NOPE, ROPE = 8, 96, 64, 32
FFN = 2816
FT = FFN // P
SSD_HEADS = 4
DIFF_HEADS = 4
ML_HEADS = 4
EPS = 1e-6
LAM_INIT = 0.8 - 0.6 * float(np.exp(-0.3 * 0))

ML_UNITS = 6
STAGE_UNITS = [("in", 18), ("mla", MLA_HEADS), ("out", KT), ("ffn", 3 * FT),
               ("diff", 1 + 4 * DIFF_HEADS), ("mlstm", 5 + ML_UNITS * (ML_HEADS - 1)),
               ("merge", 3 * KT), ("out2", KT)]
FFN_PAIRS = FT // 2
STAGE_GROUPS = [("x", TT), ("in", 18), ("krot", 1), ("cols", 1), ("ssd", 2 * 11), ("mla", 11 * MLA_HEADS),
                ("out", KT), ("ffn_first", 4), ("ffn", 12 * (FFN_PAIRS - 1)), ("ffn_last", 8),
                ("diff", 7),
                ("merge_first", 2), ("merge", 4 * (KT - 2)), ("merge_last", 4),
                ("out2", KT - 2), ("x_back", TT), ("out2_last", 2), ("y", TT)]


def starts(stages):
    at, out = 0, {}
    for name, n in stages:
        out[name] = at
        at += n
    return out, at


UNIT0, UNITS = starts(STAGE_UNITS)
assert UNITS % 2 == 0
GROUP0, GROUPS = starts(STAGE_GROUPS)
DIFF_HALVES, ML_HALVES = 12, 18
STAGE_HALVES = [("diff", DIFF_HALVES * (DIFF_HEADS - 1) + 10), ("mlstm_first", 8),
                ("mlstm", ML_HALVES * (ML_HEADS - 1) + 6)]

HALF0, _ = starts(STAGE_HALVES)

NORMS = [("mix_pre", 1), ("q", 2), ("kv", 1), ("ssd", 2), ("mix_post", 1), ("ffn_pre", 8),
         ("ffn_post", 1), ("pre2", 8), ("post2", 1)]
POST_NORMS = ["mix_post", "ffn_post", "post2"]
NORM_TILES0, _ = starts(NORMS)
NORM_INDEX = {name: i for i, (name, _) in enumerate(NORMS)}
SPLITS = [("mix_pre", 8), ("q", 2), ("kv", 1), ("mix", 8), ("ffn_pre", 8), ("pre2", 8), ("y", 8),
          ("merged", 8)]
SPLIT0, _ = starts(SPLITS)

VECTORS = [("norm_mix_pre", 8), ("norm_mix_post", 8), ("norm_ffn_pre", 8), ("norm_ffn_post", 8),
           ("norm_pre_2", 8), ("norm_post_2", 8), ("mla_q_norm", 2), ("mla_kv_norm", 1),
           ("ssd_norm", 2), ("sc_conv", 2 * 3), ("ssd_conv", 6 * 5), ("dt_bias", 1), ("a_log", 1),
           ("ssd_d", 2), ("ffn_conv", FT * 2 * 4), ("gate_bias", 1), ("ml_conv", ML_HEADS * 2 * 4),
           ("norm_a", 4), ("norm_b", 4), ("inv_freq", 1), ("phase", 1), ("turn", 1), ("sign", 1),
           ("eps", 1)]
VEC0, NVEC = starts(VECTORS)
SQUARES = ["ident", "ones", "below", "rope_sum", "ahead"]


def program(nc, wts, x_in, pos, vec_in, sq_in, aug_in, lam_in, y_out):
    spill = nc.dram_tensor("x_spill", (P, KT * S), F32).ap()
    with ExitStack() as ctx:
        KB = 1024
        base = nc.sbuf_base
        base += (-base) % 64

        def at(name, kb, shape, dt=F32):
            return nc.alloc_sbuf_tensor_at(name, shape, dt, offset=base + int(kb * KB))

        def sem(name):
            return ctx.enter_context(nc.semaphore(name))

        X = at("X", 0, [P, KT, S])
        RAW = at("RAW", 32, [P, KT, S])
        HH = at("HH", 64, [P, KT, S], F32R)
        HL = at("HL", 96, [P, KT, S], F32R)
        WR = at("WR", 128, [P, 2, KT * P])
        WH = at("WH", 136, [P, 2, KT * P], F32R)
        WL = at("WL", 144, [P, 2, KT * P], F32R)
        SQ = at("SQ", 152, [P, 2, S])
        RS = at("RS", 160, [P, S])
        T = at("T", 164, [P, 2, S])
        vec = at("vec", 204, [P, NVEC])
        cols = at("cols", 204 + 1.25, [P, 16])
        sqf = at("sqf", 204 + 1.3125, [P, 4, P])
        identb = at("identb", 204 + 3.3125, [P, P], BF16)
        aheadb = at("aheadb", 204 + 3.5625, [P, P], BF16)
        zero = at("zero", 204 + 3.8125, [P, 1])
        assert NVEC * 4 <= 1.25 * KB
        ident, ones, below, rope_sum = (sqf[:, n, :] for n in range(4))
        aheadf = at("aheadf", 152, [P, P])
        ZS = at("ZS", 172, [P, 2, S])
        XBC = at("XBC", 180, [P, 6, S])
        DR = RAW[:, 3, :]
        selA = at("selA", 70.5, [P, P])
        DTC = at("DTC", 71, [P, TT, SSD_HEADS])
        NAC = at("NAC", 71.125, [P, TT, SSD_HEADS])
        XD = at("XD", 72, [P, TT, 2, P])
        AB = at("AB", 80, [P, 2, S])
        EX = at("EX", 160, [P, 2, S])
        DD = [at("DD0", 88, [P, 2, S]), at("DD1", 152, [P, 2, S])]
        PP = at("PP", 96, [P, 2, S])
        YS = at("YS", 104, [P, 2, S])
        TAB = at("TAB", 112, [P, S])
        TABR = RAW[:, 6, :]
        ANG = at("ANG", 196, [P, S])
        KK = at("KK", 200, [P, S])
        KR = at("KR", 124, [P, S])
        POSI = at("POSI", 32 + 28, [P, S], I32)
        ROWS = at("ROWS", 184, [4, 5, S])
        QNH = at("QNH", 64, [P, 2, S], F32R)
        QNL = at("QNL", 72, [P, 2, S], F32R)
        KNH = at("KNH", 80, [P, 1, S], F32R)
        KNL = at("KNL", 84, [P, 1, S], F32R)
        QOP = at("QOP", 88, [P, 2, S])
        KOP = at("KOP", 96, [P, 2, S])
        VP = at("VP", 104, [P, 2, TT, P])
        KV = at("KV", 116, [P, 2, S])
        PR = [at("PR0", 152, [P, 2, S]), at("PR1", 160, [P, 2, S])]
        PTB = at("PTB", 172, [P, 2, TT, HALF])
        GH = at("GH", 172, [P, 2, S], F32R)
        GL = at("GL", 180, [P, 2, S], F32R)
        VG = at("VG", 188, [P, S])
        VU = at("VU", 192, [P, S])
        SG = at("SG", 196, [P, S])
        PRD = at("PRD", 200, [P, S])
        DQ = at("DQ", 0, [P, 2, S])
        DK = at("DK", 8, [P, 2, S])
        DVT = at("DVT", 16, [P, S])
        DVT0 = SQ[:, 0, :]
        DV = at("DV", 20, [P, TT, P])
        NQ = at("NQ", 164, [P, S])
        NK = at("NK", 168, [P, S])
        DO = at("DO", 28, [P, S])
        DP = at("DP", 172, [P, 2, 2, S])
        DPT = at("DPT", 188, [P, TT, HALF])
        GR = at("GR", 156, [P, S])
        GROWS = at("GROWS", 172, [4, 7, S])
        ACOL = at("ACOL", 24, [P, TT, ML_HEADS])
        selM = at("selM", 25, [P, 2, P])
        MQ = at("MQ", 0, [P, S])
        MK = at("MK", 4, [P, S])
        MO = at("MO", 8, [P, S])
        MX = at("MX", 12, [P, S])
        MVT, MV = DVT, DV
        MH = at("MH", 28, [P, S])
        MR = [NQ, NK]
        MC = [at("MCQ", 196, [P, S]), at("MCK", 200, [P, S])]
        MN = at("MN", 172, [P, S])
        ME = at("ME", 176, [P, S])
        MD = at("MD", 180, [P, 2, S])
        MP = at("MP", 188, [P, 2, S])
        lam_sb = at("lam_sb", 200, [P, 4 * 64])
        YH = at("YH", 0, [P, KT, S], F32R)
        YL = at("YL", 172, [P, KT, S], F32R)
        MS = [at("MS_0", 156, [P, S]), at("MS_1", 160, [P, S])]
        MS2 = [at("MS2_0", 168, [P, S]), at("MS2_1", 152, [P, S])]
        MA = at("MA", 164, [P, S])
        OUT2 = at("OUT2", 172, [P, KT, S])
        XT = RAW

        PG = ctx.enter_context(nc.psum_tensor("PG", [P, 2, S], F32))
        PT = ctx.enter_context(nc.psum_tensor("PT", [P, 2, HALF], F32))
        PO = ctx.enter_context(nc.psum_tensor("PO", [P, 2, HALF], F32))
        POf = PO[:, :, :].rearrange("p a n -> p (a n)")
        PTf = PT[:, :, :].rearrange("p a n -> p (a n)")

        w_loaded = [sem("w_loaded0"), sem("w_loaded1")]
        w_hi = sem("w_hi")
        w_split = sem("w_split")
        w_used = sem("w_used")
        zero_set = sem("zero_set")
        g_ready = sem("g_ready")
        g_free = [sem("g_free0"), sem("g_free1")]
        dve_step = sem("dve_step")
        act_step = sem("act_step")
        const_in = sem("const_in")
        x_loaded = [sem(f"x_loaded{i}") for i in range(TT)]
        x_squared = sem("x_squared")
        consts_ready = sem("consts_ready")
        n_sq, n_sq_used = sem("n_sq"), sem("n_sq_used")
        n_root = sem("n_root")
        sq_new, sq_sum = sem("sq_new"), sem("sq_sum")
        s_raw, s_hi, s_lo = sem("s_raw"), sem("s_hi"), sem("s_lo")
        n_done = sem("n_done")
        in_act, in_dve = sem("in_act"), sem("in_dve")
        xbc_ready = sem("xbc_ready")
        rows_act, rows_dve = sem("rows_act"), sem("rows_dve")
        pos_in, tab_r, tab_sin = sem("pos_in"), sem("tab_r"), sem("tab_sin")
        tab_done = sem("tab_done")
        ssd_rows, sel_set = sem("ssd_rows"), sem("sel_set")
        dd_ready, e_ready = sem("dd_ready"), sem("e_ready")
        pp_ready, pv_used, ssd_x = sem("pp_ready"), sem("pv_used"), sem("ssd_x")
        ssd_acc, ssd_y = sem("ssd_acc"), sem("ssd_y")
        krot_t, krot_done = sem("krot_t"), sem("krot_done")
        q_op, k_op, v_op, kv_cp = sem("q_op"), sem("k_op"), sem("v_op"), sem("kv_cp")
        m_neg, m_exp, m_prob = sem("m_neg"), sem("m_exp"), sem("m_prob")
        t_ready = sem("t_ready")
        t_free = sem("t_free")
        pv_half, att_free = sem("pv_half"), sem("att_free")
        f_act, f_silu, f_prod, f_hi, f_lo = (sem(n) for n in (
            "f_act", "f_silu", "f_prod", "f_hi", "f_lo"))
        spilled, aug_set, aug_k, lam_loaded, lam_prod, lam_exp, lam_ready = (sem(n) for n in (
            "spilled", "aug_set", "aug_k", "lam_loaded", "lam_prod", "lam_exp", "lam_ready"))
        d_q, d_k, d_v, d_vop = (sem(n) for n in ("d_q", "d_k", "d_v", "d_vop"))
        d_scores, d_neg, d_exp, d_prob, d_tready, d_tfree, d_half = (sem(n) for n in (
            "d_scores", "d_neg", "d_exp", "d_prob", "d_tready", "d_tfree", "d_half"))
        hb_ready = sem("hb_ready")
        hb_free = [sem("hb_free0"), sem("hb_free1")]
        d_o, d_sq, d_root, d_y = (sem(n) for n in ("d_o", "d_sq", "d_root", "d_y"))
        aug_loaded = sem("aug_loaded")
        gate_rows, m_sel = sem("gate_rows"), sem("m_sel")
        m_conv, m_taps, m_q, m_v, m_o, m_vop, m_scores = (sem(n) for n in (
            "m_conv", "m_taps", "m_q", "m_v", "m_o", "m_vop", "m_scores"))
        m_mn, m_me, m_dd, m_e, m_pp, m_used, m_acc, m_abs, m_h, m_sq, m_root, m_y = (
            sem(n) for n in ("m_mn", "m_me", "m_dd", "m_e", "m_pp", "m_used", "m_acc", "m_abs",
                             "m_h", "m_sq", "m_root", "m_y"))
        g_sig, g_done = sem("g_sig"), sem("g_done")
        x_back = sem("x_back")
        y_stored = sem("y_stored")

        PRIMED = {"pe": [pv_half, d_half, m_used],
                  "act": [att_free, d_o, d_exp],
                  "dve": [hb_free[0], hb_free[1], sq_sum, m_h, m_y, d_y, m_pp, g_done, d_prob, m_prob]}

        def primed(eng, semaphore, value):
            eng.wait_ge(semaphore, value + 1)

        def v(name, k=0):
            return vec[:, VEC0[name] + k:VEC0[name] + k + 1]

        class Groups:

            def __init__(self, stage, i=0, stride=0, first=0):
                self.base, self.i, self.stride = GROUP0[stage] + first, i, stride
                assert stride % 2 == 0

            def slot(self, k):
                return (self.base + k) % 2

            def psum(self, k):
                return PG[:, self.slot(k), :]

            def before(self, pe, k):
                n = (self.base + k) // 2
                if n or not isinstance(self.i, int):
                    pe.wait_ge(g_free[self.slot(k)], self.i * (self.stride // 2) + n)

            def ready(self, eng, k):
                eng.wait_ge(g_ready, self.i * self.stride + (self.base + k + 1))

            def free(self, k):
                return g_free[self.slot(k)]

            def wait_free(self, eng, k):
                eng.wait_ge(g_free[self.slot(k)],
                            self.i * (self.stride // 2) + ((self.base + k) // 2 + 1))

        class Steps:

            def __init__(self, eng, semaphore):
                self.eng, self.sem, self.n, self.off = eng, semaphore, 0, 0

            def __call__(self, ins):
                ins.then_inc(self.sem, 1)
                self.n += 1
                self.eng.wait_ge(self.sem, self.off + self.n)

            @contextmanager
            def loop(self, start, end, per):
                n0 = self.n
                with self.eng.Fori(start, end) as i:
                    self.off = i * per - start * per
                    yield i
                assert self.n - n0 == per, (self.n - n0, per)
                self.off, self.n = 0, n0 + per * (end - start)

        def unit_slot(stage, k):
            return (UNIT0[stage] + k) % 2

        NDONE0 = {"q": 0, "kv": 2, "ssd": 3, "mix_post": 5, "ffn_post": 5 + KT}
        NDONE = {"q": 2, "kv": 3, "ssd": 5, "mix_post": 5 + KT, "ffn_post": 5 + 2 * KT}

        def diff_scores(t, c):
            at = c * HALF if t < 4 else 0
            return PG[:, 0, at:at + (t + 1) * P]

        def diff_neg(t, c):
            return t + 1 if t < 4 else 4 + 2 * (t - 4) + c + 1

        def mla_bank(t, hh, q):
            return 2 * t + hh if t < 4 else 8 + 4 * (t - 4) + 2 * hh + q

        def halves(m):
            return slice((m % 2) * HALF, (m % 2 + 1) * HALF)

        class Halves:

            def __init__(self, stage, i=0, stride=0):
                self.base, self.i, self.stride = HALF0[stage], i, stride
                assert stride % 2 == 0 and self.base % 2 == 0

            def bank(self, m):
                return PG[:, 1, halves(m)]

            def free(self, m):
                return hb_free[m % 2]

            def before(self, pe, m):
                primed(pe, hb_free[m % 2], self.i * (self.stride // 2) + (self.base + m) // 2)

            def ready(self, eng, m):
                eng.wait_ge(hb_ready, self.i * self.stride + (self.base + m + 1))

            def wait_free(self, eng, m):
                primed(eng, hb_free[m % 2],
                       self.i * (self.stride // 2) + ((self.base + m) // 2 + 1))

        block = ctx.enter_context(nc.Block())

        @block.sync
        def _(sp):
            sp.dma_start(vec[:, :], vec_in).then_inc(const_in, 16)
            sp.dma_start(sqf[:, :, :], sq_in[:, 0:4, :]).then_inc(const_in, 16)
            sp.dma_start(aheadf[:, :], sq_in[:, 4, :]).then_inc(const_in, 16)
            for t in range(TT):
                sp.dma_start(RAW[:, t, :], x_in[t * P:(t + 1) * P, :]).then_inc(x_loaded[t], 16)

            def load(u, s):
                sp.dma_start(WR[:, s, :], u).then_inc(w_loaded[s], 16)

            load(wts[0], 0)
            load(wts[1], 1)
            with sp.Fori(1, UNITS // 2) as i:
                for s in range(2):
                    sp.wait_ge(w_split, 2 * i + (s - 1))
                    load(wts[bass.ds(2 * i + s, 1)].rearrange("a p n -> p (a n)"), s)

        @block.gpsimd
        def _(pool):
            pool.memset(zero[:, :], 0.0).then_inc(zero_set, 1)
            pool.wait_ge(zero_set, 1)

            def split(i, s, reused):
                pool.wait_ge(w_loaded[s], 16 * i + 16)
                if reused:
                    pool.wait_ge(w_used, 2 * i + s)
                pool.tensor_tensor(WH[:, s, :], WR[:, s, :], zero[:, :].to_broadcast([P, KT * P]),
                                   ALU.add).then_inc(w_hi, 1)
                pool.wait_ge(w_hi, 2 * i + (s + 1))
                pool.tensor_tensor(WL[:, s, :], WR[:, s, :], WH[:, s, :].bitcast(F32),
                                   ALU.subtract).then_inc(w_split, 1)

            split(0, 0, False)
            split(0, 1, False)
            with pool.Fori(1, UNITS // 2) as i:
                for s in range(2):
                    split(i, s, True)

        @block.tensor
        def _(pe):
            for semaphore in PRIMED["pe"]:
                pe.sem_inc(semaphore, 1)

            def product(out, blocks, first=None):
                for h in range(2):
                    cut = slice(h * HALF, (h + 1) * HALF)
                    for n, (slot, b, hi, lo) in enumerate(blocks):
                        w = slice(b * P, (b + 1) * P)
                        last = n == len(blocks) - 1
                        m = pe.matmul(out[:, cut], WH[:, slot, w], hi[:, cut], start=n == 0, stop=False)
                        if first is not None and h == 0 and n == 0:
                            m.then_inc(first, 1)
                        pe.matmul(out[:, cut], WH[:, slot, w], lo[:, cut], start=False, stop=False)
                        m = pe.matmul(out[:, cut], WL[:, slot, w], hi[:, cut], start=False, stop=last)
                return m

            def unit(stage, k, i=0, stride=0):
                pe.wait_ge(w_split, i * stride + (UNIT0[stage] + k + 1))
                return unit_slot(stage, k)

            def projection(stage, g, k, u, hi, lo, i=0, stride=0):
                slot = unit(stage, u, i, stride)
                g.before(pe, k)
                product(g.psum(k), [(slot, b, hi[:, b, :], lo[:, b, :]) for b in range(KT)],
                        w_used).then_inc(g_ready, 1)

            def first_pair(stage, g, k, name, hi=HH, lo=HL):
                for b in range(KT):
                    pe.wait_ge(s_lo, SPLIT0[name] + b + 1)
                    w = slice(b * P, (b + 1) * P)
                    for n in range(2):
                        slot = unit(stage, n)
                        if b == 0:
                            g.before(pe, k + n)
                        for h in range(2):
                            cut = slice(h * HALF, (h + 1) * HALF)
                            out = g.psum(k + n)[:, cut]
                            m = pe.matmul(out, WH[:, slot, w], hi[:, b, cut], start=b == 0, stop=False)
                            if b == 0 and n == 0 and h == 0:
                                m.then_inc(w_used, 1)
                            m = pe.matmul(out, WH[:, slot, w], lo[:, b, cut], start=False, stop=False)
                            if b == KT - 1 and n == 1 and h == 1:
                                m.then_inc(w_used, 1)
                            m = pe.matmul(out, WL[:, slot, w], hi[:, b, cut], start=False,
                                          stop=b == KT - 1)
                        if b == KT - 1:
                            m.then_inc(g_ready, 1)

            def norm(name):
                tiles, t0, n = dict(NORMS)[name], NORM_TILES0[name], NORM_INDEX[name]
                for k in range(tiles):
                    pe.wait_ge(n_sq, t0 + k + 1)
                    for h in range(2):
                        m = pe.matmul(PO[:, h, :], ones, SQ[:, k % 2, h * HALF:(h + 1) * HALF],
                                      start=k == 0, stop=k == tiles - 1)
                        if h == 1:
                            m.then_inc(n_sq_used, 1)

            def turn_tiles(g, src):
                for t in range(TT):
                    g.before(pe, t)
                    for k in range(KT):
                        m = pe.transpose(g.psum(t)[:, k * P:(k + 1) * P],
                                         src[:, k, t * P:(t + 1) * P], ident)
                    m.then_inc(g_ready, 1)

            def wait_split(name):
                pe.wait_ge(s_lo, SPLIT0[name] + dict(SPLITS)[name])

            def turn(out, src):
                for t in range(TT):
                    m = pe.transpose(out[:, t * P:(t + 1) * P], src[:, t * P:(t + 1) * P], ident)
                return m

            pe.wait_ge(consts_ready, 1)
            g = Groups("x")
            for t in range(TT):
                pe.wait_ge(x_loaded[t], 16)
                g.before(pe, t)
                turn(g.psum(t), RAW[:, t, :]).then_inc(g_ready, 1)
            norm("mix_pre")

            first_pair("in", Groups("in"), 0, "mix_pre")
            for k in (2, 3, 4, 5):
                projection("in", Groups("in"), k, k, HH, HL)
                if k == 4:
                    norm("q")
            norm("kv")
            with pe.Fori(3, 9) as i:
                g = Groups("in", i, 2)
                for k in range(2):
                    projection("in", g, k, k, HH, HL, i, 2)

            g = Groups("krot")
            pe.wait_ge(krot_t, 1)
            g.before(pe, 0)
            for h in range(2):
                m = pe.matmul(g.psum(0)[:, h * HALF:(h + 1) * HALF], rope_sum,
                              RAW[:, 3, h * HALF:(h + 1) * HALF], start=True, stop=True)
            m.then_inc(g_ready, 1)
            g = Groups("cols")
            pe.wait_ge(ssd_rows, 1)
            g.before(pe, 0)
            turn(g.psum(0), DR).then_inc(g_ready, 1)

            pe.wait_ge(xbc_ready, 6)
            for grp in range(2):
                g = Groups("ssd", first=11 * grp)
                g.before(pe, 0)
                turn(g.psum(0), XBC[:, grp, :]).then_inc(g_ready, 1)
                for hh in range(2):
                    pe.wait_ge(sel_set, 2 * grp + hh + 1)
                    g.before(pe, 1 + hh)
                    for h in range(2):
                        m = pe.matmul(g.psum(1 + hh)[:, h * HALF:(h + 1) * HALF], selA[:, :],
                                      DR[:, h * HALF:(h + 1) * HALF], start=True, stop=True)
                    m.then_inc(g_ready, 1)

                def scores(j):
                    g.before(pe, 3 + j)
                    for h in range(j // 4, 2):
                        a = max(h * HALF, j * P)
                        m = pe.matmul(g.psum(3 + j)[:, a:(h + 1) * HALF],
                                      XBC[:, 2 + grp, j * P:(j + 1) * P],
                                      XBC[:, 4 + grp, a:(h + 1) * HALF], start=True, stop=True)
                    m.then_inc(g_ready, 1)

                def values(j):
                    for hh in range(2):
                        pe.wait_ge(pp_ready, 16 * grp + 2 * j + hh + 1)
                        for h in range(j // 4, 2):
                            a = max(h * HALF, j * P)
                            m = pe.matmul(PO[:, h, a - h * HALF:HALF], XD[:, j, hh, :],
                                          PP[:, hh, a:(h + 1) * HALF],
                                          start=j == 0 and hh == 0,
                                          stop=hh == 1 and j == 4 * h + 3)
                        m.then_inc(pv_used, 1)

                pe.wait_ge(ssd_x, grp + 1)
                if grp:
                    pe.wait_ge(ssd_acc, grp)
                for j in range(TT):
                    scores(j)
                    if j:
                        values(j - 1)
                values(TT - 1)
            pe.wait_ge(ssd_acc, 2)
            norm("ssd")

            wait_split("kv")
            with pe.Fori(0, MLA_HEADS // 2) as i:
                g = Groups("mla", i, 22)
                for hh in range(2):
                    slot = unit("mla", hh, i, 2)
                    g.before(pe, 2 * hh)
                    product(g.psum(2 * hh), [(slot, b, QNH[:, b, :], QNL[:, b, :]) for b in range(2)],
                            w_used).then_inc(g_ready, 1)
                    g.before(pe, 2 * hh + 1)
                    product(g.psum(2 * hh + 1), [(slot, 2, KNH[:, 0, :], KNL[:, 0, :])])\
                        .then_inc(g_ready, 1)
                for hh in range(2):
                    pe.wait_ge(kv_cp, 2 * i + (hh + 1))
                    g.before(pe, 4 + hh)
                    turn(g.psum(4 + hh), KV[:, hh, :]).then_inc(g_ready, 1)

                def scores(t, hh):
                    n = 6 + 2 * t + hh
                    g.before(pe, n)
                    for h in range(t // 4 + 1):
                        end = min((h + 1) * HALF, (t + 1) * P)
                        pe.matmul(g.psum(n)[:, h * HALF:end], QOP[:, hh, t * P:(t + 1) * P],
                                  KOP[:, hh, h * HALF:end], start=True, stop=end != (t + 1) * P)
                    pe.matmul(g.psum(n)[:, t * P:(t + 1) * P], identb[:, :], aheadb[:, :],
                              start=False, stop=True).then_inc(g_ready, 1)

                def transposes(t, hh):
                    primed(pe, m_prob, i * (2 * TT) + (2 * t + hh + 1))
                    for q in range(t // 4 + 1):
                        n = mla_bank(t, hh, q)
                        if n >= 2:
                            pe.wait_ge(t_free, i * 24 + (n - 1))
                        for b in range(4 * q, min(4 * q + 4, t + 1)):
                            m = pe.transpose(PT[:, n % 2, (b - 4 * q) * P:(b - 4 * q + 1) * P],
                                             PR[t % 2][:, hh, b * P:(b + 1) * P], ident)
                        m.then_inc(t_ready, 1)

                def values(h, hh):
                    pe.wait_ge(t_free, i * 24 + (8 if h == 0 else 24) - (1 - hh) * (1 if h == 0 else 2))
                    if h == 0 and hh == 0:
                        primed(pe, att_free, i)
                    for j in range(4 * h + 4):
                        a = max(0, j * P - h * HALF)
                        m = pe.matmul(PO[:, h, a:HALF], VP[:, hh, j, :], PTB[:, hh, j, a:HALF],
                                      start=hh == 0 and j == 0, stop=hh == 1 and j == 4 * h + 3)
                    m.then_inc(pv_half, 1)

                pe.wait_ge(krot_done, 2)
                for hh in range(2):
                    pe.wait_ge(q_op, 2 * i + (hh + 1))
                    pe.wait_ge(k_op, 2 * i + (hh + 1))
                    scores(0, hh)
                for t in range(TT):
                    for hh in range(2):
                        if t + 1 < TT:
                            scores(t + 1, hh)
                    if t == 4:
                        for hh in range(2):
                            pe.wait_ge(v_op, 2 * i + (hh + 1))
                            values(0, hh)
                    for hh in range(2):
                        transposes(t, hh)
                for hh in range(2):
                    values(1, hh)

            first_pair("out", Groups("out"), 0, "mix")
            with pe.Fori(1, KT // 2) as i:
                g = Groups("out", i, 2)
                for k in range(2):
                    projection("out", g, k, k, HH, HL, i, 2)
            norm("mix_post")
            norm("ffn_pre")

            DOWN = 8

            def gate_up(g, k, u, i=0, stride=0):
                for n in range(2):
                    projection("ffn", g, k + n, u + n, HH, HL, i, stride)

            def down(g, k, u, pair, i=0, stride=0):
                pe.wait_ge(f_lo, 2 * pair + 2)
                for m in range(DOWN):
                    if m % 4 == 0:
                        slot = unit("ffn", u + m // 4, i, stride)
                    g.before(pe, k + m)
                    last = product(g.psum(k + m), [(slot, 2 * (m % 4) + b, GH[:, b, :], GL[:, b, :])
                                                   for b in range(2)], w_used if m % 4 == 0 else None)
                    last.then_inc(g_ready, 1)

            g = Groups("ffn_first")
            first_pair("ffn", g, 0, "ffn_pre")
            gate_up(g, 2, 2)
            with pe.Fori(0, FFN_PAIRS - 1) as i:
                g = Groups("ffn", i, 12)
                gate_up(g, 0, 4, i, 6)
                down(g, 2, 6, i, i, 6)
                gate_up(g, 10, 8, i, 6)
            g = Groups("ffn_last")
            down(g, 0, 4 + 6 * (FFN_PAIRS - 1), FFN_PAIRS - 1)
            norm("ffn_post")
            norm("pre2")

            g = Groups("diff")
            first_pair("diff", g, 0, "pre2")
            for k in range(2, 5):
                projection("diff", g, k, k, HH, HL)
            pe.wait_ge(d_v, 1)
            g.before(pe, 5)
            turn(g.psum(5), DVT0[:, :]).then_inc(g_ready, 1)
            pe.wait_ge(gate_rows, 1)
            g.before(pe, 6)
            turn(g.psum(6), GR[:, :]).then_inc(g_ready, 1)
            for k in (5, 6):
                g.wait_free(pe, k)

            def fill(hb, stage, unit0, n, i, stride, m0=None):
                u, h, part = n // 4, (n // 2) % 2, n % 2
                slot = unit(stage, unit0 + u, i, stride)
                bank = n // 2 if m0 is None else m0 + h
                out = hb.bank(bank)
                if part == 0:
                    hb.before(pe, bank)
                cut = slice(h * HALF, (h + 1) * HALF)
                for b in range(part * KT // 2, (part + 1) * KT // 2):
                    w = slice(b * P, (b + 1) * P)
                    m = pe.matmul(out, WH[:, slot, w], HH[:, b, cut], start=b == 0, stop=False)
                    if b == 0 and h == 0:
                        m.then_inc(w_used, 1)
                    pe.matmul(out, WH[:, slot, w], HL[:, b, cut], start=False, stop=False)
                    m = pe.matmul(out, WL[:, slot, w], HH[:, b, cut], start=False, stop=b == KT - 1)
                if part == 1:
                    m.then_inc(hb_ready, 1)

            def turn_halves(hb, m0, src, first=None):
                for m in (m0, m0 + 1):
                    hb.before(pe, m)
                    for b in range(4):
                        t = 4 * (m % 2) + b
                        ins = pe.transpose(hb.bank(m)[:, b * P:(b + 1) * P],
                                           src[:, t * P:(t + 1) * P], ident)
                        if first is not None and m == m0 and b == 0:
                            ins.then_inc(first, 1)
                    ins.then_inc(hb_ready, 1)

            def spread(hb, m0, lhs, rhs):
                for m in (m0, m0 + 1):
                    hb.before(pe, m)
                    pe.matmul(hb.bank(m), lhs, rhs[:, halves(m)], start=True, stop=True)\
                      .then_inc(hb_ready, 1)

            def diff_head(i, last=False):
                hb = Halves("diff", i, DIFF_HALVES)

                def next_head(n):
                    fill(hb, "diff", 5, n, i, 4)

                def scores(t, c):
                    before = 2 * t + c - (1 if 1 <= t < 4 else c if t == 0 else 0)
                    primed(pe, d_exp, i * (2 * TT) + before)
                    out = diff_scores(t, c)
                    for h in range(t // 4 + 1):
                        end = min((h + 1) * HALF, (t + 1) * P)
                        pe.matmul(out[:, h * HALF:end], DQ[:, c, t * P:(t + 1) * P],
                                  DK[:, c, h * HALF:end], start=True, stop=end != (t + 1) * P)
                    pe.matmul(out[:, t * P:(t + 1) * P], identb[:, :], aheadb[:, :],
                              start=False, stop=True).then_inc(d_scores, 1)

                def transposes(t):
                    primed(pe, d_prob, i * TT + (t + 1))
                    for q in range(t // 4 + 1):
                        n = t if t < 4 else 4 + 2 * (t - 4) + q
                        if n >= 2:
                            pe.wait_ge(d_tfree, i * 12 + (n - 1))
                        for b in range(4 * q, min(4 * q + 4, t + 1)):
                            m = pe.transpose(PT[:, n % 2, (b - 4 * q) * P:(b - 4 * q + 1) * P],
                                             DP[:, t % 2, 0, b * P:(b + 1) * P], ident)
                        m.then_inc(d_tready, 1)

                def values(h):
                    pe.wait_ge(d_tfree, i * 12 + (4 if h == 0 else 12))
                    if h == 0:
                        pe.wait_ge(d_vop, i + 1)
                        primed(pe, d_o, i)
                    for j in range(4 * h + 4):
                        a = max(0, j * P - h * HALF)
                        m = pe.matmul(PO[:, h, a:HALF], DV[:, j, :], DPT[:, j, a:HALF],
                                      start=j == 0, stop=j == 4 * h + 3)
                    m.then_inc(d_half, 1)

                pe.wait_ge(d_q, i + 1)
                pe.wait_ge(d_k, i + 1)
                for t in range(TT):
                    for c in range(2):
                        scores(t, c)
                        if t >= 4:
                            next_head(2 * t + c - 4)
                        elif c:
                            next_head(t)
                        if t == 5 and c == 0:
                            values(0)
                    if t:
                        transposes(t - 1)
                next_head(12)
                next_head(13)
                transposes(TT - 1)
                next_head(14)
                next_head(15)
                if not last:
                    pe.wait_ge(d_v, i + 2)
                    turn_halves(hb, 8, DVT)
                values(1)
                pe.wait_ge(d_sq, i + 1)
                spread(hb, 8 if last else 10, ones, SQ[:, 0, :])

            pe.wait_ge(aug_set, 1)
            with pe.Fori(0, DIFF_HEADS - 1) as i:
                diff_head(i)
            diff_head(DIFF_HEADS - 1, True)
            primed(pe, d_exp, DIFF_HEADS * 2 * TT)

            hb = Halves("mlstm_first")
            for n in range(4):
                fill(hb, "mlstm", 4, n, 0, 0)
            turn_halves(hb, 2, MVT)
            pe.wait_ge(m_sel, 1)
            spread(hb, 4, selM[:, 0, :], GR)
            spread(hb, 6, selM[:, 1, :], GR)

            def mlstm_head(i, last=False):
                hb = Halves("mlstm", i, ML_HALVES)

                def next_head(start, end):
                    for n in range(start, end):
                        if last:
                            fill(hb, "merge", 0, n, 0, 0)
                        else:
                            fill(hb, "mlstm", 5, n, i, ML_UNITS, 16 if n >= 16 else 2 * (n // 4))

                def scores(j):
                    primed(pe, m_pp, i * TT + j)
                    for h in range(j // 4, 2):
                        a = max(h * HALF, j * P)
                        m = pe.matmul(PG[:, 0, a:(h + 1) * HALF], MK[:, j * P:(j + 1) * P],
                                      MQ[:, a:(h + 1) * HALF], start=True, stop=True)
                    m.then_inc(m_scores, 1)

                def values(j):
                    primed(pe, m_pp, i * TT + (j + 1))
                    for lhs, acc in ((MV[:, j, :], PO), (ones, PT)):
                        for h in range(j // 4, 2):
                            a = max(h * HALF, j * P)
                            m = pe.matmul(acc[:, h, a - h * HALF:HALF], lhs,
                                          MP[:, j % 2, a:(h + 1) * HALF],
                                          start=j == 0, stop=j == 4 * h + 3)
                    m.then_inc(m_used, 1)

                pe.wait_ge(m_q, 2 * i + 2)
                for j in range(TT):
                    scores(j)
                    if last:
                        next_head(max(j - 4, 0), max(j - 3, 0))
                    else:
                        next_head(*((j, j + 1) if j < 4 else (2 * j - 4, 2 * j - 2)))
                    if j == 1:
                        pe.wait_ge(m_vop, i + 1)
                        primed(pe, m_h, i)
                    if j:
                        values(j - 1)
                if not last:
                    next_head(12, 14)
                values(TT - 1)
                next_head(*((4, 8) if last else (14, 16)))
                if not last:
                    pe.wait_ge(m_v, i + 2)
                    unit("mlstm", 9, i, ML_UNITS)
                    turn_halves(hb, 8, MVT, w_used)
                    pe.wait_ge(m_sel, i + 2)
                    spread(hb, 10, selM[:, 0, :], GR)
                    spread(hb, 12, selM[:, 1, :], GR)
                pe.wait_ge(m_sq, i + 1)
                spread(hb, 4 if last else 14, ones, SQ[:, 0, :])
                if not last:
                    next_head(20, 24)

            with pe.Fori(0, ML_HEADS - 1) as i:
                mlstm_head(i)
            mlstm_head(ML_HEADS - 1, True)
            primed(pe, m_pp, ML_HEADS * TT)
            for m in (4, 5):
                Halves("mlstm", ML_HEADS - 1, ML_HALVES).wait_free(pe, m)

            g = Groups("merge_first")
            for k in range(2):
                projection("merge", g, k, 2 + k, HH, HL)
            wait_split("y")

            def mixers(g, k, slot):
                for n in range(2):
                    g.before(pe, k + n)
                    product(g.psum(k + n), [(slot, 4 * n + b, YH[:, 4 * n + b, :], YL[:, 4 * n + b, :])
                                            for b in range(4)], w_used if n == 0 else None)\
                        .then_inc(g_ready, 1)

            with pe.Fori(0, KT // 2 - 1) as i:
                g = Groups("merge", i, 8)
                for n in range(2):
                    mixers(g, 4 * n, unit("merge", 4 + 3 * n, i, 6))
                    for k in range(2):
                        projection("merge", g, 4 * n + 2 + k, 5 + 3 * n + k, HH, HL, i, 6)
            g = Groups("merge_last")
            for n in range(2):
                mixers(g, 2 * n, unit("merge", 3 * KT - 2 + n))
            first_pair("out2", Groups("out2"), 0, "merged")
            with pe.Fori(1, KT // 2 - 1) as i:
                g = Groups("out2", i, 2)
                for k in range(2):
                    projection("out2", g, k, k, HH, HL, i, 2)
            pe.wait_ge(x_back, 16)
            turn_tiles(Groups("x_back"), X)
            for k in range(2):
                projection("out2", Groups("out2_last"), k, KT - 2 + k, HH, HL)
            pe.wait_ge(n_sq, NORM_TILES0["post2"] + 1)
            for t in range(TT):
                m = pe.matmul(PO[:, 0, t:t + 1], SQ[:, 0, t * P:(t + 1) * P], ones[:, 0:1],
                              start=True, stop=True)
            m.then_inc(n_sq_used, 1)
            Groups("out2_last").wait_free(pe, 0)
            Groups("out2_last").wait_free(pe, 1)
            turn_tiles(Groups("y"), OUT2)

        @block.scalar
        def _(act):
            for semaphore in PRIMED["act"]:
                act.sem_inc(semaphore, 1)

            step = Steps(act, act_step)

            def square(src, k):
                act.activation(T[:, k % 2, :], src, ACT.Square).then_inc(sq_new, 1)

            def root(name, width):
                act.wait_ge(n_sq_used, NORM_TILES0[name] + dict(NORMS)[name])
                act.activation(RS[:, :], POf, ACT.Sqrt, bias=v("eps"), scale=1.0 / width)\
                   .then_inc(n_root, 1)

            def norm(name, src, width, after=None, also=lambda k: None):
                tiles, t0, n = dict(NORMS)[name], NORM_TILES0[name], NORM_INDEX[name]
                for k in range(tiles):
                    if after is not None:
                        act.wait_ge(n_done, NDONE0[after] + k + 1)
                    if t0 + k >= 2:
                        act.wait_ge(n_sq_used, t0 + k - 1)
                    act.activation(SQ[:, k % 2, :], src(k), ACT.Square).then_inc(n_sq, 1)
                    also(k)
                root(name, width)

            def out_tile(g, k, n, dst, scale=1.0):
                g.ready(act, k)
                primed(act, sq_sum, n - k % 2)
                act.activation(T[:, k % 2, :], g.psum(k), ACT.Square).then_inc(sq_new, 1)
                act.activation(dst, g.psum(k), ACT.Copy, scale=scale).then_inc(g.free(k), 1)

            def split(name, hi):
                t0 = SPLIT0[name]
                for k in range(dict(SPLITS)[name]):
                    act.wait_ge(s_raw, t0 + k + 1)
                    raw = T[:, (t0 + k) % 2, :] if name in ("mix_pre", "ffn_pre", "pre2") else \
                        RAW[:, k + (2 if name == "kv" else 0), :]
                    act.activation(hi[:, k, :], raw, ACT.Copy).then_inc(s_hi, 1)

            act.wait_ge(consts_ready, 1)
            g = Groups("x")
            for t in range(TT):
                act.wait_ge(x_loaded[t], 16)
                if t >= 2:
                    act.wait_ge(x_squared, t - 1)
                act.activation(T[:, t % 2, :], RAW[:, t, :], ACT.Square,
                               accum_out=cols[:, t:t + 1]).then_inc(x_squared, 1)
                if t % 2 == 0:
                    g.ready(act, t)
                    act.activation(X[:, :, t * P:(t + 1) * P],
                                   g.psum(t).rearrange("p (k n) -> p k n", k=KT),
                                   ACT.Copy).then_inc(g.free(t), 1)
            act.wait_ge(x_squared, TT)
            g.wait_free(act, TT - 2)
            g.wait_free(act, TT - 1)
            act.dma_start(POSI[:, :], pos.to_broadcast([P, S])).then_inc(pos_in, 16)
            root("mix_pre", D)
            split("mix_pre", HH)

            def log1p_rows(base, rows, n_dve):
                act.wait_ge(rows_dve, n_dve + 1)
                act.activation(rows[:, 1, :], rows[:, 1, :], ACT.Exp, scale=-1.0).then_inc(rows_act, 1)
                act.wait_ge(rows_dve, n_dve + 2)
                act.activation(rows[:, 3, :], rows[:, 2, :], ACT.Ln).then_inc(rows_act, 1)

            act.wait_ge(tab_r, 1)
            act.activation(TABR, KK[:, :], ACT.Sin).then_inc(tab_sin, 1)
            g = Groups("in")
            for k in range(4):
                g.ready(act, k)
                act.activation(RAW[:, k, :], g.psum(k), ACT.Copy).then_inc(g.free(k), 1)
            norm("q", lambda k: RAW[:, k, :], 256)
            act.wait_ge(n_done, NDONE["q"])
            norm("kv", lambda k: RAW[:, 2, :], 128)
            for j in range(2):
                k = 4 + 3 * j
                if j:
                    act.activation(cols[0:4, 0:1], vec[0:4, VEC0["a_log"]:VEC0["a_log"] + 1], ACT.Exp)\
                       .then_inc(rows_act, 1)
                    log1p_rows(0, ROWS, 0)
                g.ready(act, k)
                if j:
                    act.wait_ge(in_dve, 3)
                else:
                    act.wait_ge(s_lo, 8)
                act.activation(T[:, 0, :], g.psum(k), ACT.Copy).then_inc(g.free(k), 1)
                g.wait_free(act, k + 1)
                act.activation(SQ[:, 0, :], T[:, 1, :], ACT.Copy, scale=v("sc_conv", 3 * j + 2))\
                   .then_inc(in_act, 1)
            for j in range(2):
                g.ready(act, 10 + j)
                act.activation(ZS[:, j, :], g.psum(10 + j), ACT.Silu).then_inc(g.free(10 + j), 1)
            for j in range(6):
                k = 12 + j
                g.ready(act, k)
                act.activation(XBC[:, j, :], g.psum(k), ACT.Identity, bias=v("ssd_conv", 5 * j + 4),
                               scale=v("ssd_conv", 5 * j + 3)).then_inc(in_act, 1)
                g.wait_free(act, k)
                act.activation(XBC[:, j, :], XBC[:, j, :], ACT.Silu).then_inc(xbc_ready, 1)

            act.wait_ge(tab_done, 1)
            g = Groups("in")
            g.ready(act, 17)
            act.activation(TAB[:, :], TABR, ACT.Copy).then_inc(tab_done, 1)
            g = Groups("krot")
            g.ready(act, 0)
            act.activation(KR[64:128, :], g.psum(0)[64:128, :], ACT.Copy)\
               .then_inc(g.free(0), 1)

            for grp in range(2):
                g = Groups("ssd", first=11 * grp)
                for hh in range(2):
                    g.ready(act, 1 + hh)
                    act.activation(AB[:, hh, :], g.psum(1 + hh), ACT.Copy).then_inc(g.free(1 + hh), 1)
                for j in range(TT):
                    for hh in range(2):
                        n, c = 16 * grp + 2 * j + hh, 2 * grp + hh
                        if j == 0:
                            act.wait_ge(dd_ready, c + 1)
                            g.wait_free(act, 1 + hh)
                        if n >= 4:
                            act.wait_ge(pp_ready, n - 3)
                        m = act.activation(DD[j % 2][:, hh, j * P:(j + 1) * P],
                                           EX[:, hh, j * P:(j + 1) * P], ACT.Exp)
                        if j < TT - 1:
                            m = act.activation(DD[j % 2][:, hh, (j + 1) * P:], AB[:, hh, (j + 1) * P:],
                                               ACT.Exp, bias=NAC[:, j, c:c + 1])
                        m.then_inc(e_ready, 1)
            act.wait_ge(ssd_y, 2)
            for k in range(2):
                act.activation(SQ[:, k, :], YS[:, k, :], ACT.Square).then_inc(n_sq, 1)
            split("q", QNH)
            split("kv", KNH)
            root("ssd", 256)

            for hh in range(2):
                m = act.activation(KOP[64:128, hh, :], KR[64:128, :], ACT.Copy)
            m.then_inc(krot_done, 1)
            with act.Fori(0, MLA_HEADS // 2) as i:
                g = Groups("mla", i, 22)
                for hh in range(2):
                    g.ready(act, 2 * hh + 1)
                    act.activation(KV[:, hh, :], g.psum(2 * hh + 1), ACT.Copy).then_inc(kv_cp, 1)
                    act.activation(KOP[0:64, hh, :], g.psum(2 * hh + 1)[0:64, :], ACT.Copy)\
                       .then_inc(k_op, 1)
                    act.wait_ge(k_op, 2 * i + (hh + 1))
                    act.sem_inc(g.free(2 * hh + 1), 1)

                def exp(t, hh):
                    act.wait_ge(m_neg, i * (2 * TT) + (2 * t + hh + 1))
                    act.activation(PR[t % 2][:, hh, 0:(t + 1) * P], g.psum(6 + 2 * t + hh)[:, 0:(t + 1) * P],
                                   ACT.Exp, bias=cols[:, 2 + hh:3 + hh],
                                   accum_out=cols[:, 4 + hh:5 + hh]).then_inc(m_exp, 1)
                    act.wait_ge(m_exp, i * (2 * TT) + (2 * t + hh + 1))
                    act.sem_inc(g.free(6 + 2 * t + hh), 1)

                def evacuate_pair(t, hh):
                    for q in range(t // 4 + 1):
                        n = mla_bank(t, hh, q)
                        act.wait_ge(t_ready, i * 24 + (n + 1))
                        if t % 4 == 0 and q == 0:
                            primed(act, pv_half, i * 4 + (1 + hh if t else 0))
                        m = min(4, t + 1 - 4 * q)
                        act.activation(PTB[:, hh, 4 * q:4 * q + m, (t % 4) * P:(t % 4 + 1) * P],
                                       PT[:, n % 2, 0:m * P].rearrange("p (b n) -> p b n", b=m),
                                       ACT.Copy).then_inc(t_free, 1)

                exp(0, 0)
                exp(0, 1)
                for t in range(TT):
                    if t + 1 < TT:
                        exp(t + 1, 0)
                        exp(t + 1, 1)
                    evacuate_pair(t, 0)
                    evacuate_pair(t, 1)
                primed(act, pv_half, 4 * i + 4)
                act.activation(RAW[:, bass.ds(i, 1), :], POf, ACT.Copy).then_inc(att_free, 1)

            split("mix", HH)
            with act.Fori(0, KT // 2) as i:
                for k in range(2):
                    out_tile(Groups("out", i, 2), k, 2 * i + k, RAW[:, bass.ds(2 * i + k, 1), :])
            root("mix_post", D)
            norm("ffn_pre", lambda k: X[:, k, :], D, "mix_post")
            split("ffn_pre", HH)

            def ffn_vec(part, tap, j, x):
                c = VEC0["ffn_conv"] + 8 * x + 4 * part + tap
                if isinstance(j, int):
                    return vec[:, c + 16 * j:c + 16 * j + 1]
                return vec[:, bass.ds(16 * j + c, 1)]

            def tile(g, k, pair, x):
                tile_no = 2 * pair + x
                for part, buf in ((0, VG), (1, VU)):
                    g.ready(act, k + part)
                    if not (isinstance(tile_no, int) and tile_no == 0):
                        act.wait_ge(f_prod, tile_no)
                    act.activation(buf[:, :], g.psum(k + part), ACT.Identity,
                                   bias=ffn_vec(part, 3, pair, x),
                                   scale=ffn_vec(part, 2, pair, x)).then_inc(f_act, 1)
                    if part == 0:
                        g.wait_free(act, k)
                        act.activation(SG[:, :], VG[:, :], ACT.Silu).then_inc(f_silu, 1)

            def hi(pair, x, downs):
                tile_no = 2 * pair + x
                act.wait_ge(f_prod, tile_no + 1)
                if downs is not None:
                    downs()
                act.activation(GH[:, x, :], PRD[:, :], ACT.Copy).then_inc(f_hi, 1)

            g = Groups("ffn_first")
            tile(g, 0, 0, 0)
            hi(0, 0, None)
            tile(g, 2, 0, 1)
            hi(0, 1, None)
            with act.Fori(1, FFN_PAIRS) as i:
                g = Groups("ffn", i, 12, first=-12)
                tile(g, 0, i, 0)
                hi(i, 0, lambda: g.ready(act, 9))
                tile(g, 10, i, 1)
                hi(i, 1, None)
            g = Groups("ffn_last")
            for k in range(KT):
                g.wait_free(act, k)
                primed(act, sq_sum, KT + max(k - 1, 0))
                square(RAW[:, k, :], k)
            act.dma_start(lam_sb[:, :], lam_in.to_broadcast([P, 4 * 64])).then_inc(lam_loaded, 16)
            root("ffn_post", D)
            def spill_tile(k):
                if k % 2:
                    cut = slice((k - 1) * S, (k + 1) * S)
                    act.dma_start(spill[:, cut], X[:, k - 1:k + 1, :].rearrange("p k n -> p (k n)"))\
                       .then_inc(spilled, 16)

            norm("pre2", lambda k: X[:, k, :], D, "ffn_post", spill_tile)
            split("pre2", HH)

            g = Groups("diff")
            g.ready(act, 0)
            gb = VEC0["gate_bias"]
            act.activation(GROWS[:, 5, :], g.psum(0)[0:4, :], ACT.Identity, bias=vec[0:4, gb:gb + 1])
            act.activation(GROWS[:, 0, :], g.psum(0)[32:36, :], ACT.Identity,
                           bias=vec[32:36, gb:gb + 1]).then_inc(g.free(0), 1)
            g.ready(act, 1)
            act.activation(NQ[:, :], g.psum(1), ACT.Copy, scale=0.125).then_inc(g.free(1), 1)
            act.wait_ge(lam_prod, 1)
            act.activation(cols[:, 8:10], cols[:, 8:10], ACT.Exp).then_inc(lam_exp, 1)
            log1p_rows(1, GROWS, 2)
            g.ready(act, 2)
            act.activation(NK[:, :], g.psum(2), ACT.Copy).then_inc(g.free(2), 1)
            g.ready(act, 3)
            act.activation(DVT0, g.psum(3), ACT.Copy).then_inc(d_v, 1)
            act.wait_ge(d_v, 1)
            act.sem_inc(g.free(3), 1)
            g.ready(act, 4)
            act.activation(RAW[:, 4, :], g.psum(4), ACT.Silu).then_inc(g.free(4), 1)
            act.wait_ge(spilled, 16 * KT // 2)
            act.wait_ge(aug_k, 1)
            for rows, c in ((slice(64, 66), 0), (slice(0, 2), 1)):
                act.dma_start(DQ[rows, c, :], aug_in[0]).then_inc(aug_loaded, 16)
                act.dma_start(DK[rows, c, :], aug_in[1]).then_inc(aug_loaded, 16)
            g.wait_free(act, 1)
            g.wait_free(act, 2)
            for buf, src, done in ((DQ, NQ, d_q), (DK, NK, d_k)):
                act.activation(buf[0:64, 0, :], src[0:64, :], ACT.Copy)
                act.activation(buf[64:128, 1, :], src[64:128, :], ACT.Copy).then_inc(done, 1)

            def diff_head(i, last=False):
                hb = Halves("diff", i, DIFF_HALVES)

                def exp(t, c):
                    act.wait_ge(d_neg, i * diff_neg(TT - 1, 1) + diff_neg(t, c))
                    act.activation(DP[:, t % 2, c, 0:(t + 1) * P], diff_scores(t, c), ACT.Exp,
                                   bias=cols[:, 4 + 2 * (t % 2) + c:5 + 2 * (t % 2) + c],
                                   accum_out=cols[:, 10 + 2 * (t % 2) + c:11 + 2 * (t % 2) + c])\
                       .then_inc(d_exp, 1)

                def transposed(t):
                    for q in range(t // 4 + 1):
                        n = t if t < 4 else 4 + 2 * (t - 4) + q
                        act.wait_ge(d_tready, i * 12 + (n + 1))
                        if t == 4 and q == 0:
                            primed(act, d_half, i * 2 + 1)
                        if t == 0:
                            primed(act, d_half, i * 2)
                        m = min(4, t + 1 - 4 * q)
                        act.activation(DPT[:, 4 * q:4 * q + m, (t % 4) * P:(t % 4 + 1) * P],
                                       PT[:, n % 2, 0:m * P].rearrange("p (b n) -> p b n", b=m),
                                       ACT.Copy).then_inc(d_tfree, 1)

                def next_half(m):
                    hb.ready(act, m)
                    if m < 4:
                        out, fn = NK[:, halves(m)], ACT.Copy
                    elif m < 6:
                        out, fn = DVT[:, halves(m)], ACT.Copy
                    else:
                        out, fn = RAW[:, 4 if last else bass.ds(i + 5, 1), halves(m)], ACT.Silu
                    act.activation(out, hb.bank(m), fn).then_inc(hb.free(m), 1)
                    if m == 5:
                        hb.wait_free(act, 4)
                        hb.wait_free(act, 5)
                        act.sem_inc(m_v if last else d_v, 1)

                for t in range(TT):
                    exp(t, 0)
                    exp(t, 1)
                    if t >= 4:
                        next_half(t - 2)
                    if t:
                        transposed(t - 1)
                if not last:
                    act.wait_ge(d_scores, i * (2 * TT) + 2 * TT)
                    act.activation(DK[0:64, 0, :], NK[0:64, :], ACT.Copy)
                    act.activation(DK[64:128, 1, :], NK[64:128, :], ACT.Copy).then_inc(d_k, 1)
                next_half(6)
                transposed(TT - 1)
                next_half(7)
                primed(act, d_half, 2 * i + 2)
                act.activation(SQ[:, 0, :], POf, ACT.Square).then_inc(d_sq, 1)
                act.wait_ge(d_sq, i + 1)
                primed(act, d_y, i)
                act.activation(DO[:, :], POf, ACT.Copy).then_inc(d_o, 1)
                for m in (8, 9) if last else (10, 11):
                    hb.ready(act, m)
                    act.activation(RS[:, halves(m)], hb.bank(m), ACT.Sqrt, bias=v("eps"),
                                   scale=1.0 / P).then_inc(d_root, 1)
                    act.wait_ge(d_root, i * 2 + (m % 2 + 1))
                    act.sem_inc(hb.free(m), 1)

            with act.Fori(0, DIFF_HEADS - 1) as i:
                diff_head(i)
            diff_head(DIFF_HEADS - 1, True)

            def conv_column(head, part, tap):
                c = VEC0["ml_conv"] + 4 * part + tap
                if isinstance(head, int):
                    return vec[:, c + 8 * head:c + 8 * head + 1]
                return vec[:, bass.ds(8 * head + c, 1)]

            def convolved(head):
                for n, buf in ((0, MQ), (1, MK)):
                    act.wait_ge(m_taps, 2 * head + (n + 1))
                    act.activation(buf[:, :], MC[n][:, :], ACT.Silu).then_inc(m_q, 1)

            def gate_rows_spread(hb, m0, head):
                for n, (buf, fn, done) in enumerate(((MN, ACT.Copy, m_mn), (ME, ACT.Exp, m_me))):
                    for m in (m0 + 2 * n, m0 + 2 * n + 1):
                        hb.ready(act, m)
                        act.activation(buf[:, halves(m)], hb.bank(m), fn).then_inc(done, 1)
                        act.wait_ge(done, 2 * head + (m % 2 + 1))
                        act.sem_inc(hb.free(m), 1)

            for n in range(2):
                for b in (0, 1) if n == 0 else (2, 3):
                    hb = Halves("diff", DIFF_HEADS - 1, DIFF_HALVES)
                    hb.wait_free(act, b)
                act.activation(MC[n][:, :], MR[n][:, :], ACT.Copy, scale=conv_column(0, n, 3))\
                   .then_inc(m_conv, 1)
            hb = Halves("mlstm_first")
            for m in range(2):
                hb.ready(act, m)
                act.activation(MO[:, halves(m)], hb.bank(m), ACT.Sigmoid).then_inc(hb.free(m), 1)
            hb.wait_free(act, 0)
            hb.wait_free(act, 1)
            act.sem_inc(m_o, 1)
            convolved(0)
            gate_rows_spread(hb, 4, 0)

            def mlstm_head(i, last=False):
                hb = Halves("mlstm", i, ML_HALVES)

                def next_half(m):
                    hb.ready(act, m)
                    cut, src = halves(m), hb.bank(m)
                    if m < 4:
                        n = m // 2
                        act.activation(MR[n][:, cut], src, ACT.Copy)
                        act.activation(MC[n][:, cut], src, ACT.Copy, scale=conv_column(i + 1, n, 3))\
                           .then_inc(hb.free(m), 1)
                        if m % 2:
                            hb.wait_free(act, m - 1)
                            hb.wait_free(act, m)
                            act.sem_inc(m_conv, 1)
                        return
                    if m < 6:
                        out, fn = MVT[:, cut], ACT.Copy
                    else:
                        out, fn = RAW[:, bass.ds(i + 5, 1), cut], ACT.Silu
                    act.activation(out, src, fn).then_inc(hb.free(m), 1)
                    if m == 5:
                        hb.wait_free(act, m - 1)
                        hb.wait_free(act, m)
                        act.sem_inc(m_v, 1)

                def merge_gate(m):
                    hb.ready(act, m)
                    act.activation((MS, MS2)[m // 2][0][:, halves(m)], hb.bank(m), ACT.Sigmoid)\
                       .then_inc(hb.free(m), 1)
                    if m % 2:
                        hb.wait_free(act, m - 1)
                        hb.wait_free(act, m)
                        act.sem_inc(g_sig, 1)

                for j in range(TT):
                    if j == 0:
                        act.wait_ge(m_dd, i + 1)
                    primed(act, m_pp, i * TT + max(j - 1, 0))
                    m = act.activation(MD[:, j % 2, j * P:(j + 1) * P], MX[:, j * P:(j + 1) * P],
                                       ACT.Exp)
                    if j < TT - 1:
                        acol = ACOL[:, j, i:i + 1] if last else ACOL[:, j, bass.ds(i, 1)]
                        m = act.activation(MD[:, j % 2, (j + 1) * P:], MN[:, (j + 1) * P:], ACT.Exp,
                                           bias=acol)
                    m.then_inc(m_e, 1)
                    if last and j == 6:
                        merge_gate(0)
                    if not last and j in (2, 4, 5, 6, 7):
                        for m in {2: (0,), 4: (1,), 5: (2,), 6: (3,), 7: (4,)}[j]:
                            next_half(m)
                if last:
                    merge_gate(1)
                else:
                    act.wait_ge(m_scores, i * TT + TT)
                    next_half(5)
                    convolved(i + 1)
                    next_half(6)
                primed(act, m_used, i * TT + TT)
                act.activation(MR[0][:, :], PTf, ACT.Abs).then_inc(m_abs, 1)
                if last:
                    merge_gate(2)
                else:
                    next_half(7)
                    for m in (8, 9):
                        hb.ready(act, m)
                        act.activation(MV[:, 4 * (m % 2):4 * (m % 2) + 4, :],
                                       hb.bank(m).rearrange("p (t n) -> p t n", t=4), ACT.Copy)\
                           .then_inc(hb.free(m), 1)
                    hb.wait_free(act, 8)
                    hb.wait_free(act, 9)
                    act.sem_inc(m_vop, 1)
                primed(act, m_h, i + 1)
                act.activation(SQ[:, 0, :], MH[:, :], ACT.Square).then_inc(m_sq, 1)
                if last:
                    merge_gate(3)
                else:
                    gate_rows_spread(hb, 10, i + 1)
                primed(act, m_y, i)
                for m in (4, 5) if last else (14, 15):
                    hb.ready(act, m)
                    act.activation(RS[:, halves(m)], hb.bank(m), ACT.Sqrt, bias=v("eps"),
                                   scale=1.0 / P).then_inc(m_root, 1)
                    act.wait_ge(m_root, 2 * i + (m % 2 + 1))
                    act.sem_inc(hb.free(m), 1)
                if not last:
                    for m in (16, 17):
                        hb.ready(act, m)
                        act.activation(MO[:, halves(m)], hb.bank(m), ACT.Sigmoid).then_inc(hb.free(m), 1)
                    hb.wait_free(act, 16)
                    hb.wait_free(act, 17)
                    act.sem_inc(m_o, 1)

            with act.Fori(0, ML_HEADS - 1) as i:
                mlstm_head(i)
            mlstm_head(ML_HEADS - 1, True)

            def merge_gates(g, k, n, done):
                for x, buf in enumerate((MS, MS2)):
                    g.ready(act, k + x)
                    act.activation(buf[n % 2][:, :], g.psum(k + x), ACT.Sigmoid).then_inc(g_sig, 1)
                    act.wait_ge(g_sig, done + x + 1)
                    act.sem_inc(g.free(k + x), 1)

            primed(act, m_y, ML_HEADS)
            split("y", YH)
            merge_gates(Groups("merge_first"), 0, 1, 2)
            with act.Fori(0, KT // 2 - 1) as i:
                g = Groups("merge", i, 8)
                for n in range(2):
                    primed(act, g_done, 2 * i + (n + 1))
                    merge_gates(g, 4 * n + 2, n, 4 * i + (4 + 2 * n))
            split("merged", HH)
            act.wait_ge(spilled, 16 * KT // 2)
            act.wait_ge(g_ready, GROUP0["out2"])
            act.dma_start(X[:, :, :].rearrange("p k n -> p (k n)"), spill).then_inc(x_back, 16)
            with act.Fori(0, KT // 2 - 1) as i:
                for k in range(2):
                    c = VEC0["norm_post_2"] + k
                    out_tile(Groups("out2", i, 2), k, 2 * i + (2 * KT + k),
                             OUT2[:, bass.ds(2 * i + k, 1), :], vec[:, bass.ds(2 * i + c, 1)])
            g = Groups("x_back")
            for t in range(0, TT, 2):
                g.ready(act, t)
                act.activation(XT[:, t, :], g.psum(t), ACT.Copy).then_inc(g.free(t), 1)
            for k in range(2):
                out_tile(Groups("out2_last"), k, 3 * KT - 2 + k, OUT2[:, KT - 2 + k, :],
                         v("norm_post_2", KT - 2 + k))
            act.wait_ge(n_sq_used, NORM_TILES0["post2"] + 1)
            act.activation(cols[:, 0:TT], PO[:, 0, 0:TT], ACT.Sqrt, bias=v("eps"), scale=1.0 / D)\
               .then_inc(n_root, 1)
            g = Groups("y")
            for t in range(TT):
                g.wait_free(act, t)
                act.dma_start(y_out[t * P:(t + 1) * P, :], XT[:, t, :]).then_inc(y_stored, 16)
            act.wait_ge(y_stored, 16 * TT)

        @block.vector
        def _(dve):
            for semaphore in PRIMED["dve"]:
                dve.sem_inc(semaphore, 1)

            step = Steps(dve, dve_step)

            def reciprocal_root(name):
                dve.wait_ge(n_root, NORM_INDEX[name] + 1)
                step(dve.reciprocal(RS[:, :], RS[:, :]))

            def norm_split(name, vname, src, lo):
                reciprocal_root(name)
                split(name, lambda k, out: dve.scalar_tensor_tensor(
                    out, src(k), v(vname, k), RS[:, :], ALU.mult, ALU.mult), lo)

            def split(name, make, lo):
                t0, n = SPLIT0[name], dict(SPLITS)[name]

                def low(k):
                    dve.wait_ge(s_hi, t0 + k + 1)
                    raw = T[:, (t0 + k) % 2, :] if make is not None else \
                        RAW[:, k + (2 if name == "kv" else 0), :]
                    dve.tensor_tensor(lo[:, k, :], raw, HI[name][:, k, :].bitcast(F32),
                                      ALU.subtract).then_inc(s_lo, 1)

                if make is None:
                    for k in range(n):
                        dve.sem_inc(s_raw, 1)
                    for k in range(n):
                        low(k)
                    return
                for k in range(n):
                    if t0 + k >= 2:
                        dve.wait_ge(s_lo, t0 + k - 1)
                    make(k, T[:, (t0 + k) % 2, :]).then_inc(s_raw, 1)
                    if k:
                        low(k - 1)
                low(n - 1)

            HI = {"mix_pre": HH, "q": QNH, "kv": KNH, "mix": HH, "ffn_pre": HH, "pre2": HH,
                  "y": YH, "merged": HH}

            def norm_residual(name, vname, src):
                reciprocal_root(name)
                for k in range(KT):
                    if k >= 2:
                        dve.wait_ge(n_done, NDONE0[name] + k - 1)
                    step(dve.scalar_tensor_tensor(T[:, k % 2, :], src(k), v(vname, k), RS[:, :],
                                                  ALU.mult, ALU.mult))
                    dve.tensor_tensor(X[:, k, :], X[:, k, :], T[:, k % 2, :], ALU.add)\
                       .then_inc(n_done, 1)
                dve.wait_ge(n_done, NDONE[name])

            def zero_sum():
                step(dve.memset(SQ[:, 0, :], 0.0))

            def add_square(n, k):
                dve.wait_ge(sq_new, n + 1)
                primed(dve, sq_sum, n)
                dve.tensor_tensor(SQ[:, 0, :], SQ[:, 0, :], T[:, k, :], ALU.add).then_inc(sq_sum, 1)

            def end_sum(post):
                primed(dve, sq_sum, KT * (POST_NORMS.index(post) + 1))
                dve.sem_inc(n_sq, 1)

            def sum_squares(pairs, n0):
                with dve.Fori(0, pairs) as i:
                    for k in range(2):
                        add_square(2 * i + (n0 + k), k)

            def taps(g, k, out, weights, then):
                for d, w in enumerate(weights, 1):
                    ins = dve.scalar_tensor_tensor(out[:, d:], g.psum(k)[:, 0:S - d], w, out[:, d:],
                                                   ALU.mult, ALU.add)
                    if d < len(weights):
                        step(ins)
                    else:
                        ins.then_inc(g.free(k), 1)

            dve.wait_ge(const_in, 48)
            step(dve.tensor_copy(identb[:, :], ident))
            dve.tensor_copy(aheadb[:, :], aheadf[:, :]).then_inc(consts_ready, 1)
            dve.wait_ge(consts_ready, 1)

            g = Groups("x")
            for t in range(1, TT, 2):
                g.ready(dve, t)
                dve.tensor_copy(X[:, :, t * P:(t + 1) * P],
                                g.psum(t).rearrange("p (k n) -> p k n", k=KT)).then_inc(g.free(t), 1)
            dve.wait_ge(x_squared, TT)
            dve.tensor_tensor(SQ[:, 0, :].rearrange("p (t n) -> p t n", t=TT),
                              ident.rearrange("p (a n) -> p a n", a=1).to_broadcast([P, TT, P]),
                              cols[:, 0:TT].rearrange("p (t a) -> p t a", a=1).to_broadcast([P, TT, P]),
                              ALU.mult).then_inc(n_sq, 1)
            g.wait_free(dve, TT - 2)
            g.wait_free(dve, TT - 1)
            norm_split("mix_pre", "norm_mix_pre", lambda k: X[:, k, :], HL)

            def softplus(rows, raw, bias, n_act):
                x0, y, u, l, s = (rows[:, n, :] for n in range(5))
                if raw is not None:
                    step(dve.tensor_scalar(x0, raw, bias, None, ALU.add))
                dve.scalar_tensor_tensor(y, x0, -1.0, x0, ALU.mult, ALU.max).then_inc(rows_dve, 1)
                dve.wait_ge(rows_act, n_act + 1)
                dve.tensor_scalar(u, y, 1.0, None, ALU.add).then_inc(rows_dve, 1)
                step(dve.tensor_scalar(s, y, -0.25, 1.0 / 3.0, ALU.mult, ALU.add))
                step(dve.tensor_tensor(s, s, y, ALU.mult))
                step(dve.tensor_scalar(s, s, -0.5, None, ALU.add))
                step(dve.tensor_tensor(s, s, y, ALU.mult))
                step(dve.tensor_scalar(s, s, 1.0, None, ALU.add))
                step(dve.tensor_tensor(s, s, y, ALU.mult))
                dve.wait_ge(rows_act, n_act + 2)
                step(dve.tensor_tensor(s, s, l, ALU.subtract))
                step(dve.tensor_scalar(u, y, 1.0 / 64, None, ALU.is_lt))
                step(dve.tensor_tensor(s, s, u, ALU.mult))
                step(dve.tensor_tensor(l, l, s, ALU.add))
                step(dve.scalar_tensor_tensor(x0, x0, 0.0, l, ALU.max, ALU.add))

            dve.wait_ge(pos_in, 16)
            step(dve.tensor_copy(KK[:, :], POSI[:, :]))
            step(dve.tensor_scalar(ANG[:, :], KK[:, :], v("inv_freq"), None, ALU.mult))
            step(dve.tensor_scalar(KK[:, :], ANG[:, :], 1.0 / (2 * np.pi), v("turn"), ALU.mult, ALU.add))
            step(dve.tensor_scalar(KK[:, :], KK[:, :], 12582912.0, None, ALU.add))
            step(dve.tensor_scalar(KK[:, :], KK[:, :], 12582912.0, None, ALU.subtract))
            c1, c2 = 6.25, 0.033203125
            for c in (c1, c2, 2 * np.pi - c1 - c2):
                step(dve.scalar_tensor_tensor(ANG[:, :], KK[:, :], -float(c), ANG[:, :],
                                              ALU.mult, ALU.add))
            step(dve.tensor_scalar(KK[:, :], ANG[:, :], v("phase"), None, ALU.add))
            dve.tensor_scalar(KK[:, :], KK[:, :], 3.1415925, -3.1415925, ALU.min, ALU.max)\
               .then_inc(tab_r, 1)
            dve.wait_ge(tab_sin, 1)
            step(dve.tensor_scalar(TABR, TABR, v("sign"), None, ALU.mult))
            step(dve.memset(RAW[0:64, 6, :], 1.0))
            dve.sem_inc(tab_done, 1)

            for name, tiles, vname in (("q", (0, 1), "mla_q_norm"), ("kv", (2,), "mla_kv_norm")):
                reciprocal_root(name)
                for n, k in enumerate(tiles):
                    dve.scalar_tensor_tensor(RAW[:, k, :], RAW[:, k, :], v(vname, n), RS[:, :],
                                             ALU.mult, ALU.mult).then_inc(n_done, 1)
                dve.wait_ge(n_done, NDONE[name])

            def time_rows():
                g = Groups("in")
                g.wait_free(dve, 3)
                db = VEC0["dt_bias"]
                softplus(ROWS, RAW[0:4, 3, :], vec[0:4, db:db + 1], 1)
                step(dve.tensor_copy(DR[0:4, :], ROWS[:, 0, :]))
                dve.wait_ge(rows_act, 1)
                step(dve.tensor_scalar(ROWS[:, 1, :], ROWS[:, 0, :], cols[0:4, 0:1], -1.0, ALU.mult, ALU.mult))
                step(dve.memset(ROWS[:, 2, :], 1.0))
                dve.tensor_tensor_scan(DR[32:36, :], ROWS[:, 2, :], ROWS[:, 1, :], 0.0, ALU.mult, ALU.add)\
                   .then_inc(ssd_rows, 1)
                dve.tensor_tensor(DR[64:128, :], DR[64:128, :], RAW[64:128, 6, :], ALU.mult)\
                   .then_inc(krot_t, 1)

            g = Groups("in")
            for j in range(2):
                k = 4 + 3 * j
                if j:
                    time_rows()
                g.wait_free(dve, k)
                g.ready(dve, k + 1)
                dve.tensor_tensor(T[:, 1, :], g.psum(k + 1), T[:, 0, :], ALU.mult)\
                   .then_inc(g.free(k + 1), 1)
                dve.wait_ge(in_act, 1 if j == 0 else 2)
                g.wait_free(dve, k + 1)
                for d in (1, 2):
                    if d == 2:
                        dve.wait_ge(in_dve, 3 * j + 1)
                    dve.scalar_tensor_tensor(SQ[:, 0, d:], T[:, 1, 0:S - d], v("sc_conv", 3 * j + 2 - d),
                                             SQ[:, 0, d:], ALU.mult, ALU.add).then_inc(in_dve, 1)
                dve.wait_ge(in_dve, 3 * j + 2)
                g.ready(dve, k + 2)
                dve.tensor_tensor(RAW[:, 4 + j, :], g.psum(k + 2), SQ[:, 0, :], ALU.mult)\
                   .then_inc(g.free(k + 2), 1)
                g.wait_free(dve, k + 2)
                dve.sem_inc(in_dve, 1)
            for j in range(6):
                k = 12 + j
                dve.wait_ge(in_act, 2 + j + 1)
                g.ready(dve, k)
                taps(g, k, XBC[:, j, :], [v("ssd_conv", 5 * j + 3 - d) for d in (1, 2, 3)], None)

            g = Groups("cols")
            g.ready(dve, 0)
            turned = g.psum(0).rearrange("p (t n) -> p t n", t=TT)
            step(dve.tensor_copy(DTC[:, :, :], turned[:, :, 0:4]))
            dve.tensor_scalar(NAC[:, :, :], turned[:, :, 32:36], -1.0, None, ALU.mult)\
               .then_inc(g.free(0), 1)
            g.wait_free(dve, 0)

            below_blocks = below.rearrange("p (a n) -> p a n", a=1).to_broadcast([P, TT, P])
            dve.wait_ge(xbc_ready, 6)
            step(dve.memset(XD[:, :, :, :].rearrange("p a b c -> p (a b c)"), 0.0))
            for grp in range(2):
                g = Groups("ssd", first=11 * grp)
                g.ready(dve, 0)
                if grp:
                    dve.wait_ge(pv_used, 16)
                xt = g.psum(0).rearrange("p (t n) -> p t n", t=TT)
                for hh in range(2):
                    c = 2 * grp + hh
                    ins = dve.tensor_tensor(XD[:, :, hh, hh * 64:(hh + 1) * 64],
                                            xt[:, :, hh * 64:(hh + 1) * 64],
                                            DTC[:, :, c:c + 1].to_broadcast([P, TT, 64]), ALU.mult)
                    if hh == 0:
                        step(ins)
                    else:
                        ins.then_inc(ssd_x, 1)
                dve.wait_ge(ssd_x, grp + 1)
                dve.sem_inc(g.free(0), 1)
                for hh in range(2):
                    c = 2 * grp + hh
                    if c:
                        prev = Groups("ssd", first=11 * ((c - 1) // 2))
                        prev.ready(dve, 1 + (c - 1) % 2)
                    dve.tensor_copy(selA[:, :], ident[:, 32 + c:33 + c].to_broadcast([P, P]))\
                       .then_inc(sel_set, 1)

                for hh in range(2):
                    c = 2 * grp + hh
                    g.wait_free(dve, 1 + hh)
                    blocks = [x[:, hh, :].rearrange("p (t n) -> p t n", t=TT) for x in (EX, AB)]
                    step(dve.tensor_tensor(blocks[0], blocks[1],
                                           NAC[:, :, c:c + 1].to_broadcast([P, TT, P]), ALU.add))
                    dve.scalar_tensor_tensor(blocks[0], blocks[0], 0.0, below_blocks, ALU.min, ALU.add)\
                       .then_inc(dd_ready, 1)

                def decayed(j):
                    g.ready(dve, 3 + j)
                    for hh in range(2):
                        n = 16 * grp + 2 * j + hh
                        dve.wait_ge(e_ready, n + 1)
                        if n >= 2:
                            dve.wait_ge(pv_used, n - 1)
                        dve.tensor_tensor(PP[:, hh, j * P:], g.psum(3 + j)[:, j * P:],
                                          DD[j % 2][:, hh, j * P:], ALU.mult).then_inc(pp_ready, 1)
                    dve.wait_ge(pp_ready, 16 * grp + 2 * j + 2)
                    dve.sem_inc(g.free(3 + j), 1)

                for j in range(TT):
                    decayed(j)
                dve.wait_ge(pv_used, 16 * grp + 16)
                dve.scalar_tensor_tensor(YS[:, grp, :], XBC[:, grp, :], v("ssd_d", grp), POf,
                                         ALU.mult, ALU.add).then_inc(ssd_acc, 1)
                dve.wait_ge(ssd_acc, grp + 1)
                dve.tensor_tensor(YS[:, grp, :], YS[:, grp, :], ZS[:, grp, :], ALU.mult)\
                   .then_inc(ssd_y, 1)
            split("q", None, QNL)
            split("kv", None, KNL)
            reciprocal_root("ssd")
            for k in range(2):
                dve.scalar_tensor_tensor(RAW[:, 6 + k, :], YS[:, k, :], v("ssd_norm", k), RS[:, :],
                                         ALU.mult, ALU.mult).then_inc(n_done, 1)
            dve.wait_ge(n_done, NDONE["ssd"])

            Groups("krot").wait_free(dve, 0)
            step(dve.memset(VP[:, :, :, :].rearrange("p a b c -> p (a b c)"), 0.0))
            dve.sem_inc(krot_done, 1)

            with step.loop(0, MLA_HEADS // 2, 2 * TT) as i:
                g = Groups("mla", i, 22)
                for hh in range(2):
                    g.ready(dve, 2 * hh)
                    dve.scalar_tensor_tensor(QOP[:, hh, :], g.psum(2 * hh), float(QK_DIM) ** -0.5,
                                             TAB[:, :], ALU.mult, ALU.mult).then_inc(q_op, 1)
                    dve.wait_ge(q_op, 2 * i + (hh + 1))
                    dve.sem_inc(g.free(2 * hh), 1)
                for hh in range(2):
                    g.ready(dve, 4 + hh)
                    dve.tensor_copy(VP[:, hh, :, hh * 64:(hh + 1) * 64],
                                    g.psum(4 + hh).rearrange("p (t n) -> p t n", t=TT)[:, :, 64:128])\
                       .then_inc(v_op, 1)
                    dve.wait_ge(v_op, 2 * i + (hh + 1))
                    dve.sem_inc(g.free(4 + hh), 1)

                def maximum(t, hh):
                    g.ready(dve, 6 + 2 * t + hh)
                    dve.reduce_max(cols[:, 2 + hh:3 + hh], g.psum(6 + 2 * t + hh)[:, 0:(t + 1) * P],
                                   AX.X, negate=True).then_inc(m_neg, 1)

                def normalise(t, hh):
                    n = (t + 1) * P
                    dve.wait_ge(m_exp, i * (2 * TT) + (2 * t + hh + 1))
                    step(dve.reciprocal(cols[:, 6 + hh:7 + hh], cols[:, 4 + hh:5 + hh]))
                    p = PR[t % 2][:, hh, 0:n]
                    dve.tensor_scalar(p, p, cols[:, 6 + hh:7 + hh], None,
                                      ALU.mult).then_inc(m_prob, 1)

                maximum(0, 0)
                maximum(0, 1)
                for t in range(TT):
                    for hh in range(2):
                        normalise(t, hh)
                        if t + 1 < TT:
                            maximum(t + 1, hh)
            primed(dve, att_free, MLA_HEADS // 2)
            split("mix", None, HL)
            zero_sum()
            sum_squares(KT // 2, 0)
            end_sum("mix_post")
            norm_residual("mix_post", "norm_mix_post", lambda k: RAW[:, k, :])
            step(dve.memset(RAW[:, :, :].rearrange("p k n -> p (k n)"), 0.0))
            norm_split("ffn_pre", "norm_ffn_pre", lambda k: X[:, k, :], HL)

            def ffn_vec(part, tap, j, x):
                c = VEC0["ffn_conv"] + 8 * x + 4 * part + tap
                if isinstance(j, int):
                    return vec[:, c + 16 * j:c + 16 * j + 1]
                return vec[:, bass.ds(16 * j + c, 1)]

            def tile(g, k, pair, x):
                tile_no = 2 * pair + x
                for part, buf in ((0, VG), (1, VU)):
                    dve.wait_ge(f_act, 2 * tile_no + (part + 1))
                    g.ready(dve, k + part)
                    taps(g, k + part, buf, [ffn_vec(part, 2 - d, pair, x) for d in (1, 2)], None)
                g.wait_free(dve, k + 1)
                dve.wait_ge(f_silu, tile_no + 1)
                if not (isinstance(tile_no, int) and tile_no == 0):
                    dve.wait_ge(f_lo, tile_no)
                dve.tensor_tensor(PRD[:, :], SG[:, :], VU[:, :], ALU.mult).then_inc(f_prod, 1)

            def low(pair, x):
                tile_no = 2 * pair + x
                dve.wait_ge(f_hi, tile_no + 1)
                dve.tensor_tensor(GL[:, x, :], PRD[:, :], GH[:, x, :].bitcast(F32),
                                  ALU.subtract).then_inc(f_lo, 1)

            def accumulate(g, k, after=lambda m: None):
                for m in range(KT):
                    g.ready(dve, k + m)
                    dve.tensor_tensor(RAW[:, m, :], RAW[:, m, :], g.psum(k + m), ALU.add)\
                       .then_inc(g.free(k + m), 1)
                    after(m)

            g = Groups("ffn_first")
            tile(g, 0, 0, 0)
            low(0, 0)
            tile(g, 2, 0, 1)
            low(0, 1)
            with step.loop(1, FFN_PAIRS, 4) as i:
                g = Groups("ffn", i, 12, first=-12)
                tile(g, 0, i, 0)
                accumulate(g, 2)
                g.wait_free(dve, 8)
                g.wait_free(dve, 9)
                low(i, 0)
                tile(g, 10, i, 1)
                low(i, 1)
            g = Groups("ffn_last")
            zero_sum()
            accumulate(g, 0, lambda m: add_square(KT + m - 1, (m - 1) % 2) if m else None)
            add_square(2 * KT - 1, 1)
            end_sum("ffn_post")
            g.wait_free(dve, 6)
            g.wait_free(dve, 7)
            norm_residual("ffn_post", "norm_ffn_post", lambda k: RAW[:, k, :])
            norm_split("pre2", "norm_pre_2", lambda k: X[:, k, :], HL)

            step(dve.memset(GR[:, :], 0.0))
            dve.wait_ge(lam_loaded, 16)
            lam4 = lam_sb[:, :].rearrange("p (a b n) -> p a b n", a=2, b=2)
            step(dve.tensor_tensor(lam4[:, :, 0, :], lam4[:, :, 0, :], lam4[:, :, 1, :], ALU.mult))
            dve.reduce_sum(cols[:, 8:10], lam4[:, :, 0, :], AX.X).then_inc(lam_prod, 1)
            dve.wait_ge(lam_exp, 1)
            step(dve.tensor_tensor(cols[:, 8:9], cols[:, 8:9], cols[:, 9:10], ALU.subtract))
            dve.tensor_scalar(cols[:, 14:15], cols[:, 8:9], LAM_INIT, -1.0, ALU.add, ALU.mult)\
               .then_inc(lam_ready, 1)
            dve.wait_ge(lam_ready, 1)
            g = Groups("diff")
            g.wait_free(dve, 0)
            step(dve.tensor_scalar(GROWS[:, 0, :], GROWS[:, 0, :], -1.0, None, ALU.mult))
            softplus(GROWS, None, None, 3)
            dve.wait_ge(spilled, 16 * KT // 2)
            step(dve.memset(DQ[:, :, :], 0.0))
            step(dve.memset(DK[:, :, :], 0.0))
            dve.sem_inc(aug_k, 1)
            def slopes():
                step(dve.tensor_scalar(DK[64:66, 0, :], DK[64:66, 0, :], 0.25, None, ALU.mult))
                step(dve.tensor_scalar(DK[0:2, 1, :], DK[0:2, 1, :], 0.25, None, ALU.mult))

            step(dve.tensor_scalar(GROWS[:, 2, :], GROWS[:, 0, :], -1.0, None, ALU.mult))
            step(dve.memset(GROWS[:, 1, :], 1.0))
            step(dve.tensor_tensor_scan(GROWS[:, 3, :], GROWS[:, 1, :], GROWS[:, 2, :], 0.0,
                                        ALU.mult, ALU.add))
            step(dve.tensor_tensor(GROWS[:, 5, :], GROWS[:, 5, :], GROWS[:, 3, :], ALU.subtract))
            step(dve.tensor_tensor_scan(GROWS[:, 4, :], GROWS[:, 5, :], GROWS[:, 5, :], 0.0,
                                        ALU.max, ALU.max))
            step(dve.tensor_copy(GR[64:68, :], GROWS[:, 5, :]))
            step(dve.tensor_scalar(GR[0:4, :], GROWS[:, 4, :], -1.0, None, ALU.mult))
            step(dve.tensor_tensor(GROWS[:, 3, :], GROWS[:, 3, :], GROWS[:, 4, :], ALU.add))
            dve.tensor_scalar(GR[32:36, :], GROWS[:, 3, :], -1.0, None, ALU.mult).then_inc(gate_rows, 1)
            dve.wait_ge(aug_loaded, 64)
            slopes()
            dve.sem_inc(aug_set, 1)
            g.ready(dve, 5)
            dve.tensor_copy(DV[:, :, :], g.psum(5).rearrange("p (t n) -> p t n", t=TT))\
               .then_inc(d_vop, 1)
            dve.wait_ge(d_vop, 1)
            dve.sem_inc(g.free(5), 1)
            g.ready(dve, 6)
            dve.tensor_copy(ACOL[:, :, :], g.psum(6).rearrange("p (t n) -> p t n", t=TT)[:, :, 64:68])\
               .then_inc(g.free(6), 1)
            g.wait_free(dve, 6)

            def diff_head(i, last=False):
                hb = Halves("diff", i, DIFF_HALVES)

                def maxima(t):
                    b = 4 + 2 * (t % 2)
                    dve.wait_ge(d_scores, i * (2 * TT) + (2 * t + 2))
                    both = PG[:, 0, :].rearrange("p (c n) -> p c n", c=2)[:, :, 0:(t + 1) * P]
                    dve.reduce_max(cols[:, b:b + 2], both, AX.X, negate=True).then_inc(d_neg, 1)

                def maximum(t, c):
                    b = 4 + 2 * (t % 2) + c
                    dve.wait_ge(d_scores, i * (2 * TT) + (2 * t + c + 1))
                    dve.reduce_max(cols[:, b:b + 1], diff_scores(t, c), AX.X, negate=True)\
                       .then_inc(d_neg, 1)

                def normalise(t):
                    b = 10 + 2 * (t % 2)
                    n = (t + 1) * P
                    primed(dve, d_exp, i * (2 * TT) + (2 * t + 2))
                    primed(dve, d_prob, i * TT + t)
                    step(dve.reciprocal(cols[:, 2:4], cols[:, b:b + 2]))
                    step(dve.tensor_tensor(cols[:, 3:4], cols[:, 3:4], cols[:, 14:15], ALU.mult))
                    step(dve.tensor_scalar(DP[:, t % 2, 0, 0:n], DP[:, t % 2, 0, 0:n],
                                           cols[:, 2:3], None, ALU.mult))
                    dve.scalar_tensor_tensor(DP[:, t % 2, 0, 0:n], DP[:, t % 2, 1, 0:n], cols[:, 3:4],
                                             DP[:, t % 2, 0, 0:n], ALU.mult, ALU.add)\
                       .then_inc(d_prob, 1)

                for t in range(TT):
                    if t < 4:
                        maxima(t)
                    else:
                        maximum(t, 0)
                    if t:
                        normalise(t - 1)
                    if t >= 4:
                        maximum(t, 1)
                    if t in (1, 3):
                        hb.ready(dve, t // 2)
                        dve.tensor_scalar(NQ[:, halves(t // 2)], hb.bank(t // 2),
                                          1.0 if last else 0.125, None, ALU.mult)\
                           .then_inc(hb.free(t // 2), 1)
                normalise(TT - 1)
                if not last:
                    dve.wait_ge(d_k, i + 2)
                    slopes()
                    hb.wait_free(dve, 0)
                    hb.wait_free(dve, 1)
                    step(dve.tensor_copy(DQ[0:64, 0, :], NQ[0:64, :]))
                    dve.tensor_copy(DQ[64:128, 1, :], NQ[64:128, :]).then_inc(d_q, 1)
                    primed(dve, d_half, 2 * i + 2)
                    turned_halves(hb, 8, DV)
                    dve.sem_inc(d_vop, 1)
                dve.wait_ge(d_root, 2 * i + 2)
                primed(dve, d_o, i + 1)
                step(dve.reciprocal(RS[:, :], RS[:, :]))
                head = (lambda n: slice(i + n, i + n + 1)) if last else (lambda n: bass.ds(i + n, 1))
                step(dve.scalar_tensor_tensor(DO[:, :], DO[:, :], vec[:, head(VEC0["norm_a"])],
                                              RS[:, :], ALU.mult, ALU.mult))
                dve.scalar_tensor_tensor(RAW[:, head(0), :], DO[:, :], 1.0 - LAM_INIT,
                                         RAW[:, head(4), :], ALU.mult, ALU.mult).then_inc(d_y, 1)

            def turned_halves(hb, m0, out):
                for m in (m0, m0 + 1):
                    hb.ready(dve, m)
                    dve.tensor_copy(out[:, 4 * (m % 2):4 * (m % 2) + 4, :],
                                    hb.bank(m).rearrange("p (t n) -> p t n", t=4))\
                       .then_inc(hb.free(m), 1)
                hb.wait_free(dve, m0)
                hb.wait_free(dve, m0 + 1)

            with step.loop(0, DIFF_HEADS - 1, 3 * TT + 2 + 3) as i:
                diff_head(i)
            diff_head(DIFF_HEADS - 1, True)

            def mlstm_taps(head, n):
                dve.wait_ge(m_conv, 2 * head + (n + 1))
                for d in (1, 2, 3):
                    c = VEC0["ml_conv"] + 4 * n + 3 - d
                    w = (vec[:, c:c + 1] if isinstance(head, int) else vec[:, bass.ds(8 * head + c, 1)])
                    ins = dve.scalar_tensor_tensor(MC[n][:, d:], MR[n][:, 0:S - d], w, MC[n][:, d:],
                                                   ALU.mult, ALU.add)
                    if d < 3:
                        step(ins)
                    else:
                        ins.then_inc(m_taps, 1)

            def select(head):
                for n in range(2):
                    c = 32 * n
                    col = (ident[:, c:c + 1] if isinstance(head, int) else ident[:, bass.ds(head + c, 1)])
                    ins = dve.tensor_copy(selM[:, n, :], col.to_broadcast([P, P]))
                    if n == 0:
                        step(ins)
                    else:
                        ins.then_inc(m_sel, 1)

            def exponents(head):
                dve.wait_ge(m_mn, 2 * head + 2)
                blocks = [x[:, :].rearrange("p (t n) -> p t n", t=TT) for x in (MX, MN)]
                acol = (ACOL[:, :, head:head + 1] if isinstance(head, int) else
                        ACOL[:, :, bass.ds(head, 1)])
                step(dve.tensor_tensor(blocks[0], blocks[1], acol.to_broadcast([P, TT, P]), ALU.add))
                dve.scalar_tensor_tensor(blocks[0], blocks[0], 0.0, below_blocks, ALU.min, ALU.add)\
                   .then_inc(m_dd, 1)

            select(0)
            mlstm_taps(0, 0)
            mlstm_taps(0, 1)
            turned_halves(Halves("mlstm_first"), 2, MV)
            dve.sem_inc(m_vop, 1)
            exponents(0)

            def mlstm_head(i, last=False):
                hb = Halves("mlstm", i, ML_HALVES)
                index = (lambda n: slice(i + n, i + n + 1)) if last else (lambda n: bass.ds(i + n, 1))

                def decayed(j):
                    dve.wait_ge(m_scores, i * TT + (j + 1))
                    dve.wait_ge(m_e, i * TT + (j + 1))
                    primed(dve, m_used, i * TT + max(j - 1, 0))
                    dve.scalar_tensor_tensor(MP[:, j % 2, j * P:], PG[:, 0, j * P:],
                                             float(P) ** -0.5, MD[:, j % 2, j * P:],
                                             ALU.mult, ALU.mult).then_inc(m_pp, 1)

                for j in range(TT):
                    decayed(j)
                    if not last:
                        if j == 0:
                            select(i + 1)
                        if j == 4:
                            mlstm_taps(i + 1, 0)
                        if j == 6:
                            mlstm_taps(i + 1, 1)
                den = MR[0]
                dve.wait_ge(m_abs, i + 1)
                dve.wait_ge(m_me, 2 * i + 2)
                step(dve.tensor_tensor(den[:, :], den[:, :], ME[:, :], ALU.max))
                step(dve.reciprocal(den[:, :], den[:, :]))
                step(dve.tensor_tensor(MH[:, :], POf, den[:, :], ALU.mult))
                dve.wait_ge(m_o, i + 1)
                dve.tensor_tensor(MH[:, :], MH[:, :], MO[:, :], ALU.mult).then_inc(m_h, 1)
                if not last:
                    exponents(i + 1)
                dve.wait_ge(m_root, 2 * i + 2)
                step(dve.reciprocal(RS[:, :], RS[:, :]))
                dve.wait_ge(m_sq, i + 1)
                step(dve.scalar_tensor_tensor(MH[:, :], MH[:, :], vec[:, index(VEC0["norm_b"])],
                                              RS[:, :], ALU.mult, ALU.mult))
                z = RAW[:, index(4), :]
                dve.tensor_tensor(z, MH[:, :], z, ALU.mult).then_inc(m_y, 1)

            with step.loop(0, ML_HEADS - 1, 1 + 4 + 1 + 5) as i:
                mlstm_head(i)
            mlstm_head(ML_HEADS - 1, True)

            primed(dve, m_y, ML_HEADS)
            split("y", None, YL)
            def merge_tile(g, k, n, tile_no):
                dve.wait_ge(g_sig, 2 * tile_no + 2)
                g.ready(dve, k)
                primed(dve, g_done, tile_no)
                dve.tensor_tensor(MA[:, :], g.psum(k), MS[n][:, :], ALU.mult).then_inc(g.free(k), 1)
                g.wait_free(dve, k)
                g.ready(dve, k + 1)
                step(dve.tensor_tensor(MS2[n][:, :], g.psum(k + 1), MS2[n][:, :], ALU.mult))
                dve.sem_inc(g.free(k + 1), 1)
                at_tile = (slice(tile_no, tile_no + 1) if isinstance(tile_no, int) else
                           bass.ds(tile_no, 1))
                dve.tensor_tensor(RAW[:, at_tile, :], MA[:, :], MS2[n][:, :], ALU.add).then_inc(g_done, 1)

            with step.loop(0, KT // 2 - 1, 2) as i:
                for n in range(2):
                    merge_tile(Groups("merge", i, 8), 4 * n, n, 2 * i + n)
            for n in range(2):
                merge_tile(Groups("merge_last"), 2 * n, n, KT - 2 + n)
            primed(dve, g_done, KT)
            split("merged", None, HL)
            zero_sum()
            sum_squares(KT // 2 - 1, 2 * KT)
            g = Groups("x_back")
            for t in range(1, TT, 2):
                g.ready(dve, t)
                dve.tensor_copy(XT[:, t, :], g.psum(t)).then_inc(g.free(t), 1)
            for k in range(2):
                add_square(3 * KT - 2 + k, k)
            end_sum("post2")
            for t in (TT - 2, TT - 1):
                g.wait_free(dve, t)
            dve.wait_ge(n_root, NORM_INDEX["post2"] + 1)
            step(dve.reciprocal(cols[:, 0:TT], cols[:, 0:TT]))
            g = Groups("y")
            for t in range(TT):
                g.ready(dve, t)
                dve.scalar_tensor_tensor(XT[:, t, :], g.psum(t), cols[:, t:t + 1], XT[:, t, :],
                                         ALU.mult, ALU.add).then_inc(g.free(t), 1)


_VECTORS_P = ("norm_mix_pre", "norm_mix_post", "norm_ffn_pre", "norm_ffn_post", "norm_pre_2",
              "norm_post_2", "mla_q_norm", "mla_kv_norm", "ssd_norm")


def _blocks(w, columns):
    out = np.zeros((len(columns), P, KT, P), w.dtype)
    for u, c in enumerate(columns):
        part = w[:, c].reshape(w.shape[0] // P, P, len(c))
        out[u, :, :part.shape[0], :len(c)] = part.transpose(1, 0, 2)
    return out


def _weights(a):
    tile = lambda at: list(range(at, at + P))
    w_in = a["w_in"][0]
    c, h, z = 672, 928, 1184
    order = [tile(0), tile(128), tile(256), None]
    for j in range(2):
        order += [tile(c + j * P), tile(h + j * P), tile(416 + j * P)]
    order += [tile(z), tile(z + P)] + [tile(1440 + j * P) for j in range(6)]
    parts = _blocks(w_in, [o if o is not None else [] for o in order])
    odd = w_in.reshape(KT, P, -1).transpose(1, 0, 2)
    kr = 384
    parts[3, :, :, 0:4] = odd[:, :, 2208:2212]
    parts[3, :, :, 64:96] = odd[:, :, kr:kr + 32]
    parts[3, :, :, 96:112] = odd[:, :, kr + 16:kr + 32]
    parts[3, :, :, 112:128] = odd[:, :, kr:kr + 16]
    units = [parts]
    wq, wkv = a["mla_w_q_up"][0], a["mla_w_kv_up"][0]
    mla = np.zeros((MLA_HEADS, P, KT, P), wq.dtype)
    for n in range(MLA_HEADS):
        q = n * QK_DIM
        cols = list(range(q, q + 96)) + list(range(q + 80, q + 96)) + list(range(q + 64, q + 80))
        mla[n, :, 0:2, :] = wq[:, cols].reshape(2, P, P).transpose(1, 0, 2)
        mla[n, :, 2, :] = wkv[:, n * P:(n + 1) * P]
    units.append(mla)
    units.append(_blocks(a["w_out"][0], [tile(m * P) for m in range(KT)]))
    up, down = a["ffn_w_up"][0], a["ffn_w_down"][0]

    def gate_up(pair):
        return _blocks(up, [tile(part * FFN + (2 * pair + x) * P) for x in range(2) for part in range(2)])

    def down_of(pair):
        w = down[2 * pair * P:(2 * pair + 2) * P].reshape(2, P, 2, 4, P)
        return w.transpose(2, 1, 3, 0, 4).reshape(2, P, KT, P)

    units.append(gate_up(0))
    for pair in range(1, FFN_PAIRS):
        first = gate_up(pair)
        units += [first[0:2], down_of(pair - 1), first[2:4]]
    units.append(down_of(FFN_PAIRS - 1))
    w2 = a["w_in_2"][0]
    gates = np.zeros((1, P, KT, P), w2.dtype)
    g8 = w2[:, 4608:4616].reshape(KT, P, 8).transpose(1, 0, 2)
    gates[0, :, :, 0:4] = g8[:, :, 0:4]
    gates[0, :, :, 32:36] = g8[:, :, 4:8]
    units.append(gates)
    units.append(_blocks(w2, [tile(part * 512 + n * P) for n in range(4) for part in range(4)]))
    for n in range(ML_HEADS):
        units.append(_blocks(w2, [tile(2048 + part * 512 + n * P) for part in (0, 1, 2, 4)]))
        if n:
            units.append(np.zeros((ML_UNITS - 5, P, KT, P), w2.dtype))
        units.append(_blocks(w2, [tile(2048 + 3 * 512 + n * P)]))
    wa, wb = a["w_a_2"][0], a["w_b_2"][0]
    gates = lambda m: _blocks(w2, [tile(4616 + m * P), tile(5640 + m * P)])
    units += [gates(0), gates(1)]
    for m in range(KT):
        units.append(_blocks(np.concatenate([wa, wb]), [tile(m * P)]))
        if m + 2 < KT:
            units.append(gates(m + 2))
    units.append(_blocks(a["w_out_2"][0], [tile(m * P) for m in range(KT)]))
    return np.concatenate(units).reshape(-1, P, KT * P)


def _vectors(a):
    out = np.zeros((P, NVEC), np.float32)

    def put(name, k, column, at=0):
        out[at:at + len(column), VEC0[name] + k] = column

    for name in _VECTORS_P:
        for k, column in enumerate(a[name][0].reshape(-1, P)):
            put(name, k, column)
    for j in range(2):
        for i in range(3):
            put("sc_conv", 3 * j + i, a["sc_conv_w"][0, i, j * P:(j + 1) * P])
    for j in range(6):
        for i in range(4):
            put("ssd_conv", 5 * j + i, a["ssd_conv_w"][0, i, j * P:(j + 1) * P])
        put("ssd_conv", 5 * j + 4, a["ssd_conv_b"][0, j * P:(j + 1) * P])
    put("dt_bias", 0, a["ssd_dt_bias"][0])
    put("a_log", 0, a["ssd_a_log"][0])
    for j in range(2):
        put("ssd_d", j, np.repeat(a["ssd_d"][0, 2 * j:2 * j + 2], 64))
    for t in range(FT):
        for part in range(2):
            at = part * FFN + t * P
            for i in range(3):
                put("ffn_conv", 8 * t + 4 * part + i, a["ffn_conv_w"][0, i, at:at + P])
            put("ffn_conv", 8 * t + 4 * part + 3, a["ffn_conv_b"][0, at:at + P])
    put("gate_bias", 0, a["b_if_2"][0, 0:4])
    put("gate_bias", 0, a["b_if_2"][0, 4:8], 32)
    for n in range(ML_HEADS):
        for part in range(2):
            for i in range(4):
                at = part * 512 + n * P
                put("ml_conv", 8 * n + 4 * part + i, a["conv_qk_2"][0, i, at:at + P])
        put("norm_a", n, a["norm_a_2"][0, n * P:(n + 1) * P])
        put("norm_b", n, a["norm_b_2"][0, n * P:(n + 1) * P])
    freq = (1.0 / 10000.0 ** (np.arange(0, ROPE, 2) / ROPE)).astype(np.float32)
    put("inv_freq", 0, np.tile(freq, 4), 64)
    put("phase", 0, np.full(32, np.pi / 2, np.float32), 64)
    put("turn", 0, np.full(32, 0.25, np.float32), 64)
    put("sign", 0, np.ones(P, np.float32))
    put("sign", 0, -np.ones(16, np.float32), 96)
    put("eps", 0, np.full(P, EPS, np.float32))
    return out


def _squares():
    rows, columns = np.indices((P, P))
    rope_sum = ((columns >= 64) & (rows >= 64) & (rows % 32 == columns % 32)).astype(np.float32)
    ahead = np.where(columns > rows, np.float32(-1e30), np.float32(0))
    made = {"ident": rows == columns, "ones": np.ones((P, P)),
            "below": np.where(rows > columns, np.float32(-1e30), np.float32(0)),
            "rope_sum": rope_sum, "ahead": ahead}
    return np.stack([made[n].astype(np.float32) for n in SQUARES], axis=1)


def _aug_rows():
    t = np.arange(S, dtype=np.float32)
    one = np.ones(S, np.float32)
    return np.stack([np.stack([t, one]), np.stack([-one, t])])


def kernel(**inputs):
    import concourse.bacc as bacc
    from concourse.bass_utils import run_bass_kernel_spmd

    a = {k: np.asarray(x) for k, x in inputs.items()}
    arrays = {
        "weights": _weights(a),
        "x": a["x"].reshape(S, D),
        "positions": a["positions"].reshape(1, S),
        "vectors": _vectors(a),
        "squares": _squares(),
        "aug_rows": _aug_rows(),
        "lambda_qk": a["lambda_qk_2"].reshape(1, 4 * 64),
    }
    arrays = {k: np.ascontiguousarray(x) for k, x in arrays.items()}
    nc = bacc.Bacc("TRN2", target_bir_lowering=False, num_devices=1)
    args = [nc.dram_tensor(k, x.shape, mybir.dt.from_np(x.dtype), kind="ExternalInput").ap()
            for k, x in arrays.items()]
    args.append(nc.dram_tensor("y", (S, D), F32, kind="ExternalOutput").ap())
    program(nc, *args)
    r = run_bass_kernel_spmd(nc, [arrays], core_ids=[0])
    return np.asarray(r.results[0]["y"]).reshape(1, S, D)
```
